# Optimizing a Trainium2 kernel written in Bass

```python
import math
import jax, jax.numpy as jnp
from jax import lax
import numpy as np

D_MODEL = 1024
BATCH = 1
SEQ = 512
DEPTH = 2

D_RNN = 1024
RNN_BLOCKS = 16
RNN_BLOCK = D_RNN // RNN_BLOCKS
CONV_WIDTH = 4
LRU_C = 8.0
N_HEADS = 16
QK_NOPE = 64
QK_ROPE = 32
V_HEAD = 64
Q_LORA = 384
KV_LORA = 256
ROPE_THETA = 10000.0
Q_BLOCK = 128
D_MIX = N_HEADS * V_HEAD
IN_WIDTH = 2 * D_RNN + Q_LORA + KV_LORA + QK_ROPE + 2 * D_MIX
D_FF = 3 * D_MODEL
FFN_CONV_WIDTH = 3
ALPHA = (2 * DEPTH) ** 0.25
BETA = (8 * DEPTH) ** -0.25
EPS = 1e-6
NEG_INF = -1e30


def _split_points():
    sizes = (D_RNN, D_RNN, Q_LORA, KV_LORA, QK_ROPE, D_MIX, D_MIX)
    pts, acc = [], 0
    for s in sizes[:-1]:
        acc += s
        pts.append(acc)
    return pts

def layer_norm(x, g, b):
    xf = x.astype(jnp.float32)
    mu = xf.mean(-1, keepdims=True)
    var = jnp.square(xf - mu).mean(-1, keepdims=True)
    y = (xf - mu) * lax.rsqrt(var + EPS) * g.astype(jnp.float32) + b.astype(jnp.float32)
    return y.astype(x.dtype)

def rms_norm(x, g):
    xf = x.astype(jnp.float32)
    y = xf * lax.rsqrt(jnp.mean(xf * xf, -1, keepdims=True) + EPS) * g.astype(jnp.float32)
    return y.astype(x.dtype)

def causal_dwconv(x, w, b):
    width, c = w.shape
    y = lax.conv_general_dilated(
        x, w[:, None, :].astype(x.dtype), window_strides=(1,), padding=[(width - 1, 0)],
        dimension_numbers=("NWC", "WIO", "NWC"), feature_group_count=c)
    return y + b.astype(x.dtype)

def rope_tables(positions, dtype):
    inv_freq = ROPE_THETA ** (-jnp.arange(0, QK_ROPE, 2, dtype=jnp.float32) / QK_ROPE)
    ang = positions.astype(jnp.float32)[..., None] * inv_freq
    return jnp.cos(ang)[:, :, None, :].astype(dtype), jnp.sin(ang)[:, :, None, :].astype(dtype)

def apply_rope(x, cos, sin):
    x1, x2 = jnp.split(x, 2, axis=-1)
    return jnp.concatenate([x1 * cos - x2 * sin, x2 * cos + x1 * sin], axis=-1)

def rg_lru(x, gx_w, gx_b, ga_w, ga_b, lru_lambda):
    B, S, _ = x.shape
    xb = x.reshape(B, S, RNN_BLOCKS, RNN_BLOCK)
    gate_x = jax.nn.sigmoid(jnp.einsum("bshi,hij->bshj", xb, gx_w).reshape(B, S, D_RNN) + gx_b)
    gate_a = jax.nn.sigmoid(jnp.einsum("bshi,hij->bshj", xb, ga_w).reshape(B, S, D_RNN) + ga_b)
    log_a = -LRU_C * gate_a.astype(jnp.float32) * jax.nn.softplus(-lru_lambda.astype(jnp.float32))
    a = jnp.exp(log_a)
    mult = jnp.sqrt(-jnp.expm1(2.0 * log_a))
    u = mult * (gate_x * x).astype(jnp.float32)

    def step(h, au):
        a_t, u_t = au
        h = a_t * h + u_t
        return h, h

    _, hs = lax.scan(step, jnp.zeros((B, D_RNN), jnp.float32),
                     (jnp.swapaxes(a, 0, 1), jnp.swapaxes(u, 0, 1)))
    return jnp.swapaxes(hs, 0, 1).astype(x.dtype)

def mla_attention(q_lat, kv_lat, k_rope_raw, cos, sin, q_norm_g, w_uq, kv_norm_g, w_ukv):
    B, S, _ = q_lat.shape
    q = (rms_norm(q_lat, q_norm_g) @ w_uq).reshape(B, S, N_HEADS, QK_NOPE + QK_ROPE)
    q_nope, q_pe = q[..., :QK_NOPE], apply_rope(q[..., QK_NOPE:], cos, sin)
    kv = (rms_norm(kv_lat, kv_norm_g) @ w_ukv).reshape(B, S, N_HEADS, QK_NOPE + V_HEAD)
    k_nope, v = kv[..., :QK_NOPE], kv[..., QK_NOPE:]
    k_pe = apply_rope(k_rope_raw[:, :, None, :], cos, sin)[:, :, 0, :]
    scale = (QK_NOPE + QK_ROPE) ** -0.5
    outs = []
    for start in range(0, S, Q_BLOCK):
        end = start + Q_BLOCK
        s = (jnp.einsum("bqhd,bkhd->bhqk", q_nope[:, start:end], k_nope[:, :end])
             + jnp.einsum("bqhd,bkd->bhqk", q_pe[:, start:end], k_pe[:, :end]))
        s = s.astype(jnp.float32) * scale
        causal = (start + jnp.arange(Q_BLOCK))[:, None] >= jnp.arange(end)[None, :]
        p = jax.nn.softmax(jnp.where(causal, s, NEG_INF), axis=-1).astype(v.dtype)
        outs.append(jnp.einsum("bhqk,bkhd->bqhd", p, v[:, :end]))
    return jnp.concatenate(outs, axis=1).reshape(B, S, D_MIX)

def mixer_sublayer(x, cos, sin, w_in, conv_w, conv_b, gx_w, gx_b, ga_w, ga_b, lru_lambda,
                   q_norm_g, w_uq, kv_norm_g, w_ukv, w_out):
    proj = x @ w_in
    x_rnn, g_rnn, q_lat, kv_lat, k_rope, gate_a, gate_b = jnp.split(proj, _split_points(), axis=-1)
    y_rnn = jax.nn.gelu(g_rnn) * rg_lru(causal_dwconv(x_rnn, conv_w, conv_b),
                                        gx_w, gx_b, ga_w, ga_b, lru_lambda)
    y_mla = mla_attention(q_lat, kv_lat, k_rope, cos, sin, q_norm_g, w_uq, kv_norm_g, w_ukv)
    merged = jax.nn.sigmoid(gate_a) * y_rnn + jax.nn.sigmoid(gate_b) * y_mla
    return merged @ w_out

def conv_ffn(x, w_up, ffn_conv_w, ffn_conv_b, w_down):
    h = causal_dwconv(x @ w_up, ffn_conv_w, ffn_conv_b)
    h_gate, h_val = jnp.split(h, 2, axis=-1)
    return (jax.nn.gelu(h_gate) * h_val) @ w_down

def first_inputs(seed: int = 0) -> dict:
    key = jax.random.key(seed)
    ks = jax.random.split(key, 24)
    f32 = jnp.float32

    def nrm(k, shape, scale):
        return jax.random.normal(k, shape, f32) * scale

    x = jax.random.normal(ks[0], (BATCH, SEQ, D_MODEL), f32)
    offsets = jax.random.randint(ks[1], (BATCH, 1), 0, 4096, dtype=jnp.int32)
    positions = (jnp.arange(SEQ, dtype=jnp.int32)[None, :] + offsets).astype(jnp.int32)
    u = jax.random.uniform(ks[2], (DEPTH, D_RNN), f32, 0.9, 0.999)
    a0 = u ** (1.0 / LRU_C)
    lru_lambda = jnp.log(a0) - jnp.log1p(-a0)
    return {
        "x": x,
        "positions": positions,
        "w_in": nrm(ks[3], (DEPTH, D_MODEL, IN_WIDTH), D_MODEL ** -0.5),
        "conv_w": nrm(ks[4], (DEPTH, CONV_WIDTH, D_RNN), CONV_WIDTH ** -0.5),
        "conv_b": nrm(ks[5], (DEPTH, D_RNN), 0.02),
        "gx_w": nrm(ks[6], (DEPTH, RNN_BLOCKS, RNN_BLOCK, RNN_BLOCK), RNN_BLOCK ** -0.5),
        "gx_b": nrm(ks[7], (DEPTH, D_RNN), 0.02),
        "ga_w": nrm(ks[8], (DEPTH, RNN_BLOCKS, RNN_BLOCK, RNN_BLOCK), RNN_BLOCK ** -0.5),
        "ga_b": nrm(ks[9], (DEPTH, D_RNN), 0.02),
        "lru_lambda": lru_lambda,
        "q_norm_g": 1.0 + nrm(ks[10], (DEPTH, Q_LORA), 0.02),
        "w_uq": nrm(ks[11], (DEPTH, Q_LORA, N_HEADS * (QK_NOPE + QK_ROPE)), Q_LORA ** -0.5),
        "kv_norm_g": 1.0 + nrm(ks[12], (DEPTH, KV_LORA), 0.02),
        "w_ukv": nrm(ks[13], (DEPTH, KV_LORA, N_HEADS * (QK_NOPE + V_HEAD)), KV_LORA ** -0.5),
        "w_out": nrm(ks[14], (DEPTH, D_MIX, D_MODEL), BETA * D_MIX ** -0.5),
        "ln1_g": 1.0 + nrm(ks[15], (DEPTH, D_MODEL), 0.02),
        "ln1_b": nrm(ks[16], (DEPTH, D_MODEL), 0.02),
        "w_up": nrm(ks[17], (DEPTH, D_MODEL, 2 * D_FF), D_MODEL ** -0.5),
        "ffn_conv_w": nrm(ks[18], (DEPTH, FFN_CONV_WIDTH, 2 * D_FF), FFN_CONV_WIDTH ** -0.5),
        "ffn_conv_b": nrm(ks[19], (DEPTH, 2 * D_FF), 0.02),
        "w_down": nrm(ks[20], (DEPTH, D_FF, D_MODEL), BETA * D_FF ** -0.5),
        "ln2_g": 1.0 + nrm(ks[21], (DEPTH, D_MODEL), 0.02),
        "ln2_b": nrm(ks[22], (DEPTH, D_MODEL), 0.02),
    }

def first_block(x, positions, w_in, conv_w, conv_b, gx_w, gx_b, ga_w, ga_b, lru_lambda,
              q_norm_g, w_uq, kv_norm_g, w_ukv, w_out, ln1_g, ln1_b,
              w_up, ffn_conv_w, ffn_conv_b, w_down, ln2_g, ln2_b):
    cos, sin = rope_tables(positions, x.dtype)
    for l in range(DEPTH):
        mix = mixer_sublayer(x, cos, sin, w_in[l], conv_w[l], conv_b[l], gx_w[l], gx_b[l],
                             ga_w[l], ga_b[l], lru_lambda[l], q_norm_g[l], w_uq[l],
                             kv_norm_g[l], w_ukv[l], w_out[l])
        x = layer_norm(ALPHA * x + mix, ln1_g[l], ln1_b[l])
        ffn = conv_ffn(x, w_up[l], ffn_conv_w[l], ffn_conv_b[l], w_down[l])
        x = layer_norm(ALPHA * x + ffn, ln2_g[l], ln2_b[l])
    return x


N_MIXERS = 4
GROUP_WIDTH = D_MODEL // N_MIXERS
HEAD_DIM = 64
N_GROUP_HEADS = GROUP_WIDTH // HEAD_DIM
D_FF_2 = 4 * D_MODEL
N_MOD = 6
RMS_EPS = 1e-6
NEG_INF_2 = -1e30

ROPE_THETA_2 = 500000.0
ROPE_DIM = HEAD_DIM // 4

CONV_WIDTH_2 = 3

CMP_BLOCK = 32
CMP_STRIDE = 16
CMP_HIDDEN = 2 * HEAD_DIM
SLC_BLOCK = 64
N_SLC = 16
N_INIT_BLOCKS = 1
N_LOCAL_BLOCKS = 2
FORCE_BONUS = 1e4
WINDOW = 512
N_BRANCH = 3

GLA_DK = HEAD_DIM // 2
GLA_DV = HEAD_DIM
GLA_RANK = 16
GLA_TAU = 16.0
GLA_CHUNK = 64

GMLP_CHUNK = 128
GMLP_DIM = GROUP_WIDTH // N_GROUP_HEADS

SPLIT_SIZES = (
    GROUP_WIDTH, GROUP_WIDTH, GROUP_WIDTH,
    GROUP_WIDTH, 2 * N_BRANCH * HEAD_DIM, N_BRANCH * N_GROUP_HEADS,
    N_GROUP_HEADS * GLA_DK, N_GROUP_HEADS * GLA_DK,
    N_GROUP_HEADS * GLA_DV, N_GROUP_HEADS * GLA_DV, GLA_RANK,
    GROUP_WIDTH, GROUP_WIDTH,
)
D_IN_PROJ = sum(SPLIT_SIZES)


def rms_norm_2(x, gain=None):
    xf = x.astype(jnp.float32)
    y = xf * lax.rsqrt(jnp.mean(xf * xf, axis=-1, keepdims=True) + RMS_EPS)
    if gain is not None:
        y = y * gain.astype(jnp.float32)
    return y.astype(x.dtype)

def layer_norm_2(x):
    xf = x.astype(jnp.float32)
    mu = jnp.mean(xf, axis=-1, keepdims=True)
    var = jnp.mean(jnp.square(xf - mu), axis=-1, keepdims=True)
    return ((xf - mu) * lax.rsqrt(var + RMS_EPS)).astype(x.dtype)

def split_cols(z, sizes):
    out, start = [], 0
    for s in sizes:
        out.append(z[..., start:start + s])
        start += s
    return out

def partial_rotary(x, positions):
    half = ROPE_DIM // 2
    inv_freq = ROPE_THETA_2 ** (-jnp.arange(0, ROPE_DIM, 2, dtype=jnp.float32) / ROPE_DIM)
    ang = positions.astype(jnp.float32)[..., None] * inv_freq
    cos = jnp.cos(ang)[:, :, None, :]
    sin = jnp.sin(ang)[:, :, None, :]
    xr = x[..., :ROPE_DIM].astype(jnp.float32)
    x1, x2 = xr[..., :half], xr[..., half:]
    rot = jnp.concatenate([x1 * cos - x2 * sin, x2 * cos + x1 * sin], axis=-1).astype(x.dtype)
    return jnp.concatenate([rot, x[..., ROPE_DIM:]], axis=-1)

def masked_softmax(s, mask):
    p = jax.nn.softmax(jnp.where(mask, s, NEG_INF_2), axis=-1)
    return jnp.where(mask, p, 0.0)

def short_conv_mixer(h_in, b_gate, c_gate, conv_w):
    z = c_gate * h_in
    y = lax.conv_general_dilated(z, conv_w.astype(z.dtype)[:, None, :], (1,), ((CONV_WIDTH_2 - 1, 0),),
                                 dimension_numbers=('NWC', 'WIO', 'NWC'),
                                 feature_group_count=GROUP_WIDTH)
    return b_gate * y

def cmp_to_slc_matrix(n_cmp, n_blk):
    cs = np.arange(n_cmp) * CMP_STRIDE
    ss = np.arange(n_blk) * SLC_BLOCK
    ov = np.minimum(cs[:, None] + CMP_BLOCK, ss[None, :] + SLC_BLOCK) - np.maximum(cs[:, None], ss[None, :])
    return jnp.asarray(np.clip(ov, 0, None) / CMP_STRIDE, dtype=jnp.float32)

def nsa_mixer(q_in, kv_in, gate_in, positions, cmp_pos, cmp_w1, cmp_w2):
    B, S, _ = q_in.shape
    H, HD = N_GROUP_HEADS, HEAD_DIM
    scale = HD ** -0.5
    q = q_in.reshape(B, S, H, HD)
    k_cmp, v_cmp, k_slc, v_slc, k_win, v_win = jnp.split(kv_in, 2 * N_BRANCH, axis=-1)

    n_cmp = (S - CMP_BLOCK) // CMP_STRIDE + 1
    blk = np.arange(n_cmp)[:, None] * CMP_STRIDE + np.arange(CMP_BLOCK)[None, :]

    def compress(t, j):
        z = (t[:, blk] + cmp_pos[j]).reshape(B, n_cmp, CMP_BLOCK * HD)
        return jax.nn.silu(z @ cmp_w1[j]) @ cmp_w2[j]

    kc, vc = compress(k_cmp, 0), compress(v_cmp, 1)
    t_idx = jnp.arange(S)
    cmp_end = jnp.arange(n_cmp) * CMP_STRIDE + CMP_BLOCK - 1
    mask_c = cmp_end[None, :] <= t_idx[:, None]
    s_c = jnp.einsum('bshd,bnd->bhsn', q, kc).astype(jnp.float32) * scale
    p_c = masked_softmax(s_c, mask_c)
    o_cmp = jnp.einsum('bhsn,bnd->bshd', p_c.astype(vc.dtype), vc)

    n_blk = S // SLC_BLOCK
    p_slc = jnp.einsum('bhsn,nj->bsj', p_c, cmp_to_slc_matrix(n_cmp, n_blk))
    cur = (t_idx // SLC_BLOCK)[:, None]
    j = jnp.arange(n_blk)[None, :]
    forced = (j < N_INIT_BLOCKS) | ((cur - j >= 0) & (cur - j < N_LOCAL_BLOCKS))
    score = jnp.where(j <= cur, p_slc + jnp.where(forced, FORCE_BONUS, 0.0), NEG_INF_2)
    n_top = min(N_SLC, n_blk)
    _, sel_idx = lax.top_k(score, n_top)

    q_r = partial_rotary(q, positions)
    rope_k = lambda t: partial_rotary(t[:, :, None, :], positions)[:, :, 0, :]
    k_s_blk = rope_k(k_slc).reshape(B, n_blk, SLC_BLOCK, HD)
    v_s_blk = v_slc.reshape(B, n_blk, SLC_BLOCK, HD)
    pad = ((0, 0), (WINDOW, 0), (0, 0))
    k_w_pad = jnp.pad(rope_k(k_win), pad)
    v_w_pad = jnp.pad(v_win, pad)

    n_qb = S // Q_BLOCK
    q_blocks = q_r.reshape(B, n_qb, Q_BLOCK, H, HD).transpose(1, 0, 3, 2, 4)
    idx_blocks = sel_idx.reshape(B, n_qb, Q_BLOCK, n_top).transpose(1, 0, 2, 3)
    take = jax.vmap(lambda blocks, idx: blocks[idx])

    def block_fn(args):
        qb, q_b, idx_b = args
        tq = qb * Q_BLOCK + jnp.arange(Q_BLOCK)
        k_sel = take(k_s_blk, idx_b).reshape(B, Q_BLOCK, n_top * SLC_BLOCK, HD)
        v_sel = take(v_s_blk, idx_b).reshape(B, Q_BLOCK, n_top * SLC_BLOCK, HD)
        kpos = (idx_b[..., None] * SLC_BLOCK + jnp.arange(SLC_BLOCK)).reshape(B, Q_BLOCK, n_top * SLC_BLOCK)
        s_s = jnp.einsum('bhqd,bqkd->bhqk', q_b, k_sel).astype(jnp.float32) * scale
        p_s = masked_softmax(s_s, (kpos <= tq[None, :, None])[:, None])
        o_s = jnp.einsum('bhqk,bqkd->bhqd', p_s.astype(v_sel.dtype), v_sel)
        start = qb * Q_BLOCK
        k_wb = lax.dynamic_slice_in_dim(k_w_pad, start, Q_BLOCK + WINDOW, axis=1)
        v_wb = lax.dynamic_slice_in_dim(v_w_pad, start, Q_BLOCK + WINDOW, axis=1)
        kpos_w = start - WINDOW + jnp.arange(Q_BLOCK + WINDOW)
        diff = tq[:, None] - kpos_w[None, :]
        m_w = (diff >= 0) & (diff < WINDOW) & (kpos_w[None, :] >= 0)
        s_w = jnp.einsum('bhqd,bkd->bhqk', q_b, k_wb).astype(jnp.float32) * scale
        p_w = masked_softmax(s_w, m_w)
        o_w = jnp.einsum('bhqk,bkd->bhqd', p_w.astype(v_wb.dtype), v_wb)
        return o_s, o_w

    o_sel, o_win = lax.map(block_fn, (jnp.arange(n_qb), q_blocks, idx_blocks))
    to_bshd = lambda o: o.transpose(1, 0, 3, 2, 4).reshape(B, S, H, HD)
    g = jax.nn.sigmoid(gate_in.astype(jnp.float32)).astype(q.dtype).reshape(B, S, H, N_BRANCH)
    o = g[..., 0:1] * o_cmp + g[..., 1:2] * to_bshd(o_sel) + g[..., 2:3] * to_bshd(o_win)
    return o.reshape(B, S, GROUP_WIDTH)

def gla_mixer(q_in, k_in, v_in, g_in, lr_in, gate_w2, gate_b):
    B, S, _ = q_in.shape
    H, C = N_GROUP_HEADS, GLA_CHUNK
    n_c = S // C
    log_a = jax.nn.log_sigmoid((lr_in @ gate_w2 + gate_b).astype(jnp.float32)) / GLA_TAU

    def chunk(t, d):
        return t.reshape(B, n_c, C, H, d).transpose(0, 3, 1, 2, 4).astype(jnp.float32)

    q = chunk(q_in, GLA_DK) * GLA_DK ** -0.5
    k = chunk(k_in, GLA_DK)
    v = chunk(v_in, GLA_DV)
    b = jnp.cumsum(chunk(log_a, GLA_DK), axis=3)
    b_last = b[:, :, :, -1:, :]
    b_mid = b[:, :, :, C // 2:C // 2 + 1, :]
    causal = jnp.tril(jnp.ones((C, C), dtype=bool))
    att = jnp.einsum('bhntd,bhnsd->bhnts', q * jnp.exp(b - b_mid), k * jnp.exp(b_mid - b))
    o_intra = jnp.einsum('bhnts,bhnsv->bhntv', jnp.where(causal, att, 0.0), v)
    kv = jnp.einsum('bhnsd,bhnsv->bhndv', k * jnp.exp(b_last - b), v)
    decay = jnp.exp(b_last[:, :, :, 0, :])

    def step(state, inp):
        dec, kv_n = inp
        return dec[..., None] * state + kv_n, state

    init = jnp.zeros((B, H, GLA_DK, GLA_DV), jnp.float32)
    _, s_prev = lax.scan(step, init, (jnp.moveaxis(decay, 2, 0), jnp.moveaxis(kv, 2, 0)))
    o_inter = jnp.einsum('bhntd,nbhdv->bhntv', q * jnp.exp(b), s_prev)
    o = (o_intra + o_inter).transpose(0, 2, 3, 1, 4).reshape(B, S, H, GLA_DV)
    g = jax.nn.silu(g_in.astype(jnp.float32)).reshape(B, S, H, GLA_DV)
    return (g * rms_norm_2(o)).reshape(B, S, GROUP_WIDTH).astype(q_in.dtype)

def gmlp_mixer(u_in, v_in, w_s, b_s):
    B, S, _ = u_in.shape
    G, T = N_GROUP_HEADS, GMLP_CHUNK
    n_ch = S // T
    v = layer_norm_2(v_in.reshape(B, S, G, GMLP_DIM)).reshape(B, n_ch, T, G, GMLP_DIM)
    w = jnp.where(jnp.tril(jnp.ones((T, T), dtype=bool)), w_s, 0.0)
    mixed = jnp.einsum('gts,bnsgc->bntgc', w, v) + b_s.T[:, :, None]
    return (u_in.reshape(B, n_ch, T, G, GMLP_DIM) * mixed).reshape(B, S, GROUP_WIDTH)

def mixer_block(h, positions, w_in, conv_w, cmp_pos, cmp_w1, cmp_w2, gla_gate_w2, gla_gate_b,
                gmlp_ws, gmlp_b, grp_gain, w_o):
    B, S, _ = h.shape
    (a_h, a_b, a_c, n_q, n_kv, n_g, l_q, l_k, l_v, l_g, l_lr, m_u, m_v) = split_cols(h @ w_in, SPLIT_SIZES)
    outs = jnp.stack([
        short_conv_mixer(a_h, a_b, a_c, conv_w),
        nsa_mixer(n_q, n_kv, n_g, positions, cmp_pos, cmp_w1, cmp_w2),
        gla_mixer(l_q, l_k, l_v, l_g, l_lr, gla_gate_w2, gla_gate_b),
        gmlp_mixer(m_u, m_v, gmlp_ws, gmlp_b),
    ], axis=2)
    outs = rms_norm_2(outs, grp_gain.reshape(N_MIXERS, GROUP_WIDTH))
    return outs.reshape(B, S, D_MODEL) @ w_o

def second_inputs(seed: int = 0) -> dict:
    key = jax.random.key(seed)
    ks = jax.random.split(key, 20)
    nrm = lambda k, shape, s: jax.random.normal(k, shape, jnp.float32) * s
    positions = (jax.random.randint(ks[2], (BATCH, 1), 0, SEQ, dtype=jnp.int32)
                 + jnp.arange(SEQ, dtype=jnp.int32)[None, :])
    return {
        'x': nrm(ks[0], (BATCH, SEQ, D_MODEL), 1.0),
        'c': nrm(ks[1], (BATCH, D_MODEL), 1.0),
        'positions': positions,
        'w_in': nrm(ks[3], (DEPTH, D_MODEL, D_IN_PROJ), D_MODEL ** -0.5),
        'conv_w': nrm(ks[4], (DEPTH, CONV_WIDTH_2, GROUP_WIDTH), CONV_WIDTH_2 ** -0.5),
        'cmp_pos': nrm(ks[5], (DEPTH, 2, CMP_BLOCK, HEAD_DIM), 0.1),
        'cmp_w1': nrm(ks[6], (DEPTH, 2, CMP_BLOCK * HEAD_DIM, CMP_HIDDEN), (CMP_BLOCK * HEAD_DIM) ** -0.5),
        'cmp_w2': nrm(ks[7], (DEPTH, 2, CMP_HIDDEN, HEAD_DIM), CMP_HIDDEN ** -0.5),
        'gla_gate_w2': nrm(ks[8], (DEPTH, GLA_RANK, N_GROUP_HEADS * GLA_DK), GLA_RANK ** -0.5),
        'gla_gate_b': nrm(ks[9], (DEPTH, N_GROUP_HEADS * GLA_DK), 0.1),
        'gmlp_ws': nrm(ks[10], (DEPTH, N_GROUP_HEADS, GMLP_CHUNK, GMLP_CHUNK), 0.5 * GMLP_CHUNK ** -0.5),
        'gmlp_b': 1.0 + nrm(ks[11], (DEPTH, N_GROUP_HEADS, GMLP_CHUNK), 0.1),
        'grp_gain': 1.0 + nrm(ks[12], (DEPTH, D_MODEL), 0.1),
        'w_o': nrm(ks[13], (DEPTH, D_MODEL, D_MODEL), D_MODEL ** -0.5),
        'norm_g': 1.0 + nrm(ks[14], (DEPTH, 4, D_MODEL), 0.1),
        'w_mod': nrm(ks[15], (DEPTH, D_MODEL, N_MOD * D_MODEL), D_MODEL ** -0.5),
        'b_mod': nrm(ks[16], (DEPTH, N_MOD * D_MODEL), 0.02),
        'w_up': nrm(ks[17], (DEPTH, D_MODEL, D_FF_2), D_MODEL ** -0.5),
        'w_down': nrm(ks[18], (DEPTH, D_FF_2, D_MODEL), D_FF_2 ** -0.5),
    }

def second_block(x, c, positions, w_in, conv_w, cmp_pos, cmp_w1, cmp_w2, gla_gate_w2, gla_gate_b,
              gmlp_ws, gmlp_b, grp_gain, w_o, norm_g, w_mod, b_mod, w_up, w_down):
    cond = jax.nn.silu(c)
    for l in range(DEPTH):
        mod = cond @ w_mod[l] + b_mod[l]
        sh1, sc1, gt1, sh2, sc2, gt2 = [m[:, None, :] for m in jnp.split(mod, N_MOD, axis=-1)]
        h = rms_norm_2(x, norm_g[l, 0]) * (1.0 + sc1) + sh1
        y = mixer_block(h, positions, w_in[l], conv_w[l], cmp_pos[l], cmp_w1[l], cmp_w2[l],
                        gla_gate_w2[l], gla_gate_b[l], gmlp_ws[l], gmlp_b[l], grp_gain[l], w_o[l])
        x = x + gt1 * rms_norm_2(y, norm_g[l, 1])
        h = rms_norm_2(x, norm_g[l, 2]) * (1.0 + sc2) + sh2
        y = jnp.square(jax.nn.relu(h @ w_up[l])) @ w_down[l]
        x = x + gt2 * rms_norm_2(y, norm_g[l, 3])
    return x


def setup_inputs(seed=0):
    out = dict(first_inputs(seed))
    for name, value in second_inputs(seed + 1).items():
        if name != "x":
            out[name + "_2"] = value
    return out


def reference(
    x, positions, w_in, conv_w, conv_b, gx_w, gx_b, ga_w, ga_b, lru_lambda, q_norm_g, w_uq,
    kv_norm_g, w_ukv, w_out, ln1_g, ln1_b, w_up, ffn_conv_w, ffn_conv_b, w_down, ln2_g, ln2_b,
    c_2, positions_2, w_in_2, conv_w_2, cmp_pos_2, cmp_w1_2, cmp_w2_2, gla_gate_w2_2,
    gla_gate_b_2, gmlp_ws_2, gmlp_b_2, grp_gain_2, w_o_2, norm_g_2, w_mod_2, b_mod_2, w_up_2,
    w_down_2,
):
    x = first_block(
        x, positions, w_in, conv_w, conv_b, gx_w, gx_b, ga_w, ga_b, lru_lambda, q_norm_g, w_uq,
        kv_norm_g, w_ukv, w_out, ln1_g, ln1_b, w_up, ffn_conv_w, ffn_conv_b, w_down, ln2_g,
        ln2_b,
    )
    return second_block(
        x, c_2, positions_2, w_in_2, conv_w_2, cmp_pos_2, cmp_w1_2, cmp_w2_2, gla_gate_w2_2,
        gla_gate_b_2, gmlp_ws_2, gmlp_b_2, grp_gain_2, w_o_2, norm_g_2, w_mod_2, b_mod_2,
        w_up_2, w_down_2,
    )


_drawn_inputs = setup_inputs


def setup_inputs(seed=0):
    import zlib

    import numpy as np

    out = dict(_drawn_inputs(seed))
    spreads = {}
    factors = {'conv_b': 2.677,
     'gx_b': 8.0,
     'ga_b': 30.78,
     'q_norm_g': 8.0,
     'kv_norm_g': 8.0,
     'ffn_conv_b': 5.001,
     'cmp_pos_2': 2.969}
    for name, (base, spread) in spreads.items():
        noise = np.random.default_rng([zlib.crc32(name.encode()), seed]).standard_normal(out[name].shape)
        drawn = base * np.exp(spread * noise) if base else spread * noise
        out[name] = __import__('jax').numpy.asarray(drawn.astype(out[name].dtype))
    for name, factor in factors.items():
        out[name] = (out[name] * factor).astype(out[name].dtype)
    return out
```

```python
from contextlib import ExitStack, contextmanager

import numpy as np

import concourse.bass as bass
from concourse import mybir

F32 = mybir.dt.float32
F32R = mybir.dt.float32r
BF16 = mybir.dt.bfloat16
I32 = mybir.dt.int32
ALU = mybir.AluOpType
ACT = mybir.ActivationFunctionType
AX = mybir.AxisListType

P = 128
S = 512
D = 1024
DEPTH = 2
TT = S // P
KD = D // P
EPS = 1e-6
MASKED = -1e30

D_RNN = 1024
KR = D_RNN // P
Q_LORA, KV_LORA, QK_NOPE, QK_ROPE, V_HEAD, HEADS = 384, 256, 64, 32, 64, 16
KQ, KKV = Q_LORA // P, KV_LORA // P
QK = QK_NOPE + QK_ROPE
D_FF = 3 * D
KF = D_FF // P
ALPHA = (2 * DEPTH) ** 0.25
CONV = 4
FFN_CONV = 3
LRU_C = 8.0
MLA_SCALE = QK ** -0.5
LAT0 = 2 * D_RNN
ROPE0 = LAT0 + Q_LORA + KV_LORA
GA0 = ROPE0 + QK_ROPE
GB0 = GA0 + D

GW = D // 4
HD = 64
GH = 4
KF2 = 4 * D // P
N_MOD = 6
CONV2 = 3
CMP, STRIDE = 32, 16
N_CMP = (S - CMP) // STRIDE + 1
DK = 32
CHUNK = 64
NCH = S // CHUNK
TAU = 16.0
RANK = 16
O_KV = 4 * GW
O_G = O_KV + 6 * HD
O_LQ = O_G + 3 * GH
O_LK = O_LQ + GH * DK
O_LV = O_LK + GH * DK
O_LG = O_LV + GW
O_LR = O_LG + GW
O_MU = O_LR + RANK
O_MV = O_MU + GW

TWO_PI = 2.0 * np.pi
PI_A = float(np.float32(6.28125))
PI_B = 0.0019350051879882812
PI_C = float(TWO_PI - PI_A - PI_B)
ROUND = 1.5 * 2.0 ** 23


def constants():
    p = np.arange(P)
    parts = {}
    parts["ident"] = np.eye(P)
    parts["causal"] = np.where(p[None, :] > p[:, None], MASKED, 0.0)
    parts["upper"] = (p[:, None] <= p[None, :]) * 1.0
    parts["chunk"] = parts["upper"] * (p[:, None] // CHUNK == p[None, :] // CHUNK)
    parts["halves"] = (p[:, None] // HD == p[None, :] // HD) * 1.0
    state = np.zeros((P, GH, HD))
    for h in range(GH):
        state[h * DK:(h + 1) * DK, h] = 1.0
    parts["state"] = state.reshape(P, GH * HD)
    pick = np.zeros((P, 3, 2, P))
    for b in range(3):
        for m in range(2):
            for r in range(2):
                pick[(2 * m + r) * 3 + b, b, m, r * HD:(r + 1) * HD] = 1.0
    parts["pick"] = pick.reshape(P, 6 * P)
    t = (np.arange(TT)[None, :] * P + p[:, None])[:, :, None]
    seen = (np.arange(N_CMP) * STRIDE + CMP - 1)[None, None, :] <= t
    parts["cmp_add"] = np.where(seen, 0.0, MASKED).reshape(P, -1)
    parts["cmp_mul"] = (seen * 1.0).reshape(P, -1)
    f1 = np.float32(10000.0) ** (-np.arange(0, 32, 2, dtype=np.float32) / np.float32(32))
    parts["freq1"] = np.array([-f1[i % 32] if i % 32 < 16 else f1[i % 32 - 16] for i in p])[:, None]
    f2 = np.float32(500000.0) ** (-np.arange(0, 16, 2, dtype=np.float32) / np.float32(16))
    parts["freq2"] = np.array([-f2[i % 64] if i % 64 < 8 else (f2[i % 64 - 8] if i % 64 < 16 else 0.0)
                               for i in p])[:, None]
    at, cols, where = 0, [], {}
    for name, a in parts.items():
        where[name] = (at, a.shape[1])
        cols.append(a.astype(np.float32))
        at += a.shape[1]
    return np.ascontiguousarray(np.concatenate(cols, axis=1)), where


class Steps:

    def __init__(self, eng, own):
        self.eng, self.own, self.count = eng, own, {}

    def go(self, ins, sem=None, n=1):
        sem = sem if sem is not None else self.own
        ins.then_inc(sem, n)
        key = id(sem)
        self.count[key] = self.count.get(key, 0) + n
        return self.count[key]

    def __call__(self, ins, sem=None, n=1):
        sem = sem if sem is not None else self.own
        self.eng.wait_ge(sem, self.go(ins, sem, n))


@contextmanager
def stage(nc):
    made = []

    def sem(name):
        h = nc.alloc_semaphore(f"{name}_{nc.next_id()}")
        made.append(h)
        return h

    with ExitStack() as mem:
        def sb(name, shape, dt=F32):
            return mem.enter_context(nc.sbuf_tensor(f"{name}_{nc.next_id()}", shape, dt))
        yield sem, sb
    for h in made:
        nc.gpsimd.sem_clear(h)
    nc.all_engine_barrier()
    for h in made:
        nc.release_semaphore(h)


class WeightRing:

    RAW, SPLIT = 3, 3

    def __init__(self, sem, sb, width=KD * P):
        self.raw = sb("raw", [P, self.RAW, width])
        self.hi = sb("w_hi", [P, self.SPLIT, width], F32R)
        self.lo = sb("w_lo", [P, self.SPLIT, width], F32R)
        self.arrived = [sem(f"raw_arrived{i}") for i in range(self.RAW)]
        self.hi_ready, self.lo_ready, self.used = sem("w_hi_ready"), sem("w_lo_ready"), sem("w_used")

    def load(self, sp, i, pieces):
        if i >= self.RAW:
            sp.wait_ge(self.lo_ready, i - self.RAW + 1)
        for view, src in pieces:
            sp.dma_start(view(self.raw[:, i % self.RAW, :]), src).then_inc(self.arrived[i % self.RAW], 16)

    def split_hi(self, act, i, width, n=1, order=None):
        act.wait_ge(self.arrived[i % self.RAW], 16 * n * (i // self.RAW + 1))
        if i >= self.SPLIT:
            act.wait_ge(self.used, i - self.SPLIT + 1)
        pairs = order(self.raw[:, i % self.RAW, :], self.hi[:, i % self.SPLIT, :]) if order else \
            [(self.raw[:, i % self.RAW, 0:width], self.hi[:, i % self.SPLIT, 0:width])]
        for a, b in pairs:
            last = act.activation(b, a, ACT.Copy)
        last.then_inc(self.hi_ready, 1)

    def split_lo(self, eng, i, width, order=None):
        eng.wait_ge(self.hi_ready, i + 1)
        raw, hi, lo = self.raw[:, i % self.RAW, :], self.hi[:, i % self.SPLIT, :], self.lo[:, i % self.SPLIT, :]
        if order is None:
            raw, hi, lo = raw[:, 0:width], hi[:, 0:width], lo[:, 0:width]
            eng.tensor_tensor(lo, raw, hi.bitcast(F32), ALU.subtract).then_inc(self.lo_ready, 1)
            return
        for (a, b), (_, c) in zip(order(raw, hi), order(raw, lo)):
            last = eng.tensor_tensor(c, a, b.bitcast(F32), ALU.subtract)
        last.then_inc(self.lo_ready, 1)

    def slot(self, i):
        return self.hi[:, i % self.SPLIT, :], self.lo[:, i % self.SPLIT, :]


def matmul3(pe, out, left, right, start, stop, **kw):
    pe.matmul(out, left[0], right[0], start=start, stop=False, **kw)
    pe.matmul(out, left[0], right[1], start=False, stop=False, **kw)
    return pe.matmul(out, left[1], right[0], start=False, stop=stop, **kw)


def conv(dve, do, out, src, taps, bias, last_sem=None):
    n = len(taps)
    if bias is None:
        do(dve.tensor_scalar(out, src, taps[-1], None, ALU.mult))
    else:
        do(dve.tensor_scalar(out, src, taps[-1], bias, ALU.mult, ALU.add))
    for back in range(1, n):
        ins = dve.scalar_tensor_tensor(out=out[:, back:], in0=src[:, :S - back], scalar=taps[n - 1 - back],
                                       in1=out[:, back:], op0=ALU.mult, op1=ALU.add)
        do(ins, last_sem if back == n - 1 else None)


def load_columns(nc, m, groups):
    with stage(nc) as (sem, sb):
        staged = sb("vector_rows", [P, len(groups), P])
        loaded, cleared, turned, copied = sem("loaded"), sem("cleared"), sem("turned"), sem("copied")
        with nc.Block() as block:
            @block.gpsimd
            def _(pool):
                pool.memset(staged[:, :, :], 0.0).then_inc(cleared, 1)

            @block.sync
            def _(sp):
                sp.wait_ge(cleared, 1)
                for g, (_, vectors) in enumerate(groups):
                    at = 0
                    for v in vectors:
                        sp.dma_start(staged[at:at + v.shape[0], g, :], v).then_inc(loaded, 16)
                        at += v.shape[0]

            @block.tensor
            def _(pe):
                pe.wait_ge(loaded, 16 * sum(len(vectors) for _, vectors in groups))
                for g in range(len(groups)):
                    pe.transpose(m.ps[:, g, 0:P], staged[:, g, :], m.ident).then_inc(turned, 1)

            @block.vector
            def _(dve):
                for g, (out, vectors) in enumerate(groups):
                    rows = sum(v.shape[0] for v in vectors)
                    dve.wait_ge(turned, g + 1)
                    dve.tensor_copy(out[:, 0:rows], m.ps[:, g, 0:rows]).then_inc(copied, 1)
                dve.wait_ge(copied, len(groups))


def start_up(nc, m, x, positions, positions_2, table):
    with stage(nc) as (sem, sb):
        loaded, done, act_done, cast, cast2 = (sem(n) for n in ("loaded", "done", "act_done", "cast", "cast2"))
        pos_i = sb("pos_i", [P, 2, S], I32)
        ang = sb("ang", [P, 4, S])
        tmp = sb("tmp", [P, S])
        with nc.Block() as block:
            @block.sync
            def _(sp):
                sp.dma_start(m.table[:, :], table).then_inc(loaded, 16)
                for t in range(TT):
                    sp.dma_start(m.x[:, t, :], x[0, t * P:(t + 1) * P, :]).then_inc(loaded, 16)
                sp.dma_start(pos_i[:, 0, :], positions[0, :].partition_broadcast(P)).then_inc(loaded, 16)
                sp.dma_start(pos_i[:, 1, :], positions_2[0, :].partition_broadcast(P)).then_inc(loaded, 16)

            @block.gpsimd
            def _(pool):
                pool.memset(m.ones[:, :], 1.0).then_inc(cast, 1)

            @block.vector
            def _(dve):
                do = Steps(dve, done)
                dve.wait_ge(loaded, 16 * (TT + 3))
                do(dve.tensor_copy(m.ident_b[:, :], m.ident))
                do(dve.tensor_copy(m.causal_b[:, :], m.causal))
                do(dve.memset(m.eps[:, :], EPS))
                for n, freq in enumerate((m.freq1, m.freq2)):
                    for c in range(2):
                        a = ang[:, 2 * n + c, :]
                        do(dve.tensor_copy(a, pos_i[:, n, :]))
                        do(dve.tensor_scalar(a, a, freq, None, ALU.mult))
                        do(dve.tensor_scalar(tmp[:, :], a, 1.0 / TWO_PI, 0.25 * c, ALU.mult, ALU.add))
                        do(dve.tensor_scalar(tmp[:, :], tmp[:, :], ROUND, ROUND, ALU.add, ALU.subtract))
                        for part in (PI_A, PI_B, PI_C):
                            do(dve.scalar_tensor_tensor(out=a, in0=tmp[:, :], scalar=-part, in1=a,
                                                        op0=ALU.mult, op1=ALU.add))
                        if c:
                            do(dve.tensor_scalar(a, a, float(np.pi / 2), None, ALU.add))
                        do(dve.tensor_scalar(a, a, 3.1415925, -3.1415925, ALU.min, ALU.max), cast2 if n == 1 and c else None)

            @block.scalar
            def _(act):
                act.wait_ge(cast2, 1)
                do = Steps(act, act_done)
                for n, (sin, cos) in enumerate(((m.sin1, m.cos1), (m.sin2, m.cos2))):
                    do(act.activation(sin[:, :], ang[:, 2 * n, :], ACT.Sin))
                    do(act.activation(cos[:, :], ang[:, 2 * n + 1, :], ACT.Sin))


def turn(nc, m, src, gain=None, shift=None):
    with stage(nc) as (sem, sb):
        turned, hi_ready, lo_ready, tmp_ready = (sem(n) for n in ("turned", "hi_ready", "lo_ready", "tmp_ready"))
        tmp = sb("affine", [P, 2, S])
        with nc.Block() as block:
            @block.tensor
            def _(pe):
                for k in range(KD):
                    for t in range(TT):
                        last = pe.transpose(m.ps[:, k, t * P:(t + 1) * P], src[:, t, k * P:(k + 1) * P], m.ident)
                    last.then_inc(turned, 1)

            @block.scalar
            def _(act):
                for k in range(KD):
                    if gain is None:
                        act.wait_ge(turned, k + 1)
                        act.activation(m.xt_hi[:, k, :], m.ps[:, k, :], ACT.Copy).then_inc(hi_ready, 1)
                    else:
                        act.wait_ge(tmp_ready, k + 1)
                        act.activation(m.xt_hi[:, k, :], tmp[:, k % 2, :], ACT.Copy).then_inc(hi_ready, 1)

            @block.vector
            def _(dve):
                def affine(k):
                    dve.wait_ge(turned, k + 1)
                    if k >= 2:
                        dve.wait_ge(lo_ready, k - 1)
                    dve.tensor_scalar(tmp[:, k % 2, :], m.ps[:, k, :], gain[:, k:k + 1], shift[:, k:k + 1],
                                      ALU.mult, ALU.add).then_inc(tmp_ready, 1)

                if gain is not None:
                    affine(0)
                for k in range(KD):
                    if gain is not None and k + 1 < KD:
                        affine(k + 1)
                    whole = m.ps[:, k, :] if gain is None else tmp[:, k % 2, :]
                    dve.wait_ge(hi_ready, k + 1)
                    dve.tensor_tensor(m.xt_lo[:, k, :], whole, m.xt_hi[:, k, :].bitcast(F32), ALU.subtract)\
                        .then_inc(lo_ready, 1)


def rms_scale(nc, m, src, out):
    with stage(nc) as (sem, sb):
        ss = sb("ss", [P, TT])
        r = sb("r", [P, TT])
        junk = sb("junk", [P, 2, D])
        summed, rooted, inverted, scaled = (sem(n) for n in ("summed", "rooted", "inverted", "scaled"))
        with nc.Block() as block:
            @block.scalar
            def _(act):
                do = Steps(act, summed)
                for t in range(TT):
                    do(act.activation(junk[:, t % 2, :], src[:, t, :], ACT.Square, accum_out=ss[:, t:t + 1]))
                act.activation(r[:, :], ss[:, :], ACT.Sqrt, scale=1.0 / D, bias=m.eps[:, 0:1]).then_inc(rooted, 1)

            @block.vector
            def _(dve):
                dve.wait_ge(rooted, 1)
                do = Steps(dve, scaled)
                do(dve.reciprocal(r[:, :], r[:, :]))
                for t in range(TT):
                    do(dve.tensor_scalar(out[:, t, :], src[:, t, :], r[:, t:t + 1], None, ALU.mult))


def token_major(nc, m, l, weight, kt, norm, act_in=None, scale_in=None):
    with stage(nc) as (sem, sb):
        ring = WeightRing(sem, sb)
        own_dve, own_act, a_hi_ready, a_lo_ready, stats, root_ready, rows_in = (
            sem(n) for n in ("own_dve", "own_act", "a_hi_ready", "a_lo_ready", "stats", "root_ready",
                             "rows_in"))
        kind, rows = norm
        if act_in is not None:
            a_hi, a_lo = sb("a_hi", [P, ring.SPLIT, S], F32R), sb("a_lo", [P, ring.SPLIT, S], F32R)
        if kind == "layer":
            gb = sb("gain_bias", [P, 2, D])
        st = sb("bn", [P, TT, 2, 6])
        mv = sb("mean_var", [P, TT, 2])
        r = sb("root", [P, TT])
        tmp = sb("scaled", [P, 2, D])
        y = [m.ps[:, 2 * t:2 * t + 2, :].rearrange("p b n -> p (b n)") for t in range(TT)]
        with nc.Block() as block:
            @block.sync
            def _(sp):
                for k in range(kt):
                    ring.load(sp, k, [(lambda v: v[:, 0:D], weight[l, k * P:(k + 1) * P, :])])
                if kind == "layer":
                    for n, v in enumerate(rows):
                        sp.dma_start(gb[:, n, :], v[l].partition_broadcast(P)).then_inc(rows_in, 16)

            @block.scalar
            def _(act):
                for k in range(kt):
                    ring.split_hi(act, k, D)
                    if act_in is not None:
                        act.activation(a_hi[:, k % ring.SPLIT, :], act_in[:, k, :], ACT.Copy).then_inc(a_hi_ready, 1)
                act.wait_ge(ring.used, kt)
                do = Steps(act, own_act)
                if kind == "rms":
                    for t in range(TT):
                        do(act.activation(tmp[:, t % 2, :], y[t], ACT.Square, accum_out=mv[:, t, 1:2]))
                else:
                    act.wait_ge(stats, TT)
                act.activation(r[:, :], mv[:, :, 1], ACT.Sqrt, scale=1.0 / D if kind == "rms" else 1.0,
                               bias=m.eps[:, 0:1]).then_inc(root_ready, 1)

            @block.gpsimd
            def _(pool):
                for k in range(kt):
                    ring.split_lo(pool, k, D)

            @block.tensor
            def _(pe):
                for k in range(kt):
                    pe.wait_ge(ring.lo_ready, k + 1)
                    w_hi, w_lo = ring.slot(k)
                    if act_in is not None:
                        pe.wait_ge(a_lo_ready, k + 1)
                        left = (a_hi[:, k % ring.SPLIT, :], a_lo[:, k % ring.SPLIT, :])
                    else:
                        left = (m.xt_hi[:, k, :], m.xt_lo[:, k, :])
                    for t in range(TT):
                        rows_t = slice(t * P, (t + 1) * P)
                        for a, b in ((0, 0), (0, 1), (1, 0)):
                            for half in range(2):
                                cols = slice(half * S, (half + 1) * S)
                                last = pe.matmul(m.ps[:, 2 * t + half, :], left[a][:, rows_t],
                                                 (w_hi, w_lo)[b][:, cols], start=(k == 0 and a + b == 0),
                                                 stop=(k == kt - 1 and a == 1))
                    last.then_inc(ring.used, 1)

            @block.vector
            def _(dve):
                if act_in is not None:
                    for k in range(kt):
                        dve.wait_ge(a_hi_ready, k + 1)
                        dve.tensor_tensor(a_lo[:, k % ring.SPLIT, :], act_in[:, k, :], a_hi[:, k % ring.SPLIT, :].bitcast(F32),
                                          ALU.subtract).then_inc(a_lo_ready, 1)
                dve.wait_ge(ring.used, kt)
                do = Steps(dve, own_dve)
                if kind == "layer":
                    for t in range(TT):
                        do(dve.scalar_tensor_tensor(out=m.x[:, t, :], in0=m.x[:, t, :], scalar=ALPHA, in1=y[t],
                                                    op0=ALU.mult, op1=ALU.add))
                        for n in range(2):
                            do(dve.bn_stats(st[:, t, n, :], m.x[:, t, n * S:(n + 1) * S]))
                        do(dve.bn_aggr(mv[:, t, :], st[:, t, :, :].rearrange("p a b -> p (a b)")), stats)
                dve.wait_ge(root_ready, 1)
                do(dve.reciprocal(r[:, :], r[:, :]))
                if kind == "layer":
                    dve.wait_ge(rows_in, 32)
                for t in range(TT):
                    xt = m.x[:, t, :]
                    if kind == "layer":
                        do(dve.tensor_scalar(xt, xt, mv[:, t, 0:1], r[:, t:t + 1], ALU.subtract, ALU.mult))
                        do(dve.tensor_tensor(xt, xt, gb[:, 0, :], ALU.mult))
                        do(dve.tensor_tensor(xt, xt, gb[:, 1, :], ALU.add))
                    else:
                        do(dve.scalar_tensor_tensor(out=tmp[:, t % 2, :], in0=y[t], scalar=r[:, t:t + 1],
                                                    in1=rows[:, :], op0=ALU.mult, op1=ALU.mult))
                        do(dve.tensor_tensor(xt, xt, tmp[:, t % 2, :], ALU.add))


def tile_weights(w, l, c0, n=P):
    return w[l, :, c0:c0 + n].rearrange("(k p) c -> p k c", p=P)


def tile_view(v):
    return v[:, 0:KD * P].rearrange("p (k c) -> p k c", k=KD)


def tile_product(pe, m, ring, i, out, cols=P):
    w_hi, w_lo = (tile_view(v) for v in ring.slot(i))
    for k in range(KD):
        last = matmul3(pe, out, (w_hi[:, k, 0:cols], w_lo[:, k, 0:cols]), (m.xt_hi[:, k, :], m.xt_lo[:, k, :]),
                       k == 0, k == KD - 1)
    return last


def in_projection(nc, m, l, w_in, gx_w, ga_w, yr, tb, lat, kpe):
    C = m.cols1
    cw = lambda tap, j: C[:, 8 * tap + j:8 * tap + j + 1]
    col = lambda base, j: C[:, base + j:base + j + 1]
    CB, GXB, GAB, LAM = 32, 40, 48, 56
    tiles = [("x", j, j * P) for j in range(KR)] + [("lat", j, LAT0 + j * P) for j in range(KQ + KKV)] \
        + [("rope", 0, ROPE0)] + [("g", j, D_RNN + j * P) for j in range(KR)] \
        + [("ga", j, GA0 + j * P) for j in range(KD)] + [("gb", j, GB0 + j * P) for j in range(KD)]
    on_act = {"g", "ga", "gb"}
    BANKS = 4
    emptied = []
    for i, (kind, _, _) in enumerate(tiles):
        emptied.append(sum((k in on_act) == (kind in on_act) for k, _, _ in tiles[:i + 1]))
    with stage(nc) as (sem, sb):
        ring = WeightRing(sem, sb)
        act_emptied, dve_emptied, own_dve, own_act, gates_done, gate_w_in, zeroed, lru_ready, tanh_ready, \
            in_ready, mult_ready, gated, ta_ready, cols_ready = (
                sem(n) for n in ("act_emptied", "dve_emptied", "own_dve", "own_act", "gates_done",
                                 "gate_w_in", "zeroed", "lru_ready", "tanh_ready", "in_ready", "mult_ready", "gated",
                                 "ta_ready", "cols_ready"))
        gw = sb("gate_blocks", [P, 2, KR, P])
        xc = sb("x_conv", [P, 2, S])
        th = sb("gate_tanh", [P, 2, 3, S])
        decay = tb
        inp = yr
        mult = sb("mult", [P, KR, S])
        gel = sb("gelu", [P, 2, S])
        tap = sb("gate_a_tanh", [P, 2, S])
        rot = sb("rot", [P, 3, S])
        c = sb("lru_columns", [P, 8, KR])
        def rope_order(raw, out):
            src = tile_view(raw)[:, :, 0:QK_ROPE]
            return [(src, tile_view(out)[:, :, QK_ROPE * q:QK_ROPE * (q + 1)]) for q in range(4)]

        with nc.Block() as block:
            @block.sync
            def _(sp):
                sp.wait_ge(zeroed, 1)
                for n, w in enumerate((gx_w, ga_w)):
                    for r in range(2):
                        blocks = w[l].rearrange("(j r) a b -> r a j b", r=2)
                        sp.dma_start(gw[64 * r:64 * r + 64, n, :, 64 * r:64 * r + 64], blocks[r]).then_inc(gate_w_in, 16)
                for i, (kind, j, c0) in enumerate(tiles):
                    n = QK_ROPE if kind == "rope" else P
                    ring.load(sp, i, [(lambda v, n=n: tile_view(v)[:, :, 0:n], tile_weights(w_in, l, c0, n))])

            @block.gpsimd
            def _(pool):
                pool.memset(gw[:, :, :, :], 0.0).then_inc(zeroed, 1)
                for i, (kind, _, _) in enumerate(tiles):
                    ring.split_lo(pool, i, KD * P, order=rope_order if kind == "rope" else None)

            @block.tensor
            def _(pe):
                def gates(j):
                    pe.wait_ge(dve_emptied, j + 1)
                    if j >= 2:
                        pe.wait_ge(tanh_ready, j - 1)
                    for n in range(2):
                        last = pe.matmul(m.ps[:, 4 + 2 * (j % 2) + n, :], gw[:, n, j, :], xc[:, j % 2, :],
                                         start=True, stop=True)
                    last.then_inc(gates_done, 1)

                pe.wait_ge(gate_w_in, 64)
                for i, (kind, j, _) in enumerate(tiles):
                    pe.wait_ge(ring.lo_ready, i + 1)
                    if i >= BANKS:
                        pe.wait_ge(act_emptied if tiles[i - BANKS][0] in on_act else dve_emptied, emptied[i - BANKS])
                    tile_product(pe, m, ring, i, m.ps[:, i % BANKS, :]).then_inc(ring.used, 1)
                    if 1 <= i <= KR:
                        gates(i - 1)

            @block.scalar
            def _(act):
                do = Steps(act, own_act)
                lam = C[:, LAM:LAM + KR]
                do(act.activation(c[:, 0, :], lam, ACT.Abs))
                do(act.activation(c[:, 1, :], c[:, 0, :], ACT.Exp, scale=-1.0))
                act.activation(c[:, 2, :], c[:, 1, :], ACT.Ln, bias=1.0).then_inc(cols_ready, 1)
                for i in range(2):
                    ring.split_hi(act, i, KD * P)

                def gate(j):
                    act.wait_ge(gates_done, j + 1)
                    if j == 0:
                        act.wait_ge(lru_ready, 1)
                    if j >= 2:
                        act.wait_ge(in_ready, j - 1)
                    b = 4 + 2 * (j % 2)
                    t3 = th[:, j % 2, :, :]
                    do.go(act.activation(t3[:, 0, :], m.ps[:, b, :], ACT.Tanh, scale=0.5, bias=c[:, 4, j:j + 1]))
                    do(act.activation(t3[:, 1, :], m.ps[:, b + 1, :], ACT.Tanh, scale=0.5, bias=c[:, 5, j:j + 1]))
                    do.go(act.activation(decay[:, j, :], t3[:, 1, :], ACT.Exp, scale=c[:, 7, j:j + 1],
                                         bias=c[:, 7, j:j + 1]))
                    do(act.activation(t3[:, 2, :], t3[:, 1, :], ACT.Tanh, scale=c[:, 6, j:j + 1],
                                      bias=c[:, 6, j:j + 1]), tanh_ready)

                for i, (kind, j, _) in enumerate(tiles):
                    if i + 2 < len(tiles):
                        ring.split_hi(act, i + 2, KD * P, order=rope_order if tiles[i + 2][0] == "rope" else None)
                    if 1 <= i <= KR:
                        gate(i - 1)
                    if i == KR + 1:
                        act.wait_ge(in_ready, KR)
                        do(act.activation(mult[:, :, :], mult[:, :, :], ACT.Sqrt, scale=0.5), mult_ready)
                    if kind in on_act:
                        act.wait_ge(ring.used, i + 1)
                    if kind == "g":
                        if j >= 2:
                            act.wait_ge(gated, j - 1)
                        do(act.activation(gel[:, j % 2, :], m.ps[:, i % BANKS, :], ACT.Gelu_apprx_tanh), act_emptied)
                    if kind == "ga":
                        if j >= 2:
                            act.wait_ge(ta_ready, j - 1)
                        do(act.activation(tap[:, j % 2, :], m.ps[:, i % BANKS, :], ACT.Tanh, scale=0.5), act_emptied)
                    if kind == "gb":
                        if j == 0:
                            act.wait_ge(ta_ready, 1)
                        do(act.activation(tb[:, j, :], m.ps[:, i % BANKS, :], ACT.Tanh, scale=0.5), act_emptied)

            @block.vector
            def _(dve):
                do = Steps(dve, own_dve)
                lam = C[:, LAM:LAM + KR]
                do(dve.tensor_scalar(c[:, 4, :], C[:, GXB:GXB + KR], 0.5, None, ALU.mult))
                do(dve.tensor_scalar(c[:, 5, :], C[:, GAB:GAB + KR], 0.5, None, ALU.mult))
                dve.wait_ge(cols_ready, 1)
                e, ln = c[:, 1, :], c[:, 2, :]
                do(dve.tensor_scalar(c[:, 0, :], e, 1.0, None, ALU.add))
                do(dve.tensor_scalar(c[:, 3, :], c[:, 0, :], 1.0, None, ALU.is_equal))
                do(dve.tensor_scalar(c[:, 0, :], c[:, 0, :], -1.0, None, ALU.add))
                do(dve.tensor_tensor(c[:, 0, :], c[:, 0, :], c[:, 3, :], ALU.add))
                do(dve.reciprocal(c[:, 0, :], c[:, 0, :]))
                do(dve.tensor_tensor(ln, ln, c[:, 3, :], ALU.add))
                do(dve.tensor_tensor(ln, ln, e, ALU.mult))
                do(dve.tensor_tensor(ln, ln, c[:, 0, :], ALU.mult))
                do(dve.tensor_scalar(c[:, 0, :], lam, -1.0, 0.0, ALU.mult, ALU.max))
                do(dve.tensor_tensor(ln, ln, c[:, 0, :], ALU.add))
                do(dve.tensor_scalar(c[:, 6, :], ln, LRU_C / 2, None, ALU.mult))
                do(dve.tensor_scalar(c[:, 7, :], ln, -LRU_C / 2, None, ALU.mult), lru_ready)

                def after_gates(j):
                    dve.wait_ge(tanh_ready, j + 1)
                    t3 = th[:, j % 2, :, :]
                    do(dve.scalar_tensor_tensor(out=inp[:, j, :], in0=t3[:, 0, :], scalar=1.0, in1=xc[:, j % 2, :],
                                                op0=ALU.add, op1=ALU.mult))
                    do(dve.tensor_scalar(mult[:, j, :], t3[:, 2, :], 1.0, None, ALU.add))
                    do(dve.reciprocal(mult[:, j, :], mult[:, j, :]))
                    do(dve.tensor_tensor(mult[:, j, :], mult[:, j, :], t3[:, 2, :], ALU.mult), in_ready)

                def recur(j):
                    do(dve.tensor_tensor(inp[:, j, :], inp[:, j, :], mult[:, j, :], ALU.mult))
                    do(dve.tensor_tensor_scan(mult[:, j, :], decay[:, j, :], inp[:, j, :], 0.0, ALU.mult, ALU.add))

                for i, (kind, j, _) in enumerate(tiles):
                    ps = m.ps[:, i % BANKS, :]
                    if kind not in on_act:
                        dve.wait_ge(ring.used, i + 1)
                    if kind == "x":
                        conv(dve, do, xc[:, j % 2, :], ps, [cw(tap_, j) for tap_ in range(CONV)], col(CB, j), dve_emptied)
                    if 1 <= i <= KR:
                        after_gates(i - 1)
                    if kind == "lat":
                        do(dve.tensor_copy(lat[:, j, :], ps), dve_emptied)
                    if kind == "rope":
                        do(dve.tensor_copy(rot[:, 0, :], ps), dve_emptied)
                        do(dve.stream_shuffle(rot[:, 1, :], rot[:, 0, :], SWAP16))
                        do(dve.tensor_tensor(rot[:, 0, :], rot[:, 0, :], m.cos1[:, :], ALU.mult))
                        do(dve.tensor_tensor(rot[:, 1, :], rot[:, 1, :], m.sin1[:, :], ALU.mult))
                        do(dve.tensor_tensor(kpe[:, :], rot[:, 0, :], rot[:, 1, :], ALU.add))
                        dve.wait_ge(mult_ready, 1)
                    if kind == "g":
                        recur(j)
                        dve.wait_ge(act_emptied, j + 1)
                        do(dve.tensor_tensor(yr[:, j, :], mult[:, j, :], gel[:, j % 2, :], ALU.mult), gated)
                    if kind == "ga":
                        dve.wait_ge(act_emptied, KR + j + 1)
                        do(dve.scalar_tensor_tensor(out=yr[:, j, :], in0=tap[:, j % 2, :], scalar=1.0,
                                                    in1=yr[:, j, :], op0=ALU.add, op1=ALU.mult), ta_ready)


SWAP16 = [(i + 16) % 32 for i in range(32)]
SWAP8 = [i + 8 if i < 8 else i - 8 if i < 16 else i for i in range(32)]


def mla_latents(nc, m, lat):
    C = m.cols1
    QG = 64
    n_lat = KQ + KKV
    with stage(nc) as (sem, sb):
        own_dve, own_act, squared, summed, rooted, lat_ready, lat_hi = (
            sem(n) for n in ("own_dve", "own_act", "squared", "summed", "rooted", "lat_ready", "lat_hi"))
        sq = sb("squares", [P, 2, S])
        root = sb("root", [P, 2, S])
        with nc.Block() as block:
            @block.scalar
            def _(act):
                do = Steps(act, own_act)
                for j in range(n_lat):
                    if j >= 2:
                        act.wait_ge(summed, j - 1)
                    do(act.activation(sq[:, j % 2, :], lat[:, j, :], ACT.Square), squared)
                act.wait_ge(summed, n_lat)
                do(act.activation(root[:, 0, :], m.ps[:, 6, :], ACT.Sqrt, scale=1.0 / Q_LORA, bias=m.eps[:, 0:1]))
                do(act.activation(root[:, 1, :], m.ps[:, 7, :], ACT.Sqrt, scale=1.0 / KV_LORA, bias=m.eps[:, 0:1]), rooted)
                for j in range(n_lat):
                    act.wait_ge(lat_ready, j + 1)
                    do(act.activation(m.xt_hi[:, j, :], lat[:, j, :], ACT.Copy), lat_hi)

            @block.tensor
            def _(pe):
                for j in range(n_lat):
                    pe.wait_ge(squared, j + 1)
                    bank = 6 if j < KQ else 7
                    pe.matmul(m.ps[:, bank, :], m.ones[:, :], sq[:, j % 2, :], start=j in (0, KQ),
                              stop=j in (KQ - 1, n_lat - 1)).then_inc(summed, 1)

            @block.vector
            def _(dve):
                do = Steps(dve, own_dve)
                dve.wait_ge(rooted, 1)
                do(dve.reciprocal(root[:, :, :], root[:, :, :]))
                for j in range(n_lat):
                    do(dve.scalar_tensor_tensor(out=lat[:, j, :], in0=lat[:, j, :], scalar=C[:, QG + j:QG + j + 1],
                                                in1=root[:, int(j >= KQ), :], op0=ALU.mult, op1=ALU.mult), lat_ready)
                for j in range(n_lat):
                    dve.wait_ge(lat_hi, j + 1)
                    do(dve.tensor_tensor(m.xt_lo[:, j, :], lat[:, j, :], m.xt_hi[:, j, :].bitcast(F32), ALU.subtract))


HG = 4


def mla_heads(nc, m, l, first, groups, w_uq, w_ukv, kpe, q_all, k_all, v_all):
    with stage(nc) as (sem, sb):
        ring = WeightRing(sem, sb, HG * QK * KQ)
        own_dve, own_act, out_ready, dve_emptied, act_emptied, spread, roped, v_ready, v_out = (
            sem(n) for n in ("own_dve", "own_act", "out_ready", "dve_emptied", "act_emptied", "spread", "roped",
                             "v_ready", "v_out"))
        rot = sb("rot", [P, 2, 2, S])
        q_pe = sb("q_pe", [P, 2, S])
        WQ, WK = HG * QK, HG * (QK_NOPE + V_HEAD)

        def by_part(raw, out, kt, width, cut):
            r = raw[:, 0:kt * width].rearrange("p (k h e) -> p k h e", k=kt, h=HG)
            o = out[:, 0:kt * width].rearrange("p (k c) -> p k c", k=kt)
            pairs = []
            for k in range(kt):
                pairs.append((r[:, k, :, 0:cut], o[:, k, 0:HG * cut].rearrange("p (h e) -> p h e", h=HG)))
                pairs.append((r[:, k, :, cut:], o[:, k, HG * cut:].rearrange("p (h e) -> p h e", h=HG)))
            return pairs

        uq_order = lambda raw, out: by_part(raw, out, KQ, WQ, QK_NOPE)
        ukv_order = lambda raw, out: by_part(raw, out, KKV, WK, QK_NOPE)

        with nc.Block() as block:
            @block.sync
            def _(sp):
                for g in range(groups):
                    h0 = first + g * HG
                    wq = w_uq[l, :, h0 * QK:(h0 + HG) * QK].rearrange("(k p) c -> p k c", p=P)
                    ring.load(sp, 2 * g, [(lambda v: v[:, 0:KQ * WQ].rearrange("p (k c) -> p k c", k=KQ), wq)])
                    wk = w_ukv[l, :, h0 * P:(h0 + HG) * P].rearrange("(k p) c -> p k c", p=P)
                    ring.load(sp, 2 * g + 1, [(lambda v: v[:, 0:KKV * WK].rearrange("p (k c) -> p k c", k=KKV), wk)])
                for h in range(groups * HG):
                    sp.dma_start(k_all[QK_NOPE:QK, h, :], kpe[0:QK_ROPE, :]).then_inc(spread, 16)
                for g in range(groups):
                    sp.wait_ge(roped, g + 1)
                    for h in range(HG):
                        sp.dma_start(q_all[QK_NOPE:QK, g * HG + h, :],
                                     q_pe[32 * h:32 * h + 32, g % 2, :]).then_inc(spread, 16)
                sp.wait_ge(spread, 16 * 2 * groups * HG)

            @block.gpsimd
            def _(pool):
                for g in range(groups):
                    ring.split_lo(pool, 2 * g, 0, order=uq_order)
                    ring.split_lo(pool, 2 * g + 1, 0, order=ukv_order)

            @block.scalar
            def _(act):
                do = Steps(act, own_act)

                def split(c):
                    if c < 2 * groups:
                        ring.split_hi(act, c, 0, order=ukv_order if c % 2 else uq_order)

                for c in range(3):
                    split(c)
                for g in range(groups):
                    for n, i in enumerate((0, 1, 3, 4)):
                        if n == 2:
                            split(2 * g + 3)
                        act.wait_ge(out_ready, 5 * g + i + 1)
                        to = q_all if n < 2 else k_all
                        ps = m.ps[:, (5 * g + i) % 6, :]
                        for r in range(2):
                            h = g * HG + 2 * (n % 2) + r
                            do(act.activation(to[0:QK_NOPE, h, :], ps[64 * r:64 * r + 64, :], ACT.Copy),
                               act_emptied if r else None)
                    split(2 * g + 4)

            @block.vector
            def _(dve):
                do = Steps(dve, own_dve)
                for g in range(groups):
                    dve.wait_ge(out_ready, 5 * g + 3)
                    a, b = rot[:, g % 2, 0, :], rot[:, g % 2, 1, :]
                    do(dve.tensor_copy(a, m.ps[:, (5 * g + 2) % 6, :]), dve_emptied)
                    do(dve.stream_shuffle(b, a, SWAP16))
                    do(dve.tensor_tensor(a, a, m.cos1[:, :], ALU.mult))
                    do(dve.tensor_tensor(b, b, m.sin1[:, :], ALU.mult))
                    do(dve.tensor_tensor(q_pe[:, g % 2, :], a, b, ALU.add), roped)
                    dve.wait_ge(v_ready, g + 1)
                    vg = m.ps[:, 6:8, :].rearrange("p b (t c) -> p (b t) c", t=2)
                    do(dve.tensor_copy(v_all[:, :, g * HG * V_HEAD:(g + 1) * HG * V_HEAD], vg), v_out)

            @block.tensor
            def _(pe):
                def emptied(i):
                    g, n = divmod(i, 5)
                    if n == 2:
                        pe.wait_ge(dve_emptied, g + 1)
                    else:
                        pe.wait_ge(act_emptied, 4 * g + (1, 2, 0, 3, 4)[n])

                for g in range(groups):
                    for n in range(5):
                        i = 5 * g + n
                        if n in (0, 3):
                            pe.wait_ge(ring.lo_ready, 2 * g + 1 + (n == 3))
                        if i >= 6:
                            emptied(i - 6)
                        kt, k0, wide = (KQ, 0, WQ) if n < 3 else (KKV, KQ, WK)
                        w = [v[:, 0:kt * wide].rearrange("p (k c) -> p k c", k=kt) for v in ring.slot(2 * g + (n >= 3))]
                        c0 = (n if n < 3 else n - 3) * P
                        for k in range(kt):
                            last = matmul3(pe, m.ps[:, i % 6, :], (w[0][:, k, c0:c0 + P], w[1][:, k, c0:c0 + P]),
                                           (m.xt_hi[:, k0 + k, :], m.xt_lo[:, k0 + k, :]), k == 0, k == kt - 1)
                        last.then_inc(out_ready, 1)
                        if n == 2:
                            pe.wait_ge(out_ready, i + 1)
                            pe.sem_inc(ring.used, 1)
                    if g:
                        pe.wait_ge(v_out, g)
                    for t in range(TT):
                        out = m.ps[:, 6 + t // 2, 256 * (t % 2):256 * (t % 2) + 256]
                        for k in range(KKV):
                            left = [v[:, KQ + k, t * P:(t + 1) * P] for v in (m.xt_hi, m.xt_lo)]
                            last = matmul3(pe, out, left, (w[0][:, k, HG * QK_NOPE:], w[1][:, k, HG * QK_NOPE:]),
                                           k == 0, k == KKV - 1)
                    last.then_inc(v_ready, 1)
                    pe.wait_ge(v_ready, g + 1)
                    pe.sem_inc(ring.used, 1)


def attention(nc, m, heads, scale, finish):
    with stage(nc) as (sem, sb):
        scored, peaked, exped, normed, turned, copied, valued, finished, own_dve = (
            sem(n) for n in ("scored", "peaked", "exped", "normed", "turned", "copied", "valued", "finished",
                             "own_dve"))
        SCORES, PROBS, TURNED = 4, 8, 3
        LAG_TURN, LAG_COPY, LAG_VALUES = 4, 5, 6
        p = sb("probs", [P, PROBS, S])
        pt = sb("probs_turned", [P, TURNED, S])
        st = sb("softmax", [P, 4, 8])
        U = len(heads) * TT
        with nc.Block() as block:
            @block.tensor
            def _(pe):
                def score(u):
                    h, t = divmod(u, TT)
                    q, k, _ = heads[h]
                    n = (t + 1) * P
                    if u >= SCORES:
                        pe.wait_ge(exped, u - SCORES + 1)
                    bank = m.ps[:, u % SCORES, :]
                    pe.matmul(bank[:, 0:n], q[:, t * P:(t + 1) * P], k[:, 0:n], start=True, stop=True)
                    pe.matmul(bank[:, t * P:n], m.ident_b[:, :], m.causal_b[:, :], start=False, stop=True,
                              skip_group_check=True).then_inc(scored, 1)

                def turn_probs(u):
                    pe.wait_ge(normed, u + 1)
                    if u >= 2:
                        pe.wait_ge(copied, u - 1)
                    for b in range(u % TT + 1):
                        last = pe.transpose(m.ps[:, 4 + u % 2, b * P:(b + 1) * P],
                                            p[:, u % PROBS, b * P:(b + 1) * P], m.ident)
                    last.then_inc(turned, 1)

                def values(u):
                    h, t = divmod(u, TT)
                    pe.wait_ge(copied, u + 1)
                    if t == 0 and h >= 2:
                        pe.wait_ge(finished, h - 1)
                    for b in range(t + 1):
                        last = pe.matmul(m.ps[:, 6 + h % 2, t * P:(t + 1) * P], heads[h][2](b),
                                         pt[:, u % TURNED, b * P:(b + 1) * P], start=(b == 0), stop=(b == t))
                    last.then_inc(valued, 1)

                for u in range(U + LAG_VALUES):
                    if u < U:
                        score(u)
                    if 0 <= u - LAG_TURN < U:
                        turn_probs(u - LAG_TURN)
                    if 0 <= u - LAG_VALUES < U:
                        values(u - LAG_VALUES)

            @block.vector
            def _(dve):
                do = Steps(dve, own_dve)
                for u in range(U + LAG_VALUES + 2):
                    if u < U:
                        n = (u % TT + 1) * P
                        dve.wait_ge(scored, u + 1)
                        do(dve.tensor_reduce(st[:, 3, u % 8:u % 8 + 1], m.ps[:, u % SCORES, 0:n], AX.X, ALU.max))
                        do.go(dve.tensor_scalar(st[:, 0, u % 8:u % 8 + 1], st[:, 3, u % 8:u % 8 + 1], -scale, None,
                                                ALU.mult), peaked)
                    v = u - 1
                    if 0 <= v < U:
                        n = (v % TT + 1) * P
                        dve.wait_ge(exped, v + 1)
                        do(dve.reciprocal(st[:, 2, v % 8:v % 8 + 1], st[:, 1, v % 8:v % 8 + 1]))
                        do.go(dve.tensor_scalar(p[:, v % PROBS, 0:n], p[:, v % PROBS, 0:n], st[:, 2, v % 8:v % 8 + 1],
                                                None, ALU.mult), normed)
                    w = u - LAG_VALUES - 1
                    if w >= 0 and w % TT == TT - 1:
                        h = w // TT
                        dve.wait_ge(valued, (h + 1) * TT)
                        finish(dve, do, h, m.ps[:, 6 + h % 2, :], finished)

            @block.scalar
            def _(act):
                for u in range(U + LAG_COPY):
                    if u < U:
                        n = (u % TT + 1) * P
                        act.wait_ge(peaked, u + 1)
                        if u >= PROBS:
                            act.wait_ge(turned, u - PROBS + 1)
                        act.activation(p[:, u % PROBS, 0:n], m.ps[:, u % SCORES, 0:n], ACT.Exp, scale=scale,
                                       bias=st[:, 0, u % 8:u % 8 + 1], accum_out=st[:, 1, u % 8:u % 8 + 1])\
                            .then_inc(exped, 1)
                    v = u - LAG_COPY
                    if v >= 0:
                        n = (v % TT + 1) * P
                        act.wait_ge(turned, v + 1)
                        if v >= TURNED:
                            act.wait_ge(valued, v - TURNED + 1)
                        act.activation(pt[:, v % TURNED, 0:n], m.ps[:, 4 + v % 2, 0:n], ACT.Copy).then_inc(copied, 1)


def split_merged(nc, m, src, scale):
    with stage(nc) as (sem, sb):
        hi, lo = sem("hi"), sem("lo")
        with nc.Block() as block:
            @block.scalar
            def _(act):
                for k in range(KD):
                    act.activation(m.xt_hi[:, k, :], src[:, k, :], ACT.Copy, scale=scale).then_inc(hi, 1)

            @block.vector
            def _(dve):
                for k in range(KD):
                    dve.wait_ge(hi, k + 1)
                    dve.scalar_tensor_tensor(out=m.xt_lo[:, k, :], in0=src[:, k, :], scalar=scale,
                                             in1=m.xt_hi[:, k, :].bitcast(F32), op0=ALU.mult,
                                             op1=ALU.subtract).then_inc(lo, 1)


MOD_COLS = 1536


def conv_up(nc, m, l, w_up, w_mod, hid):
    tap = lambda n, j: m.cols2[n][:, j:j + 1]
    with stage(nc) as (sem, sb):
        ring = WeightRing(sem, sb)
        own, conved, gelued, emptied, mod_used, mod_summed, mod_copied = (
            sem(n) for n in ("own", "conved", "gelued", "emptied", "mod_used", "mod_summed", "mod_copied"))
        mod_in = [sem(f"mod_in{i}") for i in range(2)]
        buf = sb("convolved", [P, 2, 2, S])
        gel = sb("gelu", [P, 2, S])
        w_m = sb("w_mod", [P, 2, MOD_COLS])
        acc = sb("mod_acc", [P, N_MOD * D])
        BANKS, TILES = 6, 2 * KF
        PARTS = N_MOD * D // MOD_COLS
        CHUNKS = KD * PARTS
        LAG = 4
        with nc.Block() as block:
            @block.sync
            def _(sp):
                for i in range(TILES):
                    j, half = divmod(i, 2)
                    ring.load(sp, i, [(tile_view, tile_weights(w_up, l, half * D_FF + j * P))])
                    c = i - LAG - 2
                    if 0 <= c < CHUNKS:
                        k, part = divmod(c, PARTS)
                        if c >= 2:
                            sp.wait_ge(mod_used, c - 1)
                        sp.dma_start(w_m[:, c % 2, :], w_mod[l, k * P:(k + 1) * P, part * MOD_COLS:(part + 1) * MOD_COLS])\
                            .then_inc(mod_in[c % 2], 16)

            @block.gpsimd
            def _(pool):
                for i in range(TILES):
                    ring.split_lo(pool, i, KD * P)

            @block.tensor
            def _(pe):
                for i in range(TILES):
                    pe.wait_ge(ring.lo_ready, i + 1)
                    if i >= BANKS:
                        pe.wait_ge(emptied, i - BANKS + 1)
                    tile_product(pe, m, ring, i, m.ps[:, i % BANKS, :]).then_inc(ring.used, 1)
                pe.wait_ge(mod_used, CHUNKS)
                for j in range(N_MOD * KD):
                    last = pe.matmul(m.ps[:, 6, j:j + 1], acc[:, j * P:(j + 1) * P], m.ones[:, 0:1], start=True,
                                     stop=True)
                last.then_inc(mod_summed, 1)

            @block.vector
            def _(dve):
                do = Steps(dve, own)
                for i in range(TILES + 1):
                    j, half = divmod(i, 2)
                    if i < TILES:
                        dve.wait_ge(ring.used, i + 1)
                        if half == 0 and j >= 2:
                            dve.wait_ge(gelued, j - 1)
                        conv(dve, do, buf[:, j % 2, half, :], m.ps[:, i % BANKS, :],
                             [tap(n, half * KF + j) for n in range(FFN_CONV)], tap(3, half * KF + j), emptied)
                    c = i - LAG
                    if 0 <= c < CHUNKS:
                        k, part = divmod(c, PARTS)
                        dve.wait_ge(mod_in[c % 2], 16 * (c // 2 + 1))
                        to, w, silu = acc[:, part * MOD_COLS:(part + 1) * MOD_COLS], w_m[:, c % 2, :], m.cond[:, k:k + 1]
                        if k == 0:
                            do(dve.tensor_scalar(to, w, silu, None, ALU.mult), mod_used)
                        else:
                            do(dve.scalar_tensor_tensor(out=to, in0=w, scalar=silu, in1=to, op0=ALU.mult,
                                                        op1=ALU.add), mod_used)
                    if half == 0 and j:
                        dve.wait_ge(gelued, j)
                        do(dve.tensor_tensor(hid[:, j - 1, :], gel[:, (j - 1) % 2, :], buf[:, (j - 1) % 2, 1, :],
                                             ALU.mult), conved)
                dve.wait_ge(mod_summed, 1)
                do(dve.tensor_copy(m.mod_sum[:, l, :], m.ps[:, 6, 0:N_MOD * KD]), mod_copied)

            @block.scalar
            def _(act):
                for i in range(2):
                    ring.split_hi(act, i, KD * P)
                for i in range(TILES + 1):
                    if i + 2 < TILES:
                        ring.split_hi(act, i + 2, KD * P)
                    if i % 2:
                        j = i // 2
                        act.wait_ge(emptied, 2 * j + 1)
                        if j >= 2:
                            act.wait_ge(conved, j - 1)
                        act.activation(gel[:, j % 2, :], buf[:, j % 2, 0, :], ACT.Gelu_apprx_tanh).then_inc(gelued, 1)


def relu_up(nc, m, l, w_up, hid):
    with stage(nc) as (sem, sb):
        ring = WeightRing(sem, sb)
        emptied, squared = sem("emptied"), sem("squared")
        pos = sb("positive", [P, 2, S])
        BANKS = 6
        with nc.Block() as block:
            @block.sync
            def _(sp):
                for i in range(KF2):
                    ring.load(sp, i, [(tile_view, tile_weights(w_up, l, i * P))])

            @block.gpsimd
            def _(pool):
                for i in range(KF2):
                    ring.split_lo(pool, i, KD * P)

            @block.tensor
            def _(pe):
                for i in range(KF2):
                    pe.wait_ge(ring.lo_ready, i + 1)
                    if i >= BANKS:
                        pe.wait_ge(emptied, i - BANKS + 1)
                    tile_product(pe, m, ring, i, m.ps[:, i % BANKS, :]).then_inc(ring.used, 1)

            @block.vector
            def _(dve):
                for i in range(KF2):
                    dve.wait_ge(ring.used, i + 1)
                    if i >= 2:
                        dve.wait_ge(squared, i - 1)
                    dve.tensor_scalar(pos[:, i % 2, :], m.ps[:, i % BANKS, :], 0.0, None, ALU.max).then_inc(emptied, 1)
                    dve.wait_ge(emptied, i + 1)
                    dve.tensor_tensor(hid[:, i, :], pos[:, i % 2, :], pos[:, i % 2, :], ALU.mult).then_inc(squared, 1)

            @block.scalar
            def _(act):
                for i in range(KF2):
                    ring.split_hi(act, i, KD * P)


def silu_of_condition(nc, m, c_2):
    raw = m.cond_raw
    load_columns(nc, m, [(raw, [c_2[0].rearrange("(k p) -> k p", p=P)])])
    with stage(nc) as (sem, sb):
        tanh, own = sem("tanh"), sem("own")
        with nc.Block() as block:
            @block.scalar
            def _(act):
                act.activation(m.cond[:, :], raw[:, :], ACT.Tanh, scale=0.5).then_inc(tanh, 1)

            @block.vector
            def _(dve):
                do = Steps(dve, own)
                dve.wait_ge(tanh, 1)
                do(dve.scalar_tensor_tensor(out=m.cond[:, :], in0=m.cond[:, :], scalar=1.0, in1=raw[:, :],
                                            op0=ALU.add, op1=ALU.mult))
                do(dve.tensor_scalar(m.cond[:, :], m.cond[:, :], 0.5, None, ALU.mult))


def modulation(nc, m, l):
    C = m.cols3
    NG, BM = 15, 47
    with stage(nc) as (sem, sb):
        own, diag_ready, spread = (sem(n) for n in ("own", "diag_ready", "spread"))
        diag = sb("diag", [P, 2, P])
        with nc.Block() as block:
            @block.tensor
            def _(pe):
                for i in range(2 * KD):
                    pe.wait_ge(diag_ready, i + 1)
                    b, c = divmod(i, 4)
                    pe.matmul(m.ps[:, 2 + b, c * P:(c + 1) * P], m.ones[:, :], diag[:, i % 2, :],
                              start=True, stop=True).then_inc(spread, 1)

            @block.vector
            def _(dve):
                do = Steps(dve, own)
                do(dve.tensor_tensor(m.mod[:, :], m.mod_sum[:, l, :], C[:, BM:BM + N_MOD * KD], ALU.add))
                for n, (sc, g) in enumerate(((1, 0), (4, 2))):
                    do(dve.scalar_tensor_tensor(out=m.in_gain[:, n, :], in0=m.mod[:, sc * KD:(sc + 1) * KD], scalar=1.0,
                                                in1=C[:, NG + g * KD:NG + (g + 1) * KD], op0=ALU.add, op1=ALU.mult))
                for n, (gt, g) in enumerate(((2, 1), (5, 3))):
                    do(dve.tensor_tensor(m.out_gain[:, n, :], m.mod[:, gt * KD:(gt + 1) * KD],
                                         C[:, NG + g * KD:NG + (g + 1) * KD], ALU.mult))
                for i in range(2 * KD):
                    n, k = divmod(i, KD)
                    if i >= 2:
                        dve.wait_ge(spread, i - 1)
                    do(dve.tensor_scalar(diag[:, i % 2, :], m.ident, m.out_gain[:, n, k:k + 1], None, ALU.mult),
                       diag_ready)
                dve.wait_ge(spread, 2 * KD)
                for n in range(2):
                    do(dve.tensor_copy(m.gain_rows[:, n, :],
                                       m.ps[:, 2 + 2 * n:4 + 2 * n, :].rearrange("p b c -> p (b c)")))


FM = {"ah": 0, "ab": 2, "ac": 4, "q": 6, "cmp": 8, "slc": 9, "win": 10, "small": 11, "lq": 12, "lk": 13, "lg": 14,
      "mu": 16}
FM_TILES = [[(0, i * P, P)] for i in range(9)] \
    + [[(0, O_KV + 2 * HD, HD), (HD, O_KV + 2 * HD, HD)], [(0, O_KV + 4 * HD, HD), (HD, O_KV + 4 * HD, HD)],
       [(0, O_G, DK), (DK, O_LR, RANK)], [(0, O_LQ, P)], [(0, O_LK, P)], [(0, O_LG, P)], [(0, O_LG + P, P)],
       [(0, O_MU, P)], [(0, O_MU + P, P)]]
TM_COLS = [(0, O_KV + 3 * HD, HD), (HD, O_KV + 5 * HD, HD), (2 * HD, O_LV, GW), (2 * HD + GW, O_MV, GW)]
TM = 2 * HD + 2 * GW


def in_projection_2(nc, m, l, w_in, fm):
    with stage(nc) as (sem, sb):
        ring = WeightRing(sem, sb)
        emptied = sem("emptied")
        arrivals = [0] * WeightRing.RAW
        want = []
        for i, cols in enumerate(FM_TILES):
            arrivals[i % WeightRing.RAW] += 16 * len(cols)
            want.append(arrivals[i % WeightRing.RAW])
        rows = lambda i: FM_TILES[i][-1][0] + FM_TILES[i][-1][2]
        BANKS = 6
        narrow = lambda v, i: tile_view(v)[:, :, 0:rows(i)]
        with nc.Block() as block:
            @block.sync
            def _(sp):
                for i, cols in enumerate(FM_TILES):
                    ring.load(sp, i, [(lambda v, a=a, n=n: tile_view(v)[:, :, a:a + n], tile_weights(w_in, l, c, n))
                                      for a, c, n in cols])

            @block.scalar
            def _(act):
                for i in range(len(FM_TILES)):
                    act.wait_ge(ring.arrived[i % ring.RAW], want[i])
                    if i >= ring.SPLIT:
                        act.wait_ge(ring.used, i - ring.SPLIT + 1)
                    act.activation(narrow(ring.hi[:, i % ring.SPLIT, :], i), narrow(ring.raw[:, i % ring.RAW, :], i),
                                   ACT.Copy).then_inc(ring.hi_ready, 1)

            @block.gpsimd
            def _(pool):
                for i in range(len(FM_TILES)):
                    ring.split_lo(pool, i, 0, order=lambda raw, out, i=i: [(narrow(raw, i), narrow(out, i))])

            @block.tensor
            def _(pe):
                for i in range(len(FM_TILES)):
                    pe.wait_ge(ring.lo_ready, i + 1)
                    if i >= BANKS:
                        pe.wait_ge(emptied, i - BANKS + 1)
                    tile_product(pe, m, ring, i, m.ps[0:rows(i), i % BANKS, :], rows(i)).then_inc(ring.used, 1)

            @block.vector
            def _(dve):
                for i in range(len(FM_TILES)):
                    dve.wait_ge(ring.used, i + 1)
                    dve.tensor_copy(fm[0:rows(i), i, :], m.ps[0:rows(i), i % BANKS, :]).then_inc(emptied, 1)


def in_projection_tokens(nc, m, l, w_in, tm):
    A = 2 * HD + GW
    with stage(nc) as (sem, sb):
        ring = WeightRing(sem, sb)
        done = sem("done")
        with nc.Block() as block:
            @block.sync
            def _(sp):
                for k in range(KD):
                    ring.load(sp, k, [(lambda v, a=a, n=n: v[:, a:a + n], w_in[l, k * P:(k + 1) * P, c:c + n])
                                      for a, c, n in TM_COLS])

            @block.scalar
            def _(act):
                for k in range(KD):
                    ring.split_hi(act, k, TM, n=len(TM_COLS))

            @block.gpsimd
            def _(pool):
                for k in range(KD):
                    ring.split_lo(pool, k, TM)

            @block.tensor
            def _(pe):
                for k in range(KD):
                    pe.wait_ge(ring.lo_ready, k + 1)
                    w = ring.slot(k)
                    for t in range(TT):
                        left = [v[:, k, t * P:(t + 1) * P] for v in (m.xt_hi, m.xt_lo)]
                        matmul3(pe, m.ps[:, t, 0:A], left, (w[0][:, 0:A], w[1][:, 0:A]), k == 0, k == KD - 1)
                        last = matmul3(pe, m.ps[:, TT + t, 0:GW], left, (w[0][:, A:TM], w[1][:, A:TM]),
                                       k == 0, k == KD - 1)
                    last.then_inc(ring.used, 1)

            @block.vector
            def _(dve):
                dve.wait_ge(ring.used, KD)
                for t in range(TT):
                    dve.tensor_copy(tm[:, t, 0:A], m.ps[:, t, 0:A]).then_inc(done, 1)
                    dve.tensor_copy(tm[:, t, A:TM], m.ps[:, TT + t, 0:GW]).then_inc(done, 1)
                dve.wait_ge(done, 2 * TT)


def short_conv_and_rotary(nc, m, fm, tm, merged, qr, kz, vd, gates):
    C = m.cols3
    with stage(nc) as (sem, sb):
        own, zeroed, tanh, sig_ready, spread, copied = (sem(n) for n in ("own", "zeroed", "tanh", "sig_ready",
                                                                        "spread", "copied"))
        a = sb("a", [P, 2, S])
        sig = sb("sig", [P, S])
        with nc.Block() as block:
            @block.gpsimd
            def _(pool):
                pool.memset(kz[:, :, :, :], 0.0).then_inc(zeroed, 1)

            @block.scalar
            def _(act):
                act.activation(sig[0:3 * GH, :], fm[0:3 * GH, FM["small"], :], ACT.Tanh, scale=0.5).then_inc(tanh, 1)
                for i in range(6):
                    act.wait_ge(spread, i + 1)
                    act.activation(gates[:, i, :], m.ps[:, i, :], ACT.Copy).then_inc(copied, 1)

            @block.tensor
            def _(pe):
                pe.wait_ge(sig_ready, 1)
                for i in range(6):
                    pe.matmul(m.ps[:, i, :], m.pick[0:3 * GH, i * P:(i + 1) * P], sig[0:3 * GH, :],
                              start=True, stop=True).then_inc(spread, 1)

            @block.vector
            def _(dve):
                do = Steps(dve, own)
                dve.wait_ge(tanh, 1)
                do(dve.tensor_scalar(sig[0:3 * GH, :], sig[0:3 * GH, :], 0.5, 0.5, ALU.mult, ALU.add), sig_ready)
                for j in range(2):
                    do(dve.tensor_tensor(a[:, 0, :], fm[:, FM["ac"] + j, :], fm[:, FM["ah"] + j, :], ALU.mult))
                    conv(dve, do, a[:, 1, :], a[:, 0, :], [C[:, 2 * n + j:2 * n + j + 1] for n in range(CONV2)], None)
                    do(dve.tensor_tensor(merged[:, j, :], a[:, 1, :], fm[:, FM["ab"] + j, :], ALU.mult))
                dve.wait_ge(zeroed, 1)
                for n, src in enumerate((FM["q"], FM["q"] + 1, FM["slc"], FM["win"])):
                    do(dve.stream_shuffle(a[:, 0, :], fm[:, src, :], SWAP8))
                    do(dve.tensor_tensor(a[:, 0, :], a[:, 0, :], m.sin2[:, :], ALU.mult))
                    do(dve.tensor_tensor(a[:, 1, :], fm[:, src, :], m.cos2[:, :], ALU.mult))
                    if n < 2:
                        do(dve.tensor_tensor(qr[:, n, :], a[:, 0, :], a[:, 1, :], ALU.add))
                    else:
                        for r in range(2):
                            half = slice(64 * r, 64 * r + 64)
                            do(dve.tensor_tensor(kz[half, n - 2, r, :], a[half, 0, :], a[half, 1, :], ALU.add))
                for b in range(2):
                    for r in range(2):
                        do(dve.tensor_copy(vd[:, b, :, r * HD:(r + 1) * HD], tm[:, :, b * HD:(b + 1) * HD]))


def compressed(nc, m, l, cmp_pos, cmp_w1, cmp_w2, fm, gates, merged):
    scale = HD ** -0.5
    N = N_CMP
    with stage(nc) as (sem, sb):
        w_in, zeroed, pos_turned, own, z_ready, hid_done, tanh, hid_ready, kv_done, kv_ready, scored, shifted, exped, \
            p_ready, turned, pct_ready, valued = (
                sem(n) for n in ("w_in", "zeroed", "pos_turned", "own", "z_ready", "hid_done", "tanh", "hid_ready",
                                 "kv_done", "kv_ready", "scored", "shifted", "exped", "p_ready", "turned",
                                 "pct_ready", "valued"))
        w1 = sb("w1", [P, CMP, P])
        w2 = sb("w2", [P, 2, P])
        pos = sb("pos", [CMP, P])
        pos_t = sb("pos_t", [P, CMP])
        z = sb("windows", [P, N, CMP])
        hid = sb("hidden", [P, 2, 32])
        th = sb("hidden_tanh", [P, 2, 32])
        kc = sb("kc", [P, 2, 32])
        vc = sb("vc", [32, P])
        sc = sb("scores", [P, GH * TT, N])
        st = sb("sums", [P, 2, GH * TT])
        pct = sb("probs_turned", [32, GH, S])
        with nc.Block() as block:
            @block.gpsimd
            def _(pool):
                pool.memset(kc[:, :, :], 0.0).then_inc(zeroed, 1)

            @block.sync
            def _(sp):
                for j in range(2):
                    rows = slice(j * HD, (j + 1) * HD)
                    sp.dma_start(pos[:, rows], cmp_pos[l, j]).then_inc(w_in, 16)
                    sp.dma_start(w1[rows, :, :], cmp_w1[l, j].rearrange("(r d) c -> d r c", d=HD)).then_inc(w_in, 16)
                    for r in range(2):
                        sp.dma_start(w2[:, j, r * HD:(r + 1) * HD], cmp_w2[l, j]).then_inc(w_in, 16)

            @block.tensor
            def _(pe):
                pe.wait_ge(w_in, 16 * 8)
                pe.transpose(m.ps[:, 0, 0:CMP], pos[:, :], m.ident[0:CMP, 0:CMP]).then_inc(pos_turned, 1)
                pe.wait_ge(z_ready, 1)
                for j in range(2):
                    rows = slice(j * HD, (j + 1) * HD)
                    for r in range(CMP):
                        last = pe.matmul(m.ps[:, 1 + j, 0:N], w1[rows, r, :], z[rows, :, r], start=(r == 0),
                                         stop=(r == CMP - 1))
                last.then_inc(hid_done, 1)
                pe.wait_ge(hid_ready, 1)
                pe.matmul(m.ps[:, 3, 0:N], w2[:, 0, :], hid[:, 0, 0:N], start=True, stop=True)
                pe.matmul(m.ps[0:N, 4, 0:P], hid[:, 1, 0:N], w2[:, 1, :], start=True, stop=True).then_inc(kv_done, 1)
                pe.wait_ge(kv_ready, 1)
                for u in range(GH * TT):
                    h, t = divmod(u, TT)
                    last = pe.matmul(m.ps[:, 5, u * N:(u + 1) * N], fm[:, FM["q"] + h // 2, t * P:(t + 1) * P],
                                     kc[:, h % 2, 0:N], start=True, stop=True)
                last.then_inc(scored, 1)
                pe.wait_ge(p_ready, 1)
                for u in range(GH * TT):
                    h, t = divmod(u, TT)
                    last = pe.transpose(m.ps[0:N, h, t * P:(t + 1) * P], sc[:, u, :], m.ident)
                last.then_inc(turned, 1)
                for h in range(GH):
                    pe.wait_ge(pct_ready, h + 1)
                    pe.matmul(m.ps[:, 4 + h, :], vc[0:N, :], pct[0:N, h, :], start=True, stop=True).then_inc(valued, 1)

            @block.scalar
            def _(act):
                act.wait_ge(hid_done, 1)
                act.activation(th[:, :, 0:N], m.ps[:, 1:3, 0:N], ACT.Tanh, scale=0.5).then_inc(tanh, 1)
                act.wait_ge(shifted, 1)
                act.activation(sc[:, :, :], sc[:, :, :], ACT.Exp, scale=scale).then_inc(exped, 1)
                act.wait_ge(turned, 1)
                for h in range(GH):
                    act.activation(pct[0:N, h, :], m.ps[0:N, h, :], ACT.Copy).then_inc(pct_ready, 1)

            @block.vector
            def _(dve):
                do = Steps(dve, own)
                dve.wait_ge(pos_turned, 1)
                do(dve.tensor_copy(pos_t[:, :], m.ps[:, 0, 0:CMP]))
                blocks = fm[:, FM["cmp"], :].rearrange("p (n r) -> p n r", r=STRIDE)
                for a in range(2):
                    add = pos_t[:, a * STRIDE:(a + 1) * STRIDE].unsqueeze(1).to_broadcast([P, N, STRIDE])
                    do(dve.tensor_tensor(z[:, :, a * STRIDE:(a + 1) * STRIDE], blocks[:, a:a + N, :], add, ALU.add),
                       z_ready if a else None)
                dve.wait_ge(tanh, 1)
                do(dve.scalar_tensor_tensor(out=hid[:, :, 0:N], in0=th[:, :, 0:N], scalar=1.0, in1=m.ps[:, 1:3, 0:N],
                                            op0=ALU.add, op1=ALU.mult))
                do(dve.tensor_scalar(hid[:, :, 0:N], hid[:, :, 0:N], 0.5, None, ALU.mult), hid_ready)
                dve.wait_ge(kv_done, 1)
                dve.wait_ge(zeroed, 1)
                for r in range(2):
                    half = slice(64 * r, 64 * r + 64)
                    do(dve.tensor_copy(kc[half, r, 0:N], m.ps[half, 3, 0:N]))
                do(dve.tensor_copy(vc[0:N, :], m.ps[0:N, 4, 0:P]), kv_ready)
                dve.wait_ge(scored, 1)
                ps = m.ps[:, 5, 0:GH * TT * N].rearrange("p (h c) -> p h c", h=GH)
                s4 = sc[:, :, :].rearrange("p (h t) n -> p h (t n)", h=GH)
                over_heads = lambda v: v.unsqueeze(1).to_broadcast([P, GH, TT * N])
                over_keys = lambda v: v.unsqueeze(2).to_broadcast([P, GH * TT, N])
                do(dve.tensor_tensor(s4, ps, over_heads(m.cmp_add), ALU.add))
                do(dve.tensor_reduce(st[:, 0, :], sc[:, :, :], AX.X, ALU.max))
                do(dve.tensor_tensor(sc[:, :, :], sc[:, :, :], over_keys(st[:, 0, :]), ALU.subtract), shifted)
                dve.wait_ge(exped, 1)
                do(dve.tensor_reduce(st[:, 1, :], sc[:, :, :], AX.X, ALU.add))
                do(dve.reciprocal(st[:, 1, :], st[:, 1, :]))
                do(dve.tensor_tensor(sc[:, :, :], sc[:, :, :], over_keys(st[:, 1, :]), ALU.mult))
                do(dve.tensor_tensor(s4, s4, over_heads(m.cmp_mul), ALU.mult), p_ready)
                for h in range(GH):
                    dve.wait_ge(valued, h + 1)
                    half = slice(64 * (h % 2), 64 * (h % 2) + 64)
                    do(dve.tensor_tensor(merged[half, 2 + h // 2, :], m.ps[half, 4 + h, :], gates[half, h // 2, :],
                                         ALU.mult))


def linear_attention(nc, m, l, gate_w2, fm, tm, merged):
    C = m.cols3
    GB = 6
    with stage(nc) as (sem, sb):
        w_in, own, own_act, gate_done, ln_ready, scan_ready, diffed, exp_ready, scaled, att_done, att_ready, kl_turned, \
            kl_ready, kv_done, kv_used, state_ready, zeroed, o_done, squared, summed, rooted, silu = (
                sem(n) for n in ("w_in", "own", "own_act", "gate_done", "ln_ready", "scan_ready", "diffed",
                                 "exp_ready", "scaled", "att_done", "att_ready", "kl_turned", "kl_ready", "kv_done",
                                 "kv_used", "state_ready", "zeroed", "o_done", "squared", "summed", "rooted", "silu"))
        w2 = sb("gate_w2", [DK + RANK, P])
        la = sb("log_a", [P, 3, S])
        carry = sb("carry", [P, S])
        b = sb("cum", [P, 3, S])
        e = sb("exps", [P, 4, S])
        qk = sb("scaled_qk", [P, 4, S])
        att = sb("att", [P, GH, TT, P])
        vz = sb("vz", [P, TT, GH, P])
        klz = sb("klz", [P, 2, TT, P])
        state = sb("state", [P, NCH, GW])
        kvm = sb("kvm", [P, GW])
        sq = sb("sq", [P, 2, S])
        r = sb("root", [P, 2, S])
        chunks = lambda v: v.rearrange("p (n c) -> p n c", c=CHUNK)
        at = lambda c: chunks(b[:, 0, :])[:, :, c:c + 1].to_broadcast([P, NCH, CHUNK])
        with nc.Block() as block:
            @block.sync
            def _(sp):
                sp.dma_start(w2[DK:DK + RANK, :], gate_w2[l]).then_inc(w_in, 16)

            @block.gpsimd
            def _(pool):
                pool.memset(carry[:, :], 1.0).then_inc(zeroed, 1)
                pool.wait_ge(zeroed, 1)
                pool.memset(chunks(carry[:, :])[:, :, 0:1], 0.0).then_inc(zeroed, 1)
                pool.memset(klz[:, :, :, :], 0.0).then_inc(zeroed, 1)
                pool.memset(att[:, :, :, :], 0.0).then_inc(zeroed, 1)
                pool.memset(vz[:, :, :, :], 0.0).then_inc(zeroed, 1)
                pool.memset(state[:, 0, :], 0.0).then_inc(zeroed, 1)
                pool.wait_ge(zeroed, 6)
                for h in range(GH):
                    c0 = (h % 2) * HD
                    pool.tensor_copy(vz[:, :, h, c0:c0 + HD], tm[:, :, 2 * HD + h * HD:2 * HD + (h + 1) * HD])\
                        .then_inc(zeroed, 1)

            @block.scalar
            def _(act):
                do = Steps(act, own_act)
                act.wait_ge(gate_done, 1)
                do(act.activation(la[:, 0, :], m.ps[:, 0, :], ACT.Identity, bias=C[:, GB:GB + 1]))
                do(act.activation(la[:, 1, :], la[:, 0, :], ACT.Abs))
                do(act.activation(la[:, 1, :], la[:, 1, :], ACT.Exp, scale=-1.0))
                do(act.activation(la[:, 1, :], la[:, 1, :], ACT.Ln, bias=1.0), ln_ready)
                act.wait_ge(diffed, 1)
                do(act.activation(e[:, 0, :], b[:, 1, :], ACT.Exp))
                do(act.activation(e[:, 1, :], b[:, 1, :], ACT.Exp, scale=-1.0))
                do(act.activation(e[:, 2, :], b[:, 2, :], ACT.Exp, scale=-1.0))
                do(act.activation(e[:, 3, :], b[:, 0, :], ACT.Exp), exp_ready)
                for j in range(2):
                    do(act.activation(la[:, 1 + j, :], fm[:, FM["lg"] + j, :], ACT.Tanh, scale=0.5), silu)
                act.wait_ge(o_done, 1)
                for j in range(2):
                    do(act.activation(sq[:, j, :], m.ps[:, 4 + j, :], ACT.Square), squared)
                act.wait_ge(summed, 2)
                do(act.activation(r[:, :, :], m.ps[:, 0:2, :], ACT.Sqrt, scale=1.0 / HD, bias=m.eps[:, 0:1]), rooted)

            @block.vector
            def _(dve):
                do = Steps(dve, own)
                dve.wait_ge(ln_ready, 1)
                do(dve.scalar_tensor_tensor(out=la[:, 2, :], in0=la[:, 0, :], scalar=0.0, in1=la[:, 1, :],
                                            op0=ALU.min, op1=ALU.subtract))
                do(dve.tensor_scalar(la[:, 2, :], la[:, 2, :], 1.0 / TAU, None, ALU.mult))
                dve.wait_ge(zeroed, 6 + GH)
                do(dve.tensor_tensor_scan(b[:, 0, :], carry[:, :], la[:, 2, :], 0.0, ALU.mult, ALU.add))
                do(dve.tensor_tensor(chunks(b[:, 1, :]), chunks(b[:, 0, :]), at(CHUNK // 2), ALU.subtract))
                do(dve.tensor_tensor(chunks(b[:, 2, :]), chunks(b[:, 0, :]), at(CHUNK - 1), ALU.subtract), diffed)
                dve.wait_ge(exp_ready, 1)
                q, k = fm[:, FM["lq"], :], fm[:, FM["lk"], :]
                stt = lambda out, x, s, y, sem=None: do(dve.scalar_tensor_tensor(
                    out=out, in0=x, scalar=s, in1=y, op0=ALU.mult, op1=ALU.mult), sem)
                stt(qk[:, 2, :], k, 1.0, e[:, 2, :], scaled)
                stt(qk[:, 1, :], k, 1.0, e[:, 1, :], scaled)
                stt(qk[:, 0, :], q, DK ** -0.5, e[:, 0, :], scaled)
                stt(qk[:, 3, :], q, DK ** -0.5, e[:, 3, :], scaled)
                dve.wait_ge(kl_turned, 1)
                for par in range(2):
                    half = slice(64 * par, 64 * par + 64)
                    do(dve.tensor_copy(klz[half, par, :, :], m.ps[half, 6, :].rearrange("p (t c) -> p t c", t=TT)),
                       kl_ready)
                for h in range(GH):
                    dve.wait_ge(att_done, h + 1)
                    for par in range(2):
                        half = slice(64 * par, 64 * par + 64)
                        src = m.ps[half, h, :].rearrange("p (t c) -> p t c", t=TT)[:, :, half]
                        do(dve.tensor_scalar(att[half, h, :, half], src, 3e38, -3e38, ALU.min, ALU.max))
                    do(dve.tensor_tensor(att[:, h, :, :], att[:, h, :, :],
                                         m.chunk.unsqueeze(1).to_broadcast([P, TT, P]), ALU.mult), att_ready)
                for n in range(NCH - 1):
                    dve.wait_ge(kv_done, n + 1)
                    do(dve.tensor_tensor(kvm[:, :], m.ps[:, 6 + n % 2, 0:GW], m.state_mask, ALU.mult), kv_used)
                    decay = e[:, 3, (n + 1) * CHUNK - 1:(n + 1) * CHUNK]
                    do(dve.scalar_tensor_tensor(out=state[:, n + 1, :], in0=state[:, n, :], scalar=decay,
                                                in1=kvm[:, :], op0=ALU.mult, op1=ALU.add), state_ready)
                dve.wait_ge(silu, 2)
                for j in range(2):
                    do(dve.scalar_tensor_tensor(out=la[:, 1 + j, :], in0=la[:, 1 + j, :], scalar=1.0,
                                                in1=fm[:, FM["lg"] + j, :], op0=ALU.add, op1=ALU.mult))
                dve.wait_ge(rooted, 1)
                do(dve.reciprocal(r[:, :, :], r[:, :, :]))
                for j in range(2):
                    stt(r[:, j, :], r[:, j, :], 0.5, la[:, 1 + j, :])
                    do(dve.tensor_tensor(merged[:, 4 + j, :], m.ps[:, 4 + j, :], r[:, j, :], ALU.mult))

            @block.tensor
            def _(pe):
                pe.wait_ge(w_in, 16)
                pe.matmul(m.ps[:, 0, :], w2[DK:DK + RANK, :], fm[DK:DK + RANK, FM["small"], :], start=True,
                          stop=True).then_inc(gate_done, 1)
                pe.wait_ge(scaled, 1)
                for t in range(TT):
                    last = pe.transpose(m.ps[:, 6, t * P:(t + 1) * P], qk[:, 2, t * P:(t + 1) * P], m.ident)
                last.then_inc(kl_turned, 1)
                pe.wait_ge(scaled, 3)
                for h in range(GH):
                    rows = slice(DK * h, DK * h + DK)
                    for t in range(TT):
                        tok = slice(t * P, (t + 1) * P)
                        last = pe.matmul(m.ps[:, h, tok], qk[rows, 1, tok], qk[rows, 0, tok], start=True, stop=True,
                                         tile_position=(DK * h, 0))
                    last.then_inc(att_done, 1)
                pe.wait_ge(kl_ready, 2)
                for n in range(NCH - 1):
                    if n >= 2:
                        pe.wait_ge(kv_used, n - 1)
                    pe.matmul(m.ps[:, 6 + n % 2, 0:GW], klz[:, n % 2, n // 2, :], tm[:, n // 2, 2 * HD:2 * HD + GW],
                              start=True, stop=True).then_inc(kv_done, 1)
                pe.wait_ge(att_ready, GH)
                pe.wait_ge(scaled, 4)
                pe.wait_ge(state_ready, NCH - 1)
                for j in range(2):
                    first = True
                    for t in range(TT):
                        for h in (2 * j, 2 * j + 1):
                            pe.matmul(m.ps[:, 4 + j, t * P:(t + 1) * P], vz[:, t, h, :], att[:, h, t, :],
                                      start=first, stop=False, skip_group_check=True)
                            first = False
                        for n in (2 * t, 2 * t + 1):
                            if n:
                                last = pe.matmul(m.ps[:, 4 + j, n * CHUNK:(n + 1) * CHUNK],
                                                 state[:, n, j * P:(j + 1) * P], qk[:, 3, n * CHUNK:(n + 1) * CHUNK],
                                                 start=False, stop=(n == NCH - 1), skip_group_check=True)
                last.then_inc(o_done, 1)
                for j in range(2):
                    pe.wait_ge(squared, j + 1)
                    pe.matmul(m.ps[:, j, :], m.halves, sq[:, j, :], start=True, stop=True).then_inc(summed, 1)


def spatial_gate(nc, m, l, ws, bias, fm, tm, merged):
    G = TT * GH
    with stage(nc) as (sem, sb):
        w_in, zeroed, turned, own, w_ready, v_ready, mixed, rooted, summed = (
            sem(n) for n in ("w_in", "zeroed", "turned", "own", "w_ready", "v_ready", "mixed", "rooted", "summed"))
        w = sb("ws", [P, GH, P])
        wt = sb("ws_turned", [P, GH, P])
        bs = sb("bias", [P, 2, P])
        v = sb("v", [P, TT, GW])
        sq = sb("sq", [P, TT, GW])
        vz = sb("vz", [P, TT, GH, P])
        st = sb("st", [P, 2, G])
        tmp = sb("tmp", [P, 2, S])
        by_group = lambda a: a.rearrange("p t (g c) -> p (t g) c", c=HD)
        wide = lambda a: a.unsqueeze(2).to_broadcast([P, G, HD])
        with nc.Block() as block:
            @block.sync
            def _(sp):
                sp.dma_start(w[:, :, :], ws[l].rearrange("g t s -> t g s")).then_inc(w_in, 16)
                for g in range(GH):
                    r = g % 2
                    sp.dma_start(bs[64 * r:64 * r + 64, g // 2, :], bias[l, g].partition_broadcast(64)).then_inc(w_in, 16)

            @block.gpsimd
            def _(pool):
                pool.memset(vz[:, :, :, :], 0.0).then_inc(zeroed, 1)

            @block.scalar
            def _(act):
                act.wait_ge(summed, 1)
                act.activation(st[:, 1, :], st[:, 1, :], ACT.Sqrt, scale=1.0 / HD, bias=m.eps[:, 0:1]).then_inc(rooted, 1)

            @block.tensor
            def _(pe):
                pe.wait_ge(w_in, 16 * (1 + GH))
                for g in range(GH):
                    last = pe.transpose(m.ps[:, 0, g * P:(g + 1) * P], w[:, g, :], m.ident)
                last.then_inc(turned, 1)
                pe.wait_ge(v_ready, 1)
                for j in range(2):
                    for t in range(TT):
                        for r in range(2):
                            last = pe.matmul(m.ps[:, 1 + j, t * P:(t + 1) * P], vz[:, t, 2 * j + r, :],
                                             wt[:, 2 * j + r, :], start=(r == 0), stop=(r == 1))
                    last.then_inc(mixed, 1)

            @block.vector
            def _(dve):
                do = Steps(dve, own)
                dve.wait_ge(turned, 1)
                do(dve.tensor_tensor(wt[:, :, :], m.ps[:, 0, :].rearrange("p (g c) -> p g c", g=GH),
                                     m.upper.unsqueeze(1).to_broadcast([P, GH, P]), ALU.mult))
                src = tm[:, :, 2 * HD + GW:TM]
                s3 = src.rearrange("p t (g c) -> p t g c", c=HD)
                v3, q3 = by_group(v[:, :, :]), by_group(sq[:, :, :])
                do(dve.tensor_copy(v[:, :, :], src))
                do(dve.tensor_reduce(st[:, 0, :], v3, AX.X, ALU.add))
                do(dve.tensor_scalar(st[:, 0, :], st[:, 0, :], 1.0 / HD, None, ALU.mult))
                do(dve.tensor_tensor(v3, v3, wide(st[:, 0, :]), ALU.subtract))
                do(dve.tensor_tensor(q3, v3, v3, ALU.mult))
                do(dve.tensor_reduce(st[:, 1, :], q3, AX.X, ALU.add), summed)
                dve.wait_ge(rooted, 1)
                dve.wait_ge(zeroed, 1)
                do(dve.reciprocal(st[:, 1, :], st[:, 1, :]))
                do(dve.tensor_tensor(v3, v3, wide(st[:, 1, :]), ALU.mult))
                for r in range(2):
                    do(dve.tensor_copy(vz[:, :, r::2, r * HD:(r + 1) * HD],
                                       v[:, :, :].rearrange("p t (g c) -> p t g c", c=HD)[:, :, r::2, :]),
                       v_ready if r else None)
                for j in range(2):
                    dve.wait_ge(mixed, j + 1)
                    ps = m.ps[:, 1 + j, :].rearrange("p (t c) -> p t c", t=TT)
                    out = tmp[:, j, :].rearrange("p (t c) -> p t c", t=TT)
                    do(dve.tensor_tensor(out, ps, bs[:, j, :].unsqueeze(1).to_broadcast([P, TT, P]), ALU.add))
                    do(dve.tensor_tensor(merged[:, 6 + j, :], tmp[:, j, :], fm[:, FM["mu"] + j, :], ALU.mult))


def group_norms(nc, m, merged):
    C = m.cols3
    GG = 7
    with stage(nc) as (sem, sb):
        squared, summed, rooted, own, own_act = (sem(n) for n in ("squared", "summed", "rooted", "own", "own_act"))
        sq = sb("sq", [P, 2, S])
        r = sb("root", [P, 4, S])
        with nc.Block() as block:
            @block.scalar
            def _(act):
                do = Steps(act, own_act)
                for k in range(KD):
                    if k >= 2:
                        act.wait_ge(summed, k - 1)
                    do(act.activation(sq[:, k % 2, :], merged[:, k, :], ACT.Square), squared)
                act.wait_ge(summed, KD)
                do(act.activation(r[:, :, :], m.ps[:, 0:4, :], ACT.Sqrt, scale=1.0 / GW, bias=m.eps[:, 0:1]), rooted)

            @block.tensor
            def _(pe):
                for k in range(KD):
                    pe.wait_ge(squared, k + 1)
                    pe.matmul(m.ps[:, k // 2, :], m.ones[:, :], sq[:, k % 2, :], start=(k % 2 == 0),
                              stop=(k % 2 == 1)).then_inc(summed, 1)

            @block.vector
            def _(dve):
                do = Steps(dve, own)
                dve.wait_ge(rooted, 1)
                do(dve.reciprocal(r[:, :, :], r[:, :, :]))
                for k in range(KD):
                    do(dve.scalar_tensor_tensor(out=merged[:, k, :], in0=merged[:, k, :],
                                                scalar=C[:, GG + k:GG + k + 1], in1=r[:, k // 2, :], op0=ALU.mult,
                                                op1=ALU.mult))


def first_block_layer(nc, m, l, a):
    rows = lambda v: v[l].rearrange("(k p) -> k p", p=P)
    taps = a["ffn_conv_w"][l].rearrange("n (k p) -> n k p", p=P)
    load_columns(nc, m, [(m.cols1, [a["conv_w"][l].rearrange("n (k p) -> (n k) p", p=P)]
                          + [rows(a[v]) for v in ("conv_b", "gx_b", "ga_b", "lru_lambda", "q_norm_g", "kv_norm_g")])]
                 + [(m.cols2[n], [taps[n]]) for n in range(FFN_CONV)] + [(m.cols2[FFN_CONV], [rows(a["ffn_conv_b"])])])
    turn(nc, m, m.x)
    with ExitStack() as mem:
        sb = lambda name, shape: mem.enter_context(nc.sbuf_tensor(f"{name}_{nc.next_id()}", shape, F32))
        yr, tb, kpe = sb("y_rnn", [P, KD, S]), sb("gate_b_tanh", [P, KD, S]), sb("k_pe", [P, S])
        with nc.sbuf_tensor(f"lat_{nc.next_id()}", [P, KQ + KKV, S], F32) as lat:
            in_projection(nc, m, l, a["w_in"], a["gx_w"], a["ga_w"], yr, tb, lat, kpe)
            mla_latents(nc, m, lat)
        HALF = HEADS // 2
        q_all, k_all = sb("q_all", [QK, HALF, S]), sb("k_all", [QK, HALF, S])
        v_all = sb("v_all", [P, TT, HALF * V_HEAD])
        tmp = sb("gated", [P, S])
        for first in (0, HALF):
            mla_heads(nc, m, l, first, HALF // HG, a["w_uq"], a["w_ukv"], kpe, q_all, k_all, v_all)

            def finish(dve, do, h, out, sem):
                half, tile = slice(64 * (h % 2), 64 * (h % 2) + 64), (first + h) // 2
                do(dve.scalar_tensor_tensor(out=tmp[half, :], in0=tb[half, tile, :], scalar=1.0, in1=out[half, :],
                                            op0=ALU.add, op1=ALU.mult))
                do(dve.tensor_tensor(yr[half, tile, :], yr[half, tile, :], tmp[half, :], ALU.add), sem)

            values = lambda h: lambda b: v_all[:, b, (h // 2) * P:(h // 2 + 1) * P]
            attention(nc, m, [(q_all[:, h, :], k_all[:, h, :], values(h)) for h in range(HALF)], MLA_SCALE, finish)
        split_merged(nc, m, yr, 0.5)
    token_major(nc, m, l, a["w_out"], KD, ("layer", (a["ln1_g"], a["ln1_b"])))
    turn(nc, m, m.x)
    with nc.sbuf_tensor(f"hidden_{nc.next_id()}", [P, KF, S], F32) as hid:
        conv_up(nc, m, l, a["w_up"], a["w_mod_2"], hid)
        token_major(nc, m, l, a["w_down"], KF, ("layer", (a["ln2_g"], a["ln2_b"])), act_in=hid)


def second_block_layer(nc, m, l, a):
    rows = lambda v: v[l].rearrange("(k p) -> k p", p=P)
    load_columns(nc, m, [(m.cols3, [a["conv_w_2"][l].rearrange("n (k p) -> (n k) p", p=P), rows(a["gla_gate_b_2"]),
                                   rows(a["grp_gain_2"]), a["norm_g_2"][l].rearrange("n (k p) -> (n k) p", p=P),
                                   rows(a["b_mod_2"])])])
    modulation(nc, m, l)
    with ExitStack() as mem:
        sb = lambda name, shape: mem.enter_context(nc.sbuf_tensor(f"{name}_{nc.next_id()}", shape, F32))
        with nc.sbuf_tensor(f"normed_{nc.next_id()}", [P, TT, D], F32) as xn:
            rms_scale(nc, m, m.x, xn)
            turn(nc, m, xn, m.in_gain[:, 0, :], m.mod[:, 0:KD])
        merged = sb("merged", [P, KD, S])
        fm, tm = sb("features_major", [P, len(FM_TILES), S]), sb("token_major", [P, TT, TM])
        in_projection_2(nc, m, l, a["w_in_2"], fm)
        in_projection_tokens(nc, m, l, a["w_in_2"], tm)
        with ExitStack() as nsa:
            sbn = lambda name, shape: nsa.enter_context(nc.sbuf_tensor(f"{name}_{nc.next_id()}", shape, F32))
            qr, kz, vd, gates = sbn("qr", [P, 2, S]), sbn("kz", [P, 2, 2, S]), sbn("vd", [P, 2, TT, P]), \
                sbn("gates", [P, 6, S])
            tmp = sbn("gated", [P, S])
            short_conv_and_rotary(nc, m, fm, tm, merged, qr, kz, vd, gates)
            compressed(nc, m, l, a["cmp_pos_2"], a["cmp_w1_2"], a["cmp_w2_2"], fm, gates, merged)

            def finish(dve, do, n, out, sem):
                branch, h = divmod(n, GH)
                half, tile = slice(64 * (h % 2), 64 * (h % 2) + 64), h // 2
                do(dve.tensor_tensor(tmp[half, :], out[half, :], gates[half, 2 * (branch + 1) + tile, :], ALU.mult))
                do(dve.tensor_tensor(merged[half, 2 + tile, :], merged[half, 2 + tile, :], tmp[half, :], ALU.add), sem)

            values = lambda branch: lambda b: vd[:, branch, b, :]
            attention(nc, m, [(qr[:, h // 2, :], kz[:, branch, h % 2, :], values(branch))
                              for branch in range(2) for h in range(GH)], HD ** -0.5, finish)
        linear_attention(nc, m, l, a["gla_gate_w2_2"], fm, tm, merged)
        spatial_gate(nc, m, l, a["gmlp_ws_2"], a["gmlp_b_2"], fm, tm, merged)
        group_norms(nc, m, merged)
        split_merged(nc, m, merged, 1.0)
    token_major(nc, m, l, a["w_o_2"], KD, ("rms", m.gain_rows[:, 0, :]))
    with nc.sbuf_tensor(f"normed_{nc.next_id()}", [P, TT, D], F32) as xn:
        rms_scale(nc, m, m.x, xn)
        turn(nc, m, xn, m.in_gain[:, 1, :], m.mod[:, 3 * KD:4 * KD])
    with nc.sbuf_tensor(f"hidden_{nc.next_id()}", [P, KF2, S], F32) as hid:
        relu_up(nc, m, l, a["w_up_2"], hid)
        token_major(nc, m, l, a["w_down_2"], KF2, ("rms", m.gain_rows[:, 1, :]), act_in=hid)


class Memory:
    pass


def program(nc, a, table, where, out):
    m = Memory()
    with ExitStack() as ctx:
        def sb(name, shape, dt=F32):
            return ctx.enter_context(nc.sbuf_tensor(name, shape, dt))
        m.ps = ctx.enter_context(nc.psum_tensor("ps", [P, 8, S], F32))
        m.x = sb("x_tokens", [P, TT, D])
        m.xt_hi, m.xt_lo = sb("xt_hi", [P, KD, S], F32R), sb("xt_lo", [P, KD, S], F32R)
        m.table = sb("table", [P, table.shape[1]])
        part = lambda name: m.table[:, where[name][0]:where[name][0] + where[name][1]]
        m.ident, m.causal, m.upper, m.chunk, m.halves, m.pick = (
            part(name) for name in ("ident", "causal", "upper", "chunk", "halves", "pick"))
        m.cmp_add, m.cmp_mul, m.freq1, m.freq2, m.state_mask = (
            part(name) for name in ("cmp_add", "cmp_mul", "freq1", "freq2", "state"))
        m.ones, m.eps = sb("ones", [P, P]), sb("eps", [P, 1])
        m.ident_b, m.causal_b = sb("ident_b", [P, P], BF16), sb("causal_b", [P, P], BF16)
        m.sin1, m.cos1, m.sin2, m.cos2 = (sb(n, [P, S]) for n in ("sin1", "cos1", "sin2", "cos2"))
        start_up(nc, m, a["x"], a["positions"], a["positions_2"], table)
        m.cond_raw, m.cond, m.mod_sum = sb("cond_raw", [P, KD]), sb("cond", [P, KD]), \
            sb("mod_sum", [P, DEPTH, N_MOD * KD])
        silu_of_condition(nc, m, a["c_2"])
        with nc.sbuf_tensor("cols1", [P, 69], F32) as cols1, nc.sbuf_tensor("cols2", [P, FFN_CONV + 1, 2 * KF], F32) as cols2:
            m.cols1, m.cols2 = cols1, [cols2[:, n, :] for n in range(FFN_CONV + 1)]
            with nc.Fori(0, DEPTH) as l:
                first_block_layer(nc, m, l, a)
        m.cols3, m.mod = sb("cols3", [P, 96]), sb("mod", [P, N_MOD * KD])
        m.in_gain, m.out_gain, m.gain_rows = sb("in_gain", [P, 2, KD]), sb("out_gain", [P, 2, KD]), \
            sb("gain_rows", [P, 2, D])
        with nc.Fori(0, DEPTH) as l:
            second_block_layer(nc, m, l, a)
        with stage(nc) as (sem, sb_):
            stored = sem("stored")
            with nc.Block() as block:
                @block.sync
                def _(sp):
                    for t in range(TT):
                        sp.dma_start(out[0, t * P:(t + 1) * P, :], m.x[:, t, :]).then_inc(stored, 16)
                    sp.wait_ge(stored, 16 * TT)


def kernel(**inputs):
    import concourse.bacc as bacc
    from concourse.bass_utils import run_bass_kernel_spmd

    nc = bacc.Bacc("TRN2", target_bir_lowering=False, num_devices=1)
    table, where = constants()
    arrays, a = {"in_table": table}, {}
    for name, value in inputs.items():
        arrays[f"in_{name}"] = value = np.ascontiguousarray(value)
        a[name] = nc.dram_tensor(f"in_{name}", value.shape, mybir.dt.from_np(value.dtype),
                                       kind="ExternalInput").ap()
    table_ap = nc.dram_tensor("in_table", table.shape, F32, kind="ExternalInput").ap()
    out = nc.dram_tensor("out", (1, S, D), F32, kind="ExternalOutput").ap()
    program(nc, a, table_ap, where, out)
    results = run_bass_kernel_spmd(nc, [arrays], core_ids=[0])
    return results.results[0]["out"]
```

```python
from contextlib import ExitStack, contextmanager

import numpy as np

import concourse.bass as bass
from concourse import mybir

F32 = mybir.dt.float32
F32R = mybir.dt.float32r
BF16 = mybir.dt.bfloat16
I32 = mybir.dt.int32
ALU = mybir.AluOpType
ACT = mybir.ActivationFunctionType
AX = mybir.AxisListType

P = 128
S = 512
D = 1024
DEPTH = 2
TT = S // P
KD = D // P
EPS = 1e-6
MASKED = -1e30

D_RNN = 1024
KR = D_RNN // P
Q_LORA, KV_LORA, QK_NOPE, QK_ROPE, V_HEAD, HEADS = 384, 256, 64, 32, 64, 16
KQ, KKV = Q_LORA // P, KV_LORA // P
QK = QK_NOPE + QK_ROPE
D_FF = 3 * D
KF = D_FF // P
ALPHA = (2 * DEPTH) ** 0.25
CONV = 4
FFN_CONV = 3
LRU_C = 8.0
MLA_SCALE = QK ** -0.5
LAT0 = 2 * D_RNN
ROPE0 = LAT0 + Q_LORA + KV_LORA
GA0 = ROPE0 + QK_ROPE
GB0 = GA0 + D

GW = D // 4
HD = 64
GH = 4
KF2 = 4 * D // P
N_MOD = 6
CONV2 = 3
CMP, STRIDE = 32, 16
N_CMP = (S - CMP) // STRIDE + 1
DK = 32
CHUNK = 64
NCH = S // CHUNK
TAU = 16.0
RANK = 16
O_KV = 4 * GW
O_G = O_KV + 6 * HD
O_LQ = O_G + 3 * GH
O_LK = O_LQ + GH * DK
O_LV = O_LK + GH * DK
O_LG = O_LV + GW
O_LR = O_LG + GW
O_MU = O_LR + RANK
O_MV = O_MU + GW

TWO_PI = 2.0 * np.pi
PI_A = float(np.float32(6.28125))
PI_B = 0.0019350051879882812
PI_C = float(TWO_PI - PI_A - PI_B)
ROUND = 1.5 * 2.0 ** 23


def constants():
    p = np.arange(P)
    parts = {}
    parts["ident"] = np.eye(P)
    parts["causal"] = np.where(p[None, :] > p[:, None], MASKED, 0.0)
    parts["upper"] = (p[:, None] <= p[None, :]) * 1.0
    parts["chunk"] = parts["upper"] * (p[:, None] // CHUNK == p[None, :] // CHUNK)
    parts["halves"] = (p[:, None] // HD == p[None, :] // HD) * 1.0
    state = np.zeros((P, GH, HD))
    for h in range(GH):
        state[h * DK:(h + 1) * DK, h] = 1.0
    parts["state"] = state.reshape(P, GH * HD)
    pick = np.zeros((P, 3, 2, P))
    for b in range(3):
        for m in range(2):
            for r in range(2):
                pick[(2 * m + r) * 3 + b, b, m, r * HD:(r + 1) * HD] = 1.0
    parts["pick"] = pick.reshape(P, 6 * P)
    t = (np.arange(TT)[None, :] * P + p[:, None])[:, :, None]
    seen = (np.arange(N_CMP) * STRIDE + CMP - 1)[None, None, :] <= t
    parts["cmp_add"] = np.where(seen, 0.0, MASKED).reshape(P, -1)
    parts["cmp_mul"] = (seen * 1.0).reshape(P, -1)
    f1 = np.float32(10000.0) ** (-np.arange(0, 32, 2, dtype=np.float32) / np.float32(32))
    parts["freq1"] = np.array([-f1[i % 32] if i % 32 < 16 else f1[i % 32 - 16] for i in p])[:, None]
    f2 = np.float32(500000.0) ** (-np.arange(0, 16, 2, dtype=np.float32) / np.float32(16))
    parts["freq2"] = np.array([-f2[i % 64] if i % 64 < 8 else (f2[i % 64 - 8] if i % 64 < 16 else 0.0)
                               for i in p])[:, None]
    at, cols, where = 0, [], {}
    for name, a in parts.items():
        where[name] = (at, a.shape[1])
        cols.append(a.astype(np.float32))
        at += a.shape[1]
    return np.ascontiguousarray(np.concatenate(cols, axis=1)), where


class Steps:

    def __init__(self, eng, own):
        self.eng, self.own, self.count = eng, own, {}

    def go(self, ins, sem=None, n=1):
        sem = sem if sem is not None else self.own
        ins.then_inc(sem, n)
        key = id(sem)
        self.count[key] = self.count.get(key, 0) + n
        return self.count[key]

    def __call__(self, ins, sem=None, n=1):
        sem = sem if sem is not None else self.own
        self.eng.wait_ge(sem, self.go(ins, sem, n))


@contextmanager
def stage(nc):
    made = []

    def sem(name):
        h = nc.alloc_semaphore(f"{name}_{nc.next_id()}")
        made.append(h)
        return h

    with ExitStack() as mem:
        def sb(name, shape, dt=F32):
            return mem.enter_context(nc.sbuf_tensor(f"{name}_{nc.next_id()}", shape, dt))
        yield sem, sb
    for h in made:
        nc.gpsimd.sem_clear(h)
    nc.all_engine_barrier()
    for h in made:
        nc.release_semaphore(h)


class RingMemory:

    def __init__(self, sb, width=KD * P):
        self.raw = sb("raw", [P, WeightRing.RAW, width])
        self.hi = sb("w_hi", [P, WeightRing.SPLIT, width], F32R)
        self.lo = sb("w_lo", [P, WeightRing.SPLIT, width], F32R)
        self.start, self.ready = 0, 0

    def leave(self, chunks, ahead):
        self.start, self.ready = (self.start + chunks) % WeightRing.RAW, ahead


class WeightRing:

    RAW, SPLIT = 3, 3

    def __init__(self, sem, memory):
        self.memory, self.start, self.ready = memory, memory.start, memory.ready
        self.arrived = [sem(f"raw_arrived{i}") for i in range(self.RAW)]
        self.hi_ready, self.lo_ready, self.used = sem("w_hi_ready"), sem("w_lo_ready"), sem("w_used")

    def raw(self, i):
        return self.memory.raw[:, (self.start + i) % self.RAW, :]

    def hi(self, i):
        return self.memory.hi[:, (self.start + i) % self.SPLIT, :]

    def lo(self, i):
        return self.memory.lo[:, (self.start + i) % self.SPLIT, :]

    def loads(self, i):
        return len(range(i, self.ready - 1, -self.RAW))

    def load(self, sp, i, pieces):
        if i < self.ready:
            return
        if i - self.RAW >= self.ready:
            sp.wait_ge(self.lo_ready, i - self.RAW - self.ready + 1)
        for view, src in pieces:
            sp.dma_start(view(self.raw(i)), src).then_inc(self.arrived[i % self.RAW], 16)

    def split_hi(self, act, i, width, n=1, order=None, arrived=None):
        if i < self.ready:
            return
        act.wait_ge(self.arrived[i % self.RAW], arrived or 16 * n * self.loads(i))
        if i >= self.SPLIT:
            act.wait_ge(self.used, i - self.SPLIT + 1)
        pairs = order(self.raw(i), self.hi(i)) if order else [(self.raw(i)[:, 0:width], self.hi(i)[:, 0:width])]
        for a, b in pairs:
            last = act.activation(b, a, ACT.Copy)
        last.then_inc(self.hi_ready, 1)

    def split_lo(self, eng, i, width, order=None):
        if i < self.ready:
            return
        eng.wait_ge(self.hi_ready, i - self.ready + 1)
        if order is None:
            eng.tensor_tensor(self.lo(i)[:, 0:width], self.raw(i)[:, 0:width], self.hi(i)[:, 0:width].bitcast(F32),
                              ALU.subtract).then_inc(self.lo_ready, 1)
            return
        for (a, b), (_, c) in zip(order(self.raw(i), self.hi(i)), order(self.raw(i), self.lo(i))):
            last = eng.tensor_tensor(c, a, b.bitcast(F32), ALU.subtract)
        last.then_inc(self.lo_ready, 1)

    def wait_split(self, pe, i):
        if i >= self.ready:
            pe.wait_ge(self.lo_ready, i - self.ready + 1)

    def slot(self, i):
        return self.hi(i), self.lo(i)


def matmul3(pe, out, left, right, start, stop, **kw):
    pe.matmul(out, left[0], right[0], start=start, stop=False, **kw)
    pe.matmul(out, left[0], right[1], start=False, stop=False, **kw)
    return pe.matmul(out, left[1], right[0], start=False, stop=stop, **kw)


def conv(dve, do, out, src, taps, bias, last_sem=None):
    n = len(taps)
    if bias is None:
        do(dve.tensor_scalar(out, src, taps[-1], None, ALU.mult))
    else:
        do(dve.tensor_scalar(out, src, taps[-1], bias, ALU.mult, ALU.add))
    for back in range(1, n):
        ins = dve.scalar_tensor_tensor(out=out[:, back:], in0=src[:, :S - back], scalar=taps[n - 1 - back],
                                       in1=out[:, back:], op0=ALU.mult, op1=ALU.add)
        do(ins, last_sem if back == n - 1 else None)


def start_up(nc, m, x, positions, positions_2, table, vectors):
    groups, at = [], P
    sources = []
    for out, v in vectors:
        dims = "n" if len(v.shape) == 3 else ""
        layers = [v[layer].rearrange(f"{dims} (k p) -> ({dims} k) p", p=P) for layer in range(v.shape[0])]
        rows = sum(src.shape[0] for src in layers)
        if at + rows > P:
            groups.append([])
            at = 0
        groups[-1].append((out, at, rows))
        for src in layers:
            sources.append((src, len(groups) - 1, at, src.shape[0]))
            at += src.shape[0]
    G = len(groups)
    with stage(nc) as (sem, sb):
        small_in, x_in, vectors_in, cleared, done, angles, act_done, turned, hi_ready, lo_done, columns_turned, \
            columns_out = (sem(n) for n in ("small_in", "x_in", "vectors_in", "cleared", "done", "angles", "act_done",
                                            "turned", "hi_ready", "lo_done", "columns_turned", "columns_out"))
        pos_i = sb("pos_i", [P, 2, S], I32)
        ang = sb("ang", [P, 4, S])
        tmp = sb("tmp", [P, S])
        staged = sb("vector_rows", [P, G, P])
        features = lambda v, t, half: v[:, 4 * half:4 * half + 4, t * P:(t + 1) * P]
        banks = lambda t, half: m.ps[:, 2 * t + half, :].rearrange("p (k c) -> p k c", k=4)
        with nc.Block() as block:
            @block.sync
            def _(sp):
                sp.dma_start(m.table[:, :], table).then_inc(small_in, 16)
                sp.dma_start(pos_i[:, 0, :], positions[0, :].partition_broadcast(P)).then_inc(small_in, 16)
                sp.dma_start(pos_i[:, 1, :], positions_2[0, :].partition_broadcast(P)).then_inc(small_in, 16)
                for t in range(TT):
                    sp.dma_start(m.x[:, t, :], x[0, t * P:(t + 1) * P, :]).then_inc(x_in, 16)
                sp.wait_ge(cleared, 1)
                for src, g, at, rows in sources:
                    sp.dma_start(staged[at:at + rows, g, :], src).then_inc(vectors_in, 16)

            @block.gpsimd
            def _(pool):
                pool.memset(staged[:, :, :], 0.0).then_inc(cleared, 1)
                pool.memset(m.ones[:, :], 1.0).then_inc(cleared, 1)
                pool.memset(m.eps[:, :], EPS).then_inc(cleared, 1)

            @block.tensor
            def _(pe):
                pe.wait_ge(small_in, 48)
                pe.wait_ge(x_in, 16 * TT)
                for t in range(TT):
                    turn_tile(pe, m, m.x[:, t, :], t).then_inc(turned, 1)
                pe.wait_ge(vectors_in, 16 * len(sources))
                pe.wait_ge(lo_done, 2 * TT)
                for g in range(G):
                    pe.transpose(m.ps[:, g, 0:P], staged[:, g, :], m.ident).then_inc(columns_turned, 1)

            @block.scalar
            def _(act):
                for t in range(TT):
                    act.wait_ge(turned, t + 1)
                    for half in range(2):
                        act.activation(features(m.xt_hi, t, half), banks(t, half), ACT.Copy).then_inc(hi_ready, 1)
                act.wait_ge(angles, 1)
                do = Steps(act, act_done)
                for n, (sin, cos) in enumerate(((m.sin1, m.cos1), (m.sin2, m.cos2))):
                    do(act.activation(sin[:, :], ang[:, 2 * n, :], ACT.Sin))
                    do(act.activation(cos[:, :], ang[:, 2 * n + 1, :], ACT.Sin))
                act.wait_ge(columns_out, G)
                do(act.activation(m.cond[:, :], m.cond_raw[:, 0, :], ACT.Tanh, scale=0.5))

            @block.vector
            def _(dve):
                do = Steps(dve, done)
                dve.wait_ge(small_in, 48)
                do(dve.tensor_copy(m.ident_b[:, :], m.ident))
                do(dve.tensor_copy(m.causal_b[:, :], m.causal))
                for n, freq in enumerate((m.freq1, m.freq2)):
                    for c in range(2):
                        a = ang[:, 2 * n + c, :]
                        do(dve.tensor_copy(a, pos_i[:, n, :]))
                        do(dve.tensor_scalar(a, a, freq, None, ALU.mult))
                        do(dve.tensor_scalar(tmp[:, :], a, 1.0 / TWO_PI, 0.25 * c, ALU.mult, ALU.add))
                        do(dve.tensor_scalar(tmp[:, :], tmp[:, :], ROUND, ROUND, ALU.add, ALU.subtract))
                        for part in (PI_A, PI_B, PI_C):
                            do(dve.scalar_tensor_tensor(out=a, in0=tmp[:, :], scalar=-part, in1=a,
                                                        op0=ALU.mult, op1=ALU.add))
                        if c:
                            do(dve.tensor_scalar(a, a, float(np.pi / 2), None, ALU.add))
                        do(dve.tensor_scalar(a, a, 3.1415925, -3.1415925, ALU.min, ALU.max),
                           angles if n == 1 and c else None)
                for t in range(TT):
                    for half in range(2):
                        dve.wait_ge(hi_ready, 2 * t + half + 1)
                        dve.tensor_tensor(features(m.xt_lo, t, half), banks(t, half),
                                          features(m.xt_hi, t, half).bitcast(F32), ALU.subtract).then_inc(lo_done, 1)
                for g, group in enumerate(groups):
                    dve.wait_ge(columns_turned, g + 1)
                    for out, at, rows in group:
                        do(dve.tensor_copy(out, m.ps[:, g, at:at + rows].rearrange("p (l n) -> p l n", l=out.shape[1])),
                           columns_out if at == group[-1][1] else None)
                dve.wait_ge(act_done, 5)
                do(dve.scalar_tensor_tensor(out=m.cond[:, :], in0=m.cond[:, :], scalar=1.0, in1=m.cond_raw[:, 0, :],
                                            op0=ALU.add, op1=ALU.mult))
                do(dve.tensor_scalar(m.cond[:, :], m.cond[:, :], 0.5, None, ALU.mult))


def turn_tile(pe, m, src, t):
    for k in range(KD):
        last = pe.transpose(m.ps[:, 2 * t + k // 4, (k % 4) * P:(k % 4 + 1) * P], src[:, k * P:(k + 1) * P], m.ident)
    return last


class TurnedAffine:

    def __init__(self, m, sem, gain, shift, turned, tmp):
        self.m, self.gain, self.shift, self.turned = m, gain, shift, turned
        self.product_ready, self.hi_ready, self.lo_ready = sem("product_ready"), sem("hi_ready"), sem("lo_ready")
        self.tmp = tmp

    def scalar(self, act):
        def hi(k):
            act.wait_ge(self.product_ready, k + 1)
            act.activation(self.m.xt_hi[:, k, :], self.tmp[:, k, :], ACT.Copy).then_inc(self.hi_ready, 1)

        act.wait_ge(self.turned, TT)
        for k in range(KD):
            banks = self.m.ps[:, k // 4::2, (k % 4) * P:(k % 4 + 1) * P]
            act.activation(self.tmp[:, k, :].rearrange("p (t c) -> p t c", t=TT), banks, ACT.Identity,
                           scale=self.gain[:, k:k + 1], bias=self.shift[:, k:k + 1]).then_inc(self.product_ready, 1)
            if k:
                hi(k - 1)
        hi(KD - 1)

    def vector(self, dve):
        for k in range(KD):
            dve.wait_ge(self.hi_ready, k + 1)
            dve.tensor_tensor(self.m.xt_lo[:, k, :], self.tmp[:, k, :], self.m.xt_hi[:, k, :].bitcast(F32),
                              ALU.subtract).then_inc(self.lo_ready, 1)


class TokenProduct:

    def __init__(self, m, l, sem, sb, memory, weight, kt, act_in, following, act_scale=1.0):
        self.act_scale, self.act_in_ready = act_scale, None
        self.m, self.l, self.weight, self.kt, self.act_in, self.following = m, l, weight, kt, act_in, following
        self.ring = WeightRing(sem, memory)
        self.chunks = kt + len(following)
        self.y_ready = sem("y_ready")
        self.y = [m.ps[:, 2 * t:2 * t + 2, :].rearrange("p b n -> p (b n)") for t in range(TT)]
        if act_in is not None:
            self.a_hi_ready, self.a_lo_ready = sem("a_hi_ready"), sem("a_lo_ready")
            self.a_hi, self.a_lo = (sb(n, [P, WeightRing.SPLIT, S], F32R) for n in ("a_hi", "a_lo"))
        memory.leave(kt, len(following))

    def sync(self, sp):
        for k in range(self.kt):
            self.ring.load(sp, k, [(lambda v: v[:, 0:D], self.weight[self.l, k * P:(k + 1) * P, :])])
        for i, src in enumerate(self.following):
            self.ring.load(sp, self.kt + i, [src])

    def scalar(self, act):
        for k in range(self.chunks):
            self.ring.split_hi(act, k, D)
            if self.act_in is not None and k < self.kt:
                if k >= WeightRing.SPLIT:
                    act.wait_ge(self.ring.used, k - WeightRing.SPLIT + 1)
                if self.act_in_ready is not None:
                    act.wait_ge(self.act_in_ready, k // 2 + 1)
                act.activation(self.a_hi[:, k % WeightRing.SPLIT, :], self.act_in[:, k, :], ACT.Copy,
                               scale=self.act_scale)\
                    .then_inc(self.a_hi_ready, 1)

    def gpsimd(self, pool):
        for k in range(self.chunks):
            self.ring.split_lo(pool, k, D)

    def vector(self, dve):
        if self.act_in is None:
            return
        for k in range(self.kt):
            n = k % WeightRing.SPLIT
            dve.wait_ge(self.a_hi_ready, k + 1)
            if self.act_scale == 1.0:
                dve.tensor_tensor(self.a_lo[:, n, :], self.act_in[:, k, :], self.a_hi[:, n, :].bitcast(F32),
                                  ALU.subtract).then_inc(self.a_lo_ready, 1)
            else:
                dve.scalar_tensor_tensor(out=self.a_lo[:, n, :], in0=self.act_in[:, k, :], scalar=self.act_scale,
                                         in1=self.a_hi[:, n, :].bitcast(F32), op0=ALU.mult,
                                         op1=ALU.subtract).then_inc(self.a_lo_ready, 1)

    def tensor(self, pe):
        m, kt = self.m, self.kt
        for k in range(kt):
            self.ring.wait_split(pe, k)
            weights = self.ring.slot(k)
            if self.act_in is not None:
                pe.wait_ge(self.a_lo_ready, k + 1)
                n = k % WeightRing.SPLIT
                left = (self.a_hi[:, n, :], self.a_lo[:, n, :])
            else:
                left = (m.xt_hi[:, k, :], m.xt_lo[:, k, :])
            for t in range(TT):
                rows_t = slice(t * P, (t + 1) * P)
                for a, b in ((0, 0), (0, 1), (1, 0)):
                    for half in range(2):
                        last = pe.matmul(m.ps[:, 2 * t + half, :], left[a][:, rows_t],
                                         weights[b][:, half * S:(half + 1) * S], start=(k == 0 and a + b == 0),
                                         stop=(k == kt - 1 and a == 1))
                if k == kt - 1:
                    last.then_inc(self.y_ready, 1)
            if k < kt - 1:
                last.then_inc(self.ring.used, 1)
        pe.wait_ge(self.y_ready, TT)
        pe.sem_inc(self.ring.used, 1)


def product_and_layer_norm(nc, m, l, memory, weight, kt, gain, bias, act_in=None, following=(), act_scale=1.0):
    with stage(nc) as (sem, sb):
        product = TokenProduct(m, l, sem, sb, memory, weight, kt, act_in, following, act_scale)
        own_dve, own_act, stats, root_ready, rows_in, inverted, scaled, normed, turned, hi_ready = (
            sem(n) for n in ("own_dve", "own_act", "stats", "root_ready", "rows_in", "inverted", "scaled", "normed",
                             "turned", "hi_ready"))
        gb = sb("gain_bias", [P, 2, D])
        st = sb("bn", [P, TT, 2, 6])
        mv = sb("mean_var", [P, TT, 2])
        r = sb("root", [P, TT])
        features = lambda v, t, half: v[:, 4 * half:4 * half + 4, t * P:(t + 1) * P]
        banks = lambda t, half: m.ps[:, 2 * t + half, :].rearrange("p (k c) -> p k c", k=4)
        with nc.Block() as block:
            @block.sync
            def _(sp):
                product.sync(sp)
                for n, v in enumerate((gain, bias)):
                    sp.dma_start(gb[:, n, :], v[l].partition_broadcast(P)).then_inc(rows_in, 16)

            @block.gpsimd
            def _(pool):
                product.gpsimd(pool)
                pool.wait_ge(rows_in, 32)
                for t in range(TT):
                    pool.wait_ge(scaled, t + 1)
                    pool.tensor_tensor(m.x[:, t, :], m.x[:, t, :], gb[:, 1, :], ALU.add).then_inc(normed, 1)

            @block.tensor
            def _(pe):
                product.tensor(pe)
                for t in range(TT):
                    pe.wait_ge(normed, t + 1)
                    turn_tile(pe, m, m.x[:, t, :], t).then_inc(turned, 1)

            @block.scalar
            def _(act):
                product.scalar(act)
                do = Steps(act, own_act)

                def hi(t):
                    act.wait_ge(turned, t + 1)
                    for half in range(2):
                        do.go(act.activation(features(m.xt_hi, t, half), banks(t, half), ACT.Copy), hi_ready)

                for t in range(TT):
                    act.wait_ge(stats, t + 1)
                    do.go(act.activation(r[:, t:t + 1], mv[:, t, 1:2], ACT.Sqrt, bias=m.eps[:, 0:1]), root_ready)
                    act.wait_ge(inverted, t + 1)
                    do.go(act.activation(m.x[:, t, :], m.x[:, t, :], ACT.Copy, scale=r[:, t:t + 1]), scaled)
                    if t:
                        hi(t - 1)
                hi(TT - 1)

            @block.vector
            def _(dve):
                product.vector(dve)
                do = Steps(dve, own_dve)

                def lo(t):
                    for half in range(2):
                        dve.wait_ge(hi_ready, 2 * t + half + 1)
                        do.go(dve.tensor_tensor(features(m.xt_lo, t, half), banks(t, half),
                                                features(m.xt_hi, t, half).bitcast(F32), ALU.subtract))

                dve.wait_ge(rows_in, 32)
                for t in range(TT):
                    xt = m.x[:, t, :]
                    dve.wait_ge(product.y_ready, t + 1)
                    do(dve.scalar_tensor_tensor(out=xt, in0=xt, scalar=ALPHA, in1=product.y[t], op0=ALU.mult,
                                                op1=ALU.add))
                    for n in range(2):
                        do(dve.bn_stats(st[:, t, n, :], m.x[:, t, n * S:(n + 1) * S]))
                    do(dve.bn_aggr(mv[:, t, :], st[:, t, :, :].rearrange("p a b -> p (a b)")), stats)
                    do(dve.scalar_tensor_tensor(out=xt, in0=xt, scalar=mv[:, t, 0:1], in1=gb[:, 0, :],
                                                op0=ALU.subtract, op1=ALU.mult))
                    dve.wait_ge(root_ready, t + 1)
                    do.go(dve.reciprocal(r[:, t:t + 1], r[:, t:t + 1]), inverted)
                    if t >= 2:
                        lo(t - 2)
                lo(TT - 2)
                lo(TT - 1)


class GroupNorms:

    def __init__(self, m, l, sem, sb, merged):
        self.m, self.l, self.merged = m, l, merged
        self.squared, self.summed, self.rooted, self.normed = (
            sem(n) for n in ("group_squared", "group_summed", "group_rooted", "group_normed"))
        self.sq = sb("group_squares", [P, 2, S])
        self.root = sb("group_root", [P, 2, S])

    def scalar(self, act, do):
        def root(g):
            if g >= 2:
                act.wait_ge(self.normed, g - 1)
            act.wait_ge(self.summed, 2 * g + 2)
            do.go(act.activation(self.root[:, g % 2, :], self.m.ps[:, g, :], ACT.Sqrt, scale=1.0 / GW,
                                 bias=self.m.eps[:, 0:1]), self.rooted)

        for k in range(KD):
            if k >= 2:
                act.wait_ge(self.summed, k - 1)
            do.go(act.activation(self.sq[:, k % 2, :], self.merged[:, k, :], ACT.Square), self.squared)
            if k >= 2 and k % 2:
                root(k // 2 - 1)
        root(KD // 2 - 1)

    def tensor(self, pe):
        for k in range(KD):
            pe.wait_ge(self.squared, k + 1)
            pe.matmul(self.m.ps[:, k // 2, :], self.m.ones[:, :], self.sq[:, k % 2, :], start=(k % 2 == 0),
                      stop=(k % 2 == 1)).then_inc(self.summed, 1)
        pe.wait_ge(self.rooted, KD // 2)

    def vector(self, dve, do):
        GG = 7
        C = self.m.cols3[:, self.l, :]
        for g in range(KD // 2):
            dve.wait_ge(self.rooted, g + 1)
            r = self.root[:, g % 2, :]
            do(dve.reciprocal(r, r))
            for k in (2 * g, 2 * g + 1):
                t = self.merged[:, k, :]
                do(dve.scalar_tensor_tensor(out=t, in0=t, scalar=C[:, GG + k:GG + k + 1], in1=r, op0=ALU.mult,
                                            op1=ALU.mult), self.normed if k % 2 else None)


def product_and_rms_norm(nc, m, l, memory, weight, kt, gain_rows, act_in=None, following=(), turn_by=None,
                         groups=False):
    with stage(nc) as (sem, sb):
        product = TokenProduct(m, l, sem, sb, memory, weight, kt, act_in, following)
        own_dve, own_act, root_ready, added, root_2_ready, normed, turned = (
            sem(n) for n in ("own_dve", "own_act", "root_ready", "added", "root_2_ready", "normed", "turned"))
        if groups:
            group_norms = GroupNorms(m, l, sem, sb, act_in)
            product.act_in_ready = group_norms.normed
        sums = sb("square_sums", [P, 2, TT])
        tmp = sb("scaled", [P, 2, D])
        if turn_by:
            gain, shift, room = turn_by
            xn = room[:, KD:2 * KD, :].rearrange("p (t k) s -> p t (k s)", t=TT)
            squares = sb("squares", [P, 2, D])
            affine = TurnedAffine(m, sem, gain, shift, turned, room[:, 0:KD, :])
        with nc.Block() as block:
            @block.sync
            def _(sp):
                product.sync(sp)

            @block.gpsimd
            def _(pool):
                product.gpsimd(pool)

            @block.tensor
            def _(pe):
                if groups:
                    group_norms.tensor(pe)
                product.tensor(pe)
                if turn_by:
                    for t in range(TT):
                        pe.wait_ge(normed, t + 1)
                        turn_tile(pe, m, xn[:, t, :], t).then_inc(turned, 1)

            @block.scalar
            def _(act):
                do = Steps(act, own_act)
                if groups:
                    group_norms.scalar(act, do)
                product.scalar(act)

                def root(n, t, src, junk, sem):
                    s = sums[:, n, t:t + 1]
                    do(act.activation(junk, src, ACT.Square, accum_out=s))
                    do.go(act.activation(s, s, ACT.Sqrt, scale=1.0 / D, bias=m.eps[:, 0:1]), sem)

                for t in range(TT + 1):
                    if t < TT:
                        act.wait_ge(product.y_ready, t + 1)
                        if t >= 2:
                            act.wait_ge(added, t - 1)
                        root(0, t, product.y[t], tmp[:, t % 2, :], root_ready)
                    if t and turn_by:
                        act.wait_ge(added, t)
                        root(1, t - 1, m.x[:, t - 1, :], squares[:, t % 2, :], root_2_ready)
                if turn_by:
                    affine.scalar(act)

            @block.vector
            def _(dve):
                do = Steps(dve, own_dve)
                if groups:
                    group_norms.vector(dve, do)
                product.vector(dve)
                for t in range(TT + 1):
                    if t < TT:
                        xt, s = m.x[:, t, :], sums[:, 0, t:t + 1]
                        dve.wait_ge(root_ready, t + 1)
                        do(dve.reciprocal(s, s))
                        do(dve.scalar_tensor_tensor(out=tmp[:, t % 2, :], in0=product.y[t], scalar=s,
                                                    in1=gain_rows, op0=ALU.mult, op1=ALU.mult))
                        do(dve.tensor_tensor(xt, xt, tmp[:, t % 2, :], ALU.add), added)
                    if t and turn_by:
                        s = sums[:, 1, t - 1:t]
                        dve.wait_ge(root_2_ready, t)
                        do(dve.reciprocal(s, s))
                        do(dve.tensor_scalar(xn[:, t - 1, :], m.x[:, t - 1, :], s, None, ALU.mult), normed)
                if turn_by:
                    affine.vector(dve)


def modulated_turn(nc, m, l, memory, first_tiles, room):
    C = m.cols3[:, l, :]
    NG, BM = 15, 47
    with stage(nc) as (sem, sb):
        ring = WeightRing(sem, memory)
        own, own_act, summed, normed, turned, diag_ready, spread = (
            sem(n) for n in ("own", "own_act", "summed", "normed", "turned", "diag_ready", "spread"))
        diag = sb("diag", [P, 2, P])
        sums = sb("square_sums", [P, TT])
        xn = room[1].rearrange("p (t k) s -> p t (k s)", t=TT)
        squares = sb("squares", [P, 2, D])
        affine = TurnedAffine(m, sem, m.in_gain[:, 0, :], m.mod[:, 0:KD], turned, room[0])
        with nc.Block() as block:
            @block.sync
            def _(sp):
                for i, src in enumerate(first_tiles):
                    ring.load(sp, i, [src])

            @block.gpsimd
            def _(pool):
                for i in range(len(first_tiles)):
                    ring.split_lo(pool, i, KD * P)

            @block.scalar
            def _(act):
                do = Steps(act, own_act)
                for t in range(TT):
                    s = sums[:, t:t + 1]
                    do(act.activation(squares[:, t % 2, :], m.x[:, t, :], ACT.Square, accum_out=s))
                    do(act.activation(s, s, ACT.Sqrt, scale=1.0 / D, bias=m.eps[:, 0:1]), summed)
                for i in range(len(first_tiles)):
                    ring.split_hi(act, i, KD * P)
                affine.scalar(act)

            @block.tensor
            def _(pe):
                for t in range(TT):
                    pe.wait_ge(normed, t + 1)
                    turn_tile(pe, m, xn[:, t, :], t).then_inc(turned, 1)
                pe.wait_ge(affine.product_ready, KD)
                for i in range(2 * KD):
                    pe.wait_ge(diag_ready, i + 1)
                    b, c = divmod(i, 4)
                    pe.matmul(m.ps[:, b, c * P:(c + 1) * P], m.ones[:, :], diag[:, i % 2, :],
                              start=True, stop=True).then_inc(spread, 1)

            @block.vector
            def _(dve):
                do = Steps(dve, own)
                do(dve.tensor_tensor(m.mod[:, :], m.mod_sum[:, l, :], C[:, BM:BM + N_MOD * KD], ALU.add))
                for n, (sc, g) in enumerate(((1, 0), (4, 2))):
                    do(dve.scalar_tensor_tensor(out=m.in_gain[:, n, :], in0=m.mod[:, sc * KD:(sc + 1) * KD], scalar=1.0,
                                                in1=C[:, NG + g * KD:NG + (g + 1) * KD], op0=ALU.add, op1=ALU.mult))
                for n, (gt, g) in enumerate(((2, 1), (5, 3))):
                    do(dve.tensor_tensor(m.out_gain[:, n, :], m.mod[:, gt * KD:(gt + 1) * KD],
                                         C[:, NG + g * KD:NG + (g + 1) * KD], ALU.mult))
                for t in range(TT):
                    s = sums[:, t:t + 1]
                    dve.wait_ge(summed, t + 1)
                    do(dve.reciprocal(s, s))
                    do(dve.tensor_scalar(xn[:, t, :], m.x[:, t, :], s, None, ALU.mult), normed)
                affine.vector(dve)
                for i in range(2 * KD):
                    n, k = divmod(i, KD)
                    if i >= 2:
                        dve.wait_ge(spread, i - 1)
                    do(dve.tensor_scalar(diag[:, i % 2, :], m.ident, m.out_gain[:, n, k:k + 1], None, ALU.mult),
                       diag_ready)
                dve.wait_ge(spread, 2 * KD)
                for n in range(2):
                    do(dve.tensor_copy(m.gain_rows[:, n, :],
                                       m.ps[:, 2 * n:2 * n + 2, :].rearrange("p b c -> p (b c)")))
    memory.leave(0, len(first_tiles))


def tile_weights(w, l, c0, n=P):
    return w[l, :, c0:c0 + n].rearrange("(k p) c -> p k c", p=P)


def tiles_ahead(w, l, columns=(0, P, 2 * P)):
    return [(tile_view, tile_weights(w, l, c)) for c in columns]


def rows_ahead(w, l, n=3):
    return [(lambda v: v[:, 0:D], w[l, k * P:(k + 1) * P, :]) for k in range(n)]


def tile_view(v):
    return v[:, 0:KD * P].rearrange("p (k c) -> p k c", k=KD)


def tile_product(pe, m, ring, i, out, cols=P):
    w_hi, w_lo = (tile_view(v) for v in ring.slot(i))
    for k in range(KD):
        last = matmul3(pe, out, (w_hi[:, k, 0:cols], w_lo[:, k, 0:cols]), (m.xt_hi[:, k, :], m.xt_lo[:, k, :]),
                       k == 0, k == KD - 1)
    return last


def in_projection(nc, m, l, memory, w_in, gx_w, ga_w, yr, tb, mult, lat, kpe):
    C = m.cols1[:, l, :]
    cw = lambda tap, j: C[:, 8 * tap + j:8 * tap + j + 1]
    col = lambda base, j: C[:, base + j:base + j + 1]
    CB, GXB, GAB, LAM = 32, 40, 48, 56
    tiles = [("x", j, j * P) for j in range(KR)] + [("lat", j, LAT0 + j * P) for j in range(KQ + KKV)] \
        + [("rope", 0, ROPE0)] + [("g", j, D_RNN + j * P) for j in range(KR)] \
        + [("ga", j, GA0 + j * P) for j in range(KD)] + [("gb", j, GB0 + j * P) for j in range(KD)]
    on_act = {"g", "ga", "gb"}
    BANKS = 4
    emptied = []
    for i, (kind, _, _) in enumerate(tiles):
        emptied.append(sum((k in on_act) == (kind in on_act) for k, _, _ in tiles[:i + 1]))
    with stage(nc) as (sem, sb):
        ring = WeightRing(sem, memory)
        memory.leave(len(tiles), 0)
        act_emptied, dve_emptied, own_dve, own_act, gates_done, gate_w_in, zeroed, lru_ready, tanh_ready, \
            in_ready, mult_ready, gated, ta_ready, cols_ready = (
                sem(n) for n in ("act_emptied", "dve_emptied", "own_dve", "own_act", "gates_done",
                                 "gate_w_in", "zeroed", "lru_ready", "tanh_ready", "in_ready", "mult_ready", "gated",
                                 "ta_ready", "cols_ready"))
        gw = sb("gate_blocks", [P, 2, KR, P])
        xc = sb("x_conv", [P, 2, S])
        th = sb("gate_tanh", [P, 2, 3, S])
        decay = tb
        inp = yr
        gel = sb("gelu", [P, 2, S])
        tap = sb("gate_a_tanh", [P, 2, S])
        rot = sb("rot", [P, 3, S])
        c = sb("lru_columns", [P, 8, KR])
        def rope_order(raw, out):
            src = tile_view(raw)[:, :, 0:QK_ROPE]
            return [(src, tile_view(out)[:, :, QK_ROPE * q:QK_ROPE * (q + 1)]) for q in range(4)]

        with nc.Block() as block:
            @block.sync
            def _(sp):
                sp.wait_ge(zeroed, 1)
                for n, w in enumerate((gx_w, ga_w)):
                    for r in range(2):
                        blocks = w[l].rearrange("(j r) a b -> r a j b", r=2)
                        sp.dma_start(gw[64 * r:64 * r + 64, n, :, 64 * r:64 * r + 64], blocks[r]).then_inc(gate_w_in, 16)
                for i, (kind, j, c0) in enumerate(tiles):
                    n = QK_ROPE if kind == "rope" else P
                    ring.load(sp, i, [(lambda v, n=n: tile_view(v)[:, :, 0:n], tile_weights(w_in, l, c0, n))])

            @block.gpsimd
            def _(pool):
                pool.memset(gw[:, :, :, :], 0.0).then_inc(zeroed, 1)
                for i, (kind, _, _) in enumerate(tiles):
                    ring.split_lo(pool, i, KD * P, order=rope_order if kind == "rope" else None)

            @block.tensor
            def _(pe):
                def gates(j):
                    pe.wait_ge(dve_emptied, j + 1)
                    if j >= 2:
                        pe.wait_ge(tanh_ready, j - 1)
                    for n in range(2):
                        last = pe.matmul(m.ps[:, 4 + 2 * (j % 2) + n, :], gw[:, n, j, :], xc[:, j % 2, :],
                                         start=True, stop=True)
                    last.then_inc(gates_done, 1)

                pe.wait_ge(gate_w_in, 64)
                for i, (kind, j, _) in enumerate(tiles):
                    ring.wait_split(pe, i)
                    if i >= BANKS:
                        pe.wait_ge(act_emptied if tiles[i - BANKS][0] in on_act else dve_emptied, emptied[i - BANKS])
                    tile_product(pe, m, ring, i, m.ps[:, i % BANKS, :]).then_inc(ring.used, 1)
                    if 1 <= i <= KR:
                        gates(i - 1)

            @block.scalar
            def _(act):
                do = Steps(act, own_act)
                lam = C[:, LAM:LAM + KR]
                do(act.activation(c[:, 0, :], lam, ACT.Abs))
                do(act.activation(c[:, 1, :], c[:, 0, :], ACT.Exp, scale=-1.0))
                act.activation(c[:, 2, :], c[:, 1, :], ACT.Ln, bias=1.0).then_inc(cols_ready, 1)
                for i in range(2):
                    ring.split_hi(act, i, KD * P)

                def gate(j):
                    act.wait_ge(gates_done, j + 1)
                    if j == 0:
                        act.wait_ge(lru_ready, 1)
                    if j >= 2:
                        act.wait_ge(in_ready, j - 1)
                    b = 4 + 2 * (j % 2)
                    t3 = th[:, j % 2, :, :]
                    do.go(act.activation(t3[:, 0, :], m.ps[:, b, :], ACT.Tanh, scale=0.5, bias=c[:, 4, j:j + 1]))
                    do(act.activation(t3[:, 1, :], m.ps[:, b + 1, :], ACT.Tanh, scale=0.5, bias=c[:, 5, j:j + 1]))
                    do.go(act.activation(decay[:, j, :], t3[:, 1, :], ACT.Exp, scale=c[:, 7, j:j + 1],
                                         bias=c[:, 7, j:j + 1]))
                    do(act.activation(t3[:, 2, :], t3[:, 1, :], ACT.Tanh, scale=c[:, 6, j:j + 1],
                                      bias=c[:, 6, j:j + 1]), tanh_ready)

                for i, (kind, j, _) in enumerate(tiles):
                    if i + 2 < len(tiles):
                        ring.split_hi(act, i + 2, KD * P, order=rope_order if tiles[i + 2][0] == "rope" else None)
                    if 1 <= i <= KR:
                        gate(i - 1)
                    if i == KR + 1:
                        act.wait_ge(in_ready, KR)
                        do(act.activation(mult[:, :, :], mult[:, :, :], ACT.Sqrt, scale=0.5), mult_ready)
                    if kind in on_act:
                        act.wait_ge(ring.used, i + 1)
                    if kind == "g":
                        if j >= 2:
                            act.wait_ge(gated, j - 1)
                        do(act.activation(gel[:, j % 2, :], m.ps[:, i % BANKS, :], ACT.Gelu_apprx_tanh), act_emptied)
                    if kind == "ga":
                        if j >= 2:
                            act.wait_ge(ta_ready, j - 1)
                        do(act.activation(tap[:, j % 2, :], m.ps[:, i % BANKS, :], ACT.Tanh, scale=0.5), act_emptied)
                    if kind == "gb":
                        if j == 0:
                            act.wait_ge(ta_ready, 1)
                        do(act.activation(tb[:, j, :], m.ps[:, i % BANKS, :], ACT.Tanh, scale=0.5), act_emptied)

            @block.vector
            def _(dve):
                do = Steps(dve, own_dve)
                lam = C[:, LAM:LAM + KR]
                do(dve.tensor_scalar(c[:, 4, :], C[:, GXB:GXB + KR], 0.5, None, ALU.mult))
                do(dve.tensor_scalar(c[:, 5, :], C[:, GAB:GAB + KR], 0.5, None, ALU.mult))
                dve.wait_ge(cols_ready, 1)
                e, ln = c[:, 1, :], c[:, 2, :]
                do(dve.tensor_scalar(c[:, 0, :], e, 1.0, None, ALU.add))
                do(dve.tensor_scalar(c[:, 3, :], c[:, 0, :], 1.0, None, ALU.is_equal))
                do(dve.tensor_scalar(c[:, 0, :], c[:, 0, :], -1.0, None, ALU.add))
                do(dve.tensor_tensor(c[:, 0, :], c[:, 0, :], c[:, 3, :], ALU.add))
                do(dve.reciprocal(c[:, 0, :], c[:, 0, :]))
                do(dve.tensor_tensor(ln, ln, c[:, 3, :], ALU.add))
                do(dve.tensor_tensor(ln, ln, e, ALU.mult))
                do(dve.tensor_tensor(ln, ln, c[:, 0, :], ALU.mult))
                do(dve.tensor_scalar(c[:, 0, :], lam, -1.0, 0.0, ALU.mult, ALU.max))
                do(dve.tensor_tensor(ln, ln, c[:, 0, :], ALU.add))
                do(dve.tensor_scalar(c[:, 6, :], ln, LRU_C / 2, None, ALU.mult))
                do(dve.tensor_scalar(c[:, 7, :], ln, -LRU_C / 2, None, ALU.mult), lru_ready)

                def after_gates(j):
                    dve.wait_ge(tanh_ready, j + 1)
                    t3 = th[:, j % 2, :, :]
                    do(dve.scalar_tensor_tensor(out=inp[:, j, :], in0=t3[:, 0, :], scalar=1.0, in1=xc[:, j % 2, :],
                                                op0=ALU.add, op1=ALU.mult))
                    do(dve.tensor_scalar(mult[:, j, :], t3[:, 2, :], 1.0, None, ALU.add))
                    do(dve.reciprocal(mult[:, j, :], mult[:, j, :]))
                    do(dve.tensor_tensor(mult[:, j, :], mult[:, j, :], t3[:, 2, :], ALU.mult), in_ready)

                def recur(j):
                    do(dve.tensor_tensor(inp[:, j, :], inp[:, j, :], mult[:, j, :], ALU.mult))
                    do(dve.tensor_tensor_scan(mult[:, j, :], decay[:, j, :], inp[:, j, :], 0.0, ALU.mult, ALU.add))

                for i, (kind, j, _) in enumerate(tiles):
                    ps = m.ps[:, i % BANKS, :]
                    if kind not in on_act:
                        dve.wait_ge(ring.used, i + 1)
                    if kind == "x":
                        conv(dve, do, xc[:, j % 2, :], ps, [cw(tap_, j) for tap_ in range(CONV)], col(CB, j), dve_emptied)
                    if 1 <= i <= KR:
                        after_gates(i - 1)
                    if kind == "lat":
                        do(dve.tensor_copy(lat[:, j, :], ps), dve_emptied)
                    if kind == "rope":
                        do(dve.tensor_copy(rot[:, 0, :], ps), dve_emptied)
                        do(dve.stream_shuffle(rot[:, 1, :], rot[:, 0, :], SWAP16))
                        do(dve.tensor_tensor(rot[:, 0, :], rot[:, 0, :], m.cos1[:, :], ALU.mult))
                        do(dve.tensor_tensor(rot[:, 1, :], rot[:, 1, :], m.sin1[:, :], ALU.mult))
                        do(dve.tensor_tensor(kpe[:, :], rot[:, 0, :], rot[:, 1, :], ALU.add))
                        dve.wait_ge(mult_ready, 1)
                    if kind == "g":
                        recur(j)
                        dve.wait_ge(act_emptied, j + 1)
                        do(dve.tensor_tensor(yr[:, j, :], mult[:, j, :], gel[:, j % 2, :], ALU.mult), gated)
                    if kind == "ga":
                        dve.wait_ge(act_emptied, KR + j + 1)
                        do(dve.scalar_tensor_tensor(out=yr[:, j, :], in0=tap[:, j % 2, :], scalar=1.0,
                                                    in1=yr[:, j, :], op0=ALU.add, op1=ALU.mult), ta_ready)


SWAP16 = [(i + 16) % 32 for i in range(32)]
SWAP8 = [i + 8 if i < 8 else i - 8 if i < 16 else i for i in range(32)]


def mla_latents(nc, m, l, lat):
    C = m.cols1[:, l, :]
    QG = 64
    n_lat = KQ + KKV
    with stage(nc) as (sem, sb):
        own_dve, own_act, squared, summed, rooted, lat_ready, lat_hi = (
            sem(n) for n in ("own_dve", "own_act", "squared", "summed", "rooted", "lat_ready", "lat_hi"))
        sq = sb("squares", [P, 2, S])
        root = sb("root", [P, 2, S])
        with nc.Block() as block:
            @block.scalar
            def _(act):
                do = Steps(act, own_act)
                for j in range(n_lat):
                    if j >= 2:
                        act.wait_ge(summed, j - 1)
                    do(act.activation(sq[:, j % 2, :], lat[:, j, :], ACT.Square), squared)
                act.wait_ge(summed, n_lat)
                do(act.activation(root[:, 0, :], m.ps[:, 6, :], ACT.Sqrt, scale=1.0 / Q_LORA, bias=m.eps[:, 0:1]))
                do(act.activation(root[:, 1, :], m.ps[:, 7, :], ACT.Sqrt, scale=1.0 / KV_LORA, bias=m.eps[:, 0:1]), rooted)
                for j in range(n_lat):
                    act.wait_ge(lat_ready, j + 1)
                    do(act.activation(m.xt_hi[:, j, :], lat[:, j, :], ACT.Copy), lat_hi)

            @block.tensor
            def _(pe):
                for j in range(n_lat):
                    pe.wait_ge(squared, j + 1)
                    bank = 6 if j < KQ else 7
                    pe.matmul(m.ps[:, bank, :], m.ones[:, :], sq[:, j % 2, :], start=j in (0, KQ),
                              stop=j in (KQ - 1, n_lat - 1)).then_inc(summed, 1)

            @block.vector
            def _(dve):
                do = Steps(dve, own_dve)
                dve.wait_ge(rooted, 1)
                do(dve.reciprocal(root[:, :, :], root[:, :, :]))
                for j in range(n_lat):
                    do(dve.scalar_tensor_tensor(out=lat[:, j, :], in0=lat[:, j, :], scalar=C[:, QG + j:QG + j + 1],
                                                in1=root[:, int(j >= KQ), :], op0=ALU.mult, op1=ALU.mult), lat_ready)
                for j in range(n_lat):
                    dve.wait_ge(lat_hi, j + 1)
                    do(dve.tensor_tensor(m.xt_lo[:, j, :], lat[:, j, :], m.xt_hi[:, j, :].bitcast(F32), ALU.subtract))


HG = 4


def mla_heads(nc, m, l, first, groups, w_uq, w_ukv, kpe, q_all, k_all, v_all, room):
    with stage(nc) as (sem, sb):
        ring = WeightRing(sem, RingMemory(sb, HG * QK * KQ))
        own_dve, own_act, out_ready, dve_emptied, act_emptied, spread, roped, v_ready, v_out = (
            sem(n) for n in ("own_dve", "own_act", "out_ready", "dve_emptied", "act_emptied", "spread", "roped",
                             "v_ready", "v_out"))
        rot = room[:, 0:4, :].rearrange("p (g n) s -> p g n s", g=2)
        q_pe = room[:, 4:6, :]
        WQ, WK = HG * QK, HG * (QK_NOPE + V_HEAD)

        def by_part(raw, out, kt, width, cut):
            r = raw[:, 0:kt * width].rearrange("p (k h e) -> p k h e", k=kt, h=HG)
            o = out[:, 0:kt * width].rearrange("p (k c) -> p k c", k=kt)
            pairs = []
            for k in range(kt):
                pairs.append((r[:, k, :, 0:cut], o[:, k, 0:HG * cut].rearrange("p (h e) -> p h e", h=HG)))
                pairs.append((r[:, k, :, cut:], o[:, k, HG * cut:].rearrange("p (h e) -> p h e", h=HG)))
            return pairs

        uq_order = lambda raw, out: by_part(raw, out, KQ, WQ, QK_NOPE)
        ukv_order = lambda raw, out: by_part(raw, out, KKV, WK, QK_NOPE)

        with nc.Block() as block:
            @block.sync
            def _(sp):
                for g in range(groups):
                    h0 = first + g * HG
                    wq = w_uq[l, :, h0 * QK:(h0 + HG) * QK].rearrange("(k p) c -> p k c", p=P)
                    ring.load(sp, 2 * g, [(lambda v: v[:, 0:KQ * WQ].rearrange("p (k c) -> p k c", k=KQ), wq)])
                    wk = w_ukv[l, :, h0 * P:(h0 + HG) * P].rearrange("(k p) c -> p k c", p=P)
                    ring.load(sp, 2 * g + 1, [(lambda v: v[:, 0:KKV * WK].rearrange("p (k c) -> p k c", k=KKV), wk)])
                for h in range(groups * HG):
                    sp.dma_start(k_all[QK_NOPE:QK, h, :], kpe[0:QK_ROPE, :]).then_inc(spread, 16)
                for g in range(groups):
                    sp.wait_ge(roped, g + 1)
                    for h in range(HG):
                        sp.dma_start(q_all[QK_NOPE:QK, g * HG + h, :],
                                     q_pe[32 * h:32 * h + 32, g % 2, :]).then_inc(spread, 16)
                sp.wait_ge(spread, 16 * 2 * groups * HG)

            @block.gpsimd
            def _(pool):
                for g in range(groups):
                    ring.split_lo(pool, 2 * g, 0, order=uq_order)
                    ring.split_lo(pool, 2 * g + 1, 0, order=ukv_order)

            @block.scalar
            def _(act):
                do = Steps(act, own_act)

                def split(c):
                    if c < 2 * groups:
                        ring.split_hi(act, c, 0, order=ukv_order if c % 2 else uq_order)

                for c in range(3):
                    split(c)
                for g in range(groups):
                    for n, i in enumerate((0, 1, 3, 4)):
                        if n == 2:
                            split(2 * g + 3)
                        act.wait_ge(out_ready, 5 * g + i + 1)
                        to = q_all if n < 2 else k_all
                        ps = m.ps[:, (5 * g + i) % 6, :]
                        for r in range(2):
                            h = g * HG + 2 * (n % 2) + r
                            do(act.activation(to[0:QK_NOPE, h, :], ps[64 * r:64 * r + 64, :], ACT.Copy),
                               act_emptied if r else None)
                    split(2 * g + 4)

            @block.vector
            def _(dve):
                do = Steps(dve, own_dve)
                for g in range(groups):
                    dve.wait_ge(out_ready, 5 * g + 3)
                    a, b = rot[:, g % 2, 0, :], rot[:, g % 2, 1, :]
                    do(dve.tensor_copy(a, m.ps[:, (5 * g + 2) % 6, :]), dve_emptied)
                    do(dve.stream_shuffle(b, a, SWAP16))
                    do(dve.tensor_tensor(a, a, m.cos1[:, :], ALU.mult))
                    do(dve.tensor_tensor(b, b, m.sin1[:, :], ALU.mult))
                    do(dve.tensor_tensor(q_pe[:, g % 2, :], a, b, ALU.add), roped)
                    dve.wait_ge(v_ready, g + 1)
                    vg = m.ps[:, 6:8, :].rearrange("p b (t c) -> p (b t) c", t=2)
                    do(dve.tensor_copy(v_all[:, :, g * HG * V_HEAD:(g + 1) * HG * V_HEAD], vg), v_out)

            @block.tensor
            def _(pe):
                def emptied(i):
                    g, n = divmod(i, 5)
                    if n == 2:
                        pe.wait_ge(dve_emptied, g + 1)
                    else:
                        pe.wait_ge(act_emptied, 4 * g + (1, 2, 0, 3, 4)[n])

                for g in range(groups):
                    for n in range(5):
                        i = 5 * g + n
                        if n in (0, 3):
                            ring.wait_split(pe, 2 * g + (n == 3))
                        if i >= 6:
                            emptied(i - 6)
                        kt, k0, wide = (KQ, 0, WQ) if n < 3 else (KKV, KQ, WK)
                        w = [v[:, 0:kt * wide].rearrange("p (k c) -> p k c", k=kt) for v in ring.slot(2 * g + (n >= 3))]
                        c0 = (n if n < 3 else n - 3) * P
                        for k in range(kt):
                            last = matmul3(pe, m.ps[:, i % 6, :], (w[0][:, k, c0:c0 + P], w[1][:, k, c0:c0 + P]),
                                           (m.xt_hi[:, k0 + k, :], m.xt_lo[:, k0 + k, :]), k == 0, k == kt - 1)
                        last.then_inc(out_ready, 1)
                        if n == 2:
                            pe.wait_ge(out_ready, i + 1)
                            pe.sem_inc(ring.used, 1)
                    if g:
                        pe.wait_ge(v_out, g)
                    for t in range(TT):
                        out = m.ps[:, 6 + t // 2, 256 * (t % 2):256 * (t % 2) + 256]
                        for k in range(KKV):
                            left = [v[:, KQ + k, t * P:(t + 1) * P] for v in (m.xt_hi, m.xt_lo)]
                            last = matmul3(pe, out, left, (w[0][:, k, HG * QK_NOPE:], w[1][:, k, HG * QK_NOPE:]),
                                           k == 0, k == KKV - 1)
                    last.then_inc(v_ready, 1)
                    pe.wait_ge(v_ready, g + 1)
                    pe.sem_inc(ring.used, 1)


def attention(nc, m, heads, scale, finish):
    with stage(nc) as (sem, sb):
        scored, peaked, exped, normed, turned, copied, valued, finished, own_dve = (
            sem(n) for n in ("scored", "peaked", "exped", "normed", "turned", "copied", "valued", "finished",
                             "own_dve"))
        SCORES, PROBS, TURNED = 4, 8, 3
        LAG_TURN, LAG_COPY, LAG_VALUES = 4, 5, 6
        p = sb("probs", [P, PROBS, S])
        pt = sb("probs_turned", [P, TURNED, S])
        st = sb("softmax", [P, 4, 8])
        U = len(heads) * TT
        with nc.Block() as block:
            @block.tensor
            def _(pe):
                def score(u):
                    h, t = divmod(u, TT)
                    q, k, _ = heads[h]
                    n = (t + 1) * P
                    if u >= SCORES:
                        pe.wait_ge(exped, u - SCORES + 1)
                    bank = m.ps[:, u % SCORES, :]
                    pe.matmul(bank[:, 0:n], q[:, t * P:(t + 1) * P], k[:, 0:n], start=True, stop=True)
                    pe.matmul(bank[:, t * P:n], m.ident_b[:, :], m.causal_b[:, :], start=False, stop=True,
                              skip_group_check=True).then_inc(scored, 1)

                def turn_probs(u):
                    pe.wait_ge(normed, u + 1)
                    if u >= 2:
                        pe.wait_ge(copied, u - 1)
                    for b in range(u % TT + 1):
                        last = pe.transpose(m.ps[:, 4 + u % 2, b * P:(b + 1) * P],
                                            p[:, u % PROBS, b * P:(b + 1) * P], m.ident)
                    last.then_inc(turned, 1)

                def values(u):
                    h, t = divmod(u, TT)
                    pe.wait_ge(copied, u + 1)
                    if t == 0 and h >= 2:
                        pe.wait_ge(finished, h - 1)
                    for b in range(t + 1):
                        last = pe.matmul(m.ps[:, 6 + h % 2, t * P:(t + 1) * P], heads[h][2](b),
                                         pt[:, u % TURNED, b * P:(b + 1) * P], start=(b == 0), stop=(b == t))
                    last.then_inc(valued, 1)

                for u in range(U + LAG_VALUES):
                    if u < U:
                        score(u)
                    if 0 <= u - LAG_TURN < U:
                        turn_probs(u - LAG_TURN)
                    if 0 <= u - LAG_VALUES < U:
                        values(u - LAG_VALUES)

            @block.vector
            def _(dve):
                do = Steps(dve, own_dve)
                for u in range(U + LAG_VALUES + 2):
                    if u < U:
                        n = (u % TT + 1) * P
                        dve.wait_ge(scored, u + 1)
                        do(dve.tensor_reduce(st[:, 3, u % 8:u % 8 + 1], m.ps[:, u % SCORES, 0:n], AX.X, ALU.max))
                        do.go(dve.tensor_scalar(st[:, 0, u % 8:u % 8 + 1], st[:, 3, u % 8:u % 8 + 1], -scale, None,
                                                ALU.mult), peaked)
                    v = u - 1
                    if 0 <= v < U:
                        n = (v % TT + 1) * P
                        dve.wait_ge(exped, v + 1)
                        do(dve.reciprocal(st[:, 2, v % 8:v % 8 + 1], st[:, 1, v % 8:v % 8 + 1]))
                        do.go(dve.tensor_scalar(p[:, v % PROBS, 0:n], p[:, v % PROBS, 0:n], st[:, 2, v % 8:v % 8 + 1],
                                                None, ALU.mult), normed)
                    w = u - LAG_VALUES - 1
                    if w >= 0 and w % TT == TT - 1:
                        h = w // TT
                        dve.wait_ge(valued, (h + 1) * TT)
                        finish(dve, do, h, m.ps[:, 6 + h % 2, :], finished)

            @block.scalar
            def _(act):
                for u in range(U + LAG_COPY):
                    if u < U:
                        n = (u % TT + 1) * P
                        act.wait_ge(peaked, u + 1)
                        if u >= PROBS:
                            act.wait_ge(turned, u - PROBS + 1)
                        act.activation(p[:, u % PROBS, 0:n], m.ps[:, u % SCORES, 0:n], ACT.Exp, scale=scale,
                                       bias=st[:, 0, u % 8:u % 8 + 1], accum_out=st[:, 1, u % 8:u % 8 + 1])\
                            .then_inc(exped, 1)
                    v = u - LAG_COPY
                    if v >= 0:
                        n = (v % TT + 1) * P
                        act.wait_ge(turned, v + 1)
                        if v >= TURNED:
                            act.wait_ge(valued, v - TURNED + 1)
                        act.activation(pt[:, v % TURNED, 0:n], m.ps[:, 4 + v % 2, 0:n], ACT.Copy).then_inc(copied, 1)


MOD_COLS = 1536


def conv_up(nc, m, l, memory, w_up, w_mod, hid, following):
    tap = lambda n, j: m.cols2[:, l, 2 * KF * n + j:2 * KF * n + j + 1]
    with stage(nc) as (sem, sb):
        ring = WeightRing(sem, memory)
        memory.leave(2 * KF, len(following))
        own, conved, gelued, emptied, mod_used, mod_summed, mod_copied = (
            sem(n) for n in ("own", "conved", "gelued", "emptied", "mod_used", "mod_summed", "mod_copied"))
        mod_in = [sem(f"mod_in{i}") for i in range(2)]
        buf = sb("convolved", [P, 2, 2, S])
        gel = sb("gelu", [P, 2, S])
        w_m = sb("w_mod", [P, 2, MOD_COLS])
        acc = sb("mod_acc", [P, N_MOD * D])
        BANKS, TILES = 6, 2 * KF
        PARTS = N_MOD * D // MOD_COLS
        CHUNKS = KD * PARTS
        LAG = 4
        with nc.Block() as block:
            @block.sync
            def _(sp):
                for i in range(TILES):
                    j, half = divmod(i, 2)
                    ring.load(sp, i, [(tile_view, tile_weights(w_up, l, half * D_FF + j * P))])
                    c = i - LAG - 2
                    if 0 <= c < CHUNKS:
                        k, part = divmod(c, PARTS)
                        if c >= 2:
                            sp.wait_ge(mod_used, c - 1)
                        sp.dma_start(w_m[:, c % 2, :], w_mod[l, k * P:(k + 1) * P, part * MOD_COLS:(part + 1) * MOD_COLS])\
                            .then_inc(mod_in[c % 2], 16)

                for i, src in enumerate(following):
                    ring.load(sp, TILES + i, [src])

            @block.gpsimd
            def _(pool):
                for i in range(TILES + len(following)):
                    ring.split_lo(pool, i, KD * P)

            @block.tensor
            def _(pe):
                for i in range(TILES):
                    ring.wait_split(pe, i)
                    if i >= BANKS:
                        pe.wait_ge(emptied, i - BANKS + 1)
                    tile_product(pe, m, ring, i, m.ps[:, i % BANKS, :]).then_inc(ring.used, 1)
                pe.wait_ge(mod_used, CHUNKS)
                for j in range(N_MOD * KD):
                    last = pe.matmul(m.ps[:, 6, j:j + 1], acc[:, j * P:(j + 1) * P], m.ones[:, 0:1], start=True,
                                     stop=True)
                last.then_inc(mod_summed, 1)

            @block.vector
            def _(dve):
                do = Steps(dve, own)
                for i in range(TILES + 1):
                    j, half = divmod(i, 2)
                    if i < TILES:
                        dve.wait_ge(ring.used, i + 1)
                        if half == 0 and j >= 2:
                            dve.wait_ge(gelued, j - 1)
                        conv(dve, do, buf[:, j % 2, half, :], m.ps[:, i % BANKS, :],
                             [tap(n, half * KF + j) for n in range(FFN_CONV)], tap(3, half * KF + j), emptied)
                    c = i - LAG
                    if 0 <= c < CHUNKS:
                        k, part = divmod(c, PARTS)
                        dve.wait_ge(mod_in[c % 2], 16 * (c // 2 + 1))
                        to, w, silu = acc[:, part * MOD_COLS:(part + 1) * MOD_COLS], w_m[:, c % 2, :], m.cond[:, k:k + 1]
                        if k == 0:
                            do(dve.tensor_scalar(to, w, silu, None, ALU.mult), mod_used)
                        else:
                            do(dve.scalar_tensor_tensor(out=to, in0=w, scalar=silu, in1=to, op0=ALU.mult,
                                                        op1=ALU.add), mod_used)
                    if half == 0 and j:
                        dve.wait_ge(gelued, j)
                        do(dve.tensor_tensor(hid[:, j - 1, :], gel[:, (j - 1) % 2, :], buf[:, (j - 1) % 2, 1, :],
                                             ALU.mult), conved)
                dve.wait_ge(mod_summed, 1)
                do(dve.tensor_copy(m.mod_sum[:, l, :], m.ps[:, 6, 0:N_MOD * KD]), mod_copied)

            @block.scalar
            def _(act):
                for i in range(2):
                    ring.split_hi(act, i, KD * P)
                for i in range(TILES + 1):
                    if i + 2 < TILES + len(following):
                        ring.split_hi(act, i + 2, KD * P)
                    if i % 2:
                        j = i // 2
                        act.wait_ge(emptied, 2 * j + 1)
                        if j >= 2:
                            act.wait_ge(conved, j - 1)
                        act.activation(gel[:, j % 2, :], buf[:, j % 2, 0, :], ACT.Gelu_apprx_tanh).then_inc(gelued, 1)


def relu_up(nc, m, l, memory, w_up, hid, following):
    with stage(nc) as (sem, sb):
        ring = WeightRing(sem, memory)
        memory.leave(KF2, len(following))
        emptied, squared = sem("emptied"), sem("squared")
        pos = sb("positive", [P, 2, S])
        BANKS = 6
        with nc.Block() as block:
            @block.sync
            def _(sp):
                for i in range(KF2):
                    ring.load(sp, i, [(tile_view, tile_weights(w_up, l, i * P))])
                for i, src in enumerate(following):
                    ring.load(sp, KF2 + i, [src])

            @block.gpsimd
            def _(pool):
                for i in range(KF2 + len(following)):
                    ring.split_lo(pool, i, KD * P)

            @block.tensor
            def _(pe):
                for i in range(KF2):
                    ring.wait_split(pe, i)
                    if i >= BANKS:
                        pe.wait_ge(emptied, i - BANKS + 1)
                    tile_product(pe, m, ring, i, m.ps[:, i % BANKS, :]).then_inc(ring.used, 1)

            @block.vector
            def _(dve):
                for i in range(KF2):
                    dve.wait_ge(ring.used, i + 1)
                    if i >= 2:
                        dve.wait_ge(squared, i - 1)
                    dve.tensor_scalar(pos[:, i % 2, :], m.ps[:, i % BANKS, :], 0.0, None, ALU.max).then_inc(emptied, 1)
                    dve.wait_ge(emptied, i + 1)
                    dve.tensor_tensor(hid[:, i, :], pos[:, i % 2, :], pos[:, i % 2, :], ALU.mult).then_inc(squared, 1)

            @block.scalar
            def _(act):
                for i in range(KF2 + len(following)):
                    ring.split_hi(act, i, KD * P)


FM = {"ah": 0, "ab": 2, "ac": 4, "q": 6, "cmp": 8, "slc": 9, "win": 10, "small": 11, "lq": 12, "lk": 13, "lg": 14,
      "mu": 16}
FM_TILES = [[(0, i * P, P)] for i in range(9)] \
    + [[(0, O_KV + 2 * HD, HD), (HD, O_KV + 2 * HD, HD)], [(0, O_KV + 4 * HD, HD), (HD, O_KV + 4 * HD, HD)],
       [(0, O_G, DK), (DK, O_LR, RANK)], [(0, O_LQ, P)], [(0, O_LK, P)], [(0, O_LG, P)], [(0, O_LG + P, P)],
       [(0, O_MU, P)], [(0, O_MU + P, P)]]
TM_COLS = [(0, O_KV + 3 * HD, HD), (HD, O_KV + 5 * HD, HD), (2 * HD, O_LV, GW), (2 * HD + GW, O_MV, GW)]
TM = 2 * HD + 2 * GW


def in_projection_2(nc, m, l, memory, w_in, fm):
    with stage(nc) as (sem, sb):
        ring = WeightRing(sem, memory)
        memory.leave(len(FM_TILES), 0)
        emptied = sem("emptied")
        arrivals = [0] * WeightRing.RAW
        want = []
        for i, cols in enumerate(FM_TILES):
            arrivals[i % WeightRing.RAW] += 16 * len(cols) * (i >= ring.ready)
            want.append(arrivals[i % WeightRing.RAW])
        rows = lambda i: FM_TILES[i][-1][0] + FM_TILES[i][-1][2]
        BANKS = 6
        narrow = lambda v, i: tile_view(v)[:, :, 0:rows(i)]
        with nc.Block() as block:
            @block.sync
            def _(sp):
                for i, cols in enumerate(FM_TILES):
                    ring.load(sp, i, [(lambda v, a=a, n=n: tile_view(v)[:, :, a:a + n], tile_weights(w_in, l, c, n))
                                      for a, c, n in cols])

            @block.scalar
            def _(act):
                for i in range(len(FM_TILES)):
                    ring.split_hi(act, i, 0, order=lambda raw, out, i=i: [(narrow(raw, i), narrow(out, i))],
                                  arrived=want[i])

            @block.gpsimd
            def _(pool):
                for i in range(len(FM_TILES)):
                    ring.split_lo(pool, i, 0, order=lambda raw, out, i=i: [(narrow(raw, i), narrow(out, i))])

            @block.tensor
            def _(pe):
                for i in range(len(FM_TILES)):
                    ring.wait_split(pe, i)
                    if i >= BANKS:
                        pe.wait_ge(emptied, i - BANKS + 1)
                    tile_product(pe, m, ring, i, m.ps[0:rows(i), i % BANKS, :], rows(i)).then_inc(ring.used, 1)

            @block.vector
            def _(dve):
                for i in range(len(FM_TILES)):
                    dve.wait_ge(ring.used, i + 1)
                    dve.tensor_copy(fm[0:rows(i), i, :], m.ps[0:rows(i), i % BANKS, :]).then_inc(emptied, 1)


def in_projection_tokens(nc, m, l, memory, w_in, tm):
    A = 2 * HD + GW
    with stage(nc) as (sem, sb):
        ring = WeightRing(sem, memory)
        memory.leave(KD, 0)
        done = sem("done")
        with nc.Block() as block:
            @block.sync
            def _(sp):
                for k in range(KD):
                    ring.load(sp, k, [(lambda v, a=a, n=n: v[:, a:a + n], w_in[l, k * P:(k + 1) * P, c:c + n])
                                      for a, c, n in TM_COLS])

            @block.scalar
            def _(act):
                for k in range(KD):
                    ring.split_hi(act, k, TM, n=len(TM_COLS))

            @block.gpsimd
            def _(pool):
                for k in range(KD):
                    ring.split_lo(pool, k, TM)

            @block.tensor
            def _(pe):
                for k in range(KD):
                    ring.wait_split(pe, k)
                    w = ring.slot(k)
                    for t in range(TT):
                        left = [v[:, k, t * P:(t + 1) * P] for v in (m.xt_hi, m.xt_lo)]
                        matmul3(pe, m.ps[:, t, 0:A], left, (w[0][:, 0:A], w[1][:, 0:A]), k == 0, k == KD - 1)
                        last = matmul3(pe, m.ps[:, TT + t, 0:GW], left, (w[0][:, A:TM], w[1][:, A:TM]),
                                       k == 0, k == KD - 1)
                    last.then_inc(ring.used, 1)

            @block.vector
            def _(dve):
                dve.wait_ge(ring.used, KD)
                for t in range(TT):
                    dve.tensor_copy(tm[:, t, 0:A], m.ps[:, t, 0:A]).then_inc(done, 1)
                    dve.tensor_copy(tm[:, t, A:TM], m.ps[:, TT + t, 0:GW]).then_inc(done, 1)
                dve.wait_ge(done, 2 * TT)


def short_conv_and_rotary(nc, m, l, fm, tm, merged, qr, kz, vd, gates):
    C = m.cols3[:, l, :]
    with stage(nc) as (sem, sb):
        own, zeroed, tanh, sig_ready, spread, copied = (sem(n) for n in ("own", "zeroed", "tanh", "sig_ready",
                                                                        "spread", "copied"))
        a = sb("a", [P, 2, S])
        sig = sb("sig", [P, S])
        with nc.Block() as block:
            @block.gpsimd
            def _(pool):
                pool.memset(kz[:, :, :, :], 0.0).then_inc(zeroed, 1)

            @block.scalar
            def _(act):
                act.activation(sig[0:3 * GH, :], fm[0:3 * GH, FM["small"], :], ACT.Tanh, scale=0.5).then_inc(tanh, 1)
                for i in range(6):
                    act.wait_ge(spread, i + 1)
                    act.activation(gates[:, i, :], m.ps[:, i, :], ACT.Copy).then_inc(copied, 1)

            @block.tensor
            def _(pe):
                pe.wait_ge(sig_ready, 1)
                for i in range(6):
                    pe.matmul(m.ps[:, i, :], m.pick[0:3 * GH, i * P:(i + 1) * P], sig[0:3 * GH, :],
                              start=True, stop=True).then_inc(spread, 1)

            @block.vector
            def _(dve):
                do = Steps(dve, own)
                dve.wait_ge(tanh, 1)
                do(dve.tensor_scalar(sig[0:3 * GH, :], sig[0:3 * GH, :], 0.5, 0.5, ALU.mult, ALU.add), sig_ready)
                for j in range(2):
                    do(dve.tensor_tensor(a[:, 0, :], fm[:, FM["ac"] + j, :], fm[:, FM["ah"] + j, :], ALU.mult))
                    conv(dve, do, a[:, 1, :], a[:, 0, :], [C[:, 2 * n + j:2 * n + j + 1] for n in range(CONV2)], None)
                    do(dve.tensor_tensor(merged[:, j, :], a[:, 1, :], fm[:, FM["ab"] + j, :], ALU.mult))
                dve.wait_ge(zeroed, 1)
                for n, src in enumerate((FM["q"], FM["q"] + 1, FM["slc"], FM["win"])):
                    do(dve.stream_shuffle(a[:, 0, :], fm[:, src, :], SWAP8))
                    do(dve.tensor_tensor(a[:, 0, :], a[:, 0, :], m.sin2[:, :], ALU.mult))
                    do(dve.tensor_tensor(a[:, 1, :], fm[:, src, :], m.cos2[:, :], ALU.mult))
                    if n < 2:
                        do(dve.tensor_tensor(qr[:, n, :], a[:, 0, :], a[:, 1, :], ALU.add))
                    else:
                        for r in range(2):
                            half = slice(64 * r, 64 * r + 64)
                            do(dve.tensor_tensor(kz[half, n - 2, r, :], a[half, 0, :], a[half, 1, :], ALU.add))
                for b in range(2):
                    for r in range(2):
                        do(dve.tensor_copy(vd[:, b, :, r * HD:(r + 1) * HD], tm[:, :, b * HD:(b + 1) * HD]))


def compressed(nc, m, l, cmp_pos, cmp_w1, cmp_w2, fm, gates, merged):
    scale = HD ** -0.5
    N = N_CMP
    with stage(nc) as (sem, sb):
        w_in, zeroed, pos_turned, own, z_ready, hid_done, tanh, hid_ready, kv_done, kv_ready, scored, shifted, exped, \
            p_ready, turned, pct_ready, valued = (
                sem(n) for n in ("w_in", "zeroed", "pos_turned", "own", "z_ready", "hid_done", "tanh", "hid_ready",
                                 "kv_done", "kv_ready", "scored", "shifted", "exped", "p_ready", "turned",
                                 "pct_ready", "valued"))
        w1 = sb("w1", [P, CMP, P])
        w2 = sb("w2", [P, 2, P])
        pos = sb("pos", [CMP, P])
        pos_t = sb("pos_t", [P, CMP])
        z = sb("windows", [P, N, CMP])
        hid = sb("hidden", [P, 2, 32])
        th = sb("hidden_tanh", [P, 2, 32])
        kc = sb("kc", [P, 2, 32])
        vc = sb("vc", [32, P])
        sc = sb("scores", [P, GH * TT, N])
        st = sb("sums", [P, 2, GH * TT])
        pct = sb("probs_turned", [32, GH, S])
        with nc.Block() as block:
            @block.gpsimd
            def _(pool):
                pool.memset(kc[:, :, :], 0.0).then_inc(zeroed, 1)

            @block.sync
            def _(sp):
                for j in range(2):
                    rows = slice(j * HD, (j + 1) * HD)
                    sp.dma_start(pos[:, rows], cmp_pos[l, j]).then_inc(w_in, 16)
                    sp.dma_start(w1[rows, :, :], cmp_w1[l, j].rearrange("(r d) c -> d r c", d=HD)).then_inc(w_in, 16)
                    for r in range(2):
                        sp.dma_start(w2[:, j, r * HD:(r + 1) * HD], cmp_w2[l, j]).then_inc(w_in, 16)

            @block.tensor
            def _(pe):
                pe.wait_ge(w_in, 16 * 8)
                pe.transpose(m.ps[:, 0, 0:CMP], pos[:, :], m.ident[0:CMP, 0:CMP]).then_inc(pos_turned, 1)
                pe.wait_ge(z_ready, 1)
                for j in range(2):
                    rows = slice(j * HD, (j + 1) * HD)
                    for r in range(CMP):
                        last = pe.matmul(m.ps[:, 1 + j, 0:N], w1[rows, r, :], z[rows, :, r], start=(r == 0),
                                         stop=(r == CMP - 1))
                last.then_inc(hid_done, 1)
                pe.wait_ge(hid_ready, 1)
                pe.matmul(m.ps[:, 3, 0:N], w2[:, 0, :], hid[:, 0, 0:N], start=True, stop=True)
                pe.matmul(m.ps[0:N, 4, 0:P], hid[:, 1, 0:N], w2[:, 1, :], start=True, stop=True).then_inc(kv_done, 1)
                pe.wait_ge(kv_ready, 1)
                for u in range(GH * TT):
                    h, t = divmod(u, TT)
                    last = pe.matmul(m.ps[:, 5, u * N:(u + 1) * N], fm[:, FM["q"] + h // 2, t * P:(t + 1) * P],
                                     kc[:, h % 2, 0:N], start=True, stop=True)
                last.then_inc(scored, 1)
                pe.wait_ge(p_ready, 1)
                for u in range(GH * TT):
                    h, t = divmod(u, TT)
                    last = pe.transpose(m.ps[0:N, h, t * P:(t + 1) * P], sc[:, u, :], m.ident)
                last.then_inc(turned, 1)
                for h in range(GH):
                    pe.wait_ge(pct_ready, h + 1)
                    pe.matmul(m.ps[:, 4 + h, :], vc[0:N, :], pct[0:N, h, :], start=True, stop=True).then_inc(valued, 1)

            @block.scalar
            def _(act):
                act.wait_ge(hid_done, 1)
                act.activation(th[:, :, 0:N], m.ps[:, 1:3, 0:N], ACT.Tanh, scale=0.5).then_inc(tanh, 1)
                act.wait_ge(shifted, 1)
                act.activation(sc[:, :, :], sc[:, :, :], ACT.Exp, scale=scale).then_inc(exped, 1)
                act.wait_ge(turned, 1)
                for h in range(GH):
                    act.activation(pct[0:N, h, :], m.ps[0:N, h, :], ACT.Copy).then_inc(pct_ready, 1)

            @block.vector
            def _(dve):
                do = Steps(dve, own)
                dve.wait_ge(pos_turned, 1)
                do(dve.tensor_copy(pos_t[:, :], m.ps[:, 0, 0:CMP]))
                blocks = fm[:, FM["cmp"], :].rearrange("p (n r) -> p n r", r=STRIDE)
                for a in range(2):
                    add = pos_t[:, a * STRIDE:(a + 1) * STRIDE].unsqueeze(1).to_broadcast([P, N, STRIDE])
                    do(dve.tensor_tensor(z[:, :, a * STRIDE:(a + 1) * STRIDE], blocks[:, a:a + N, :], add, ALU.add),
                       z_ready if a else None)
                dve.wait_ge(tanh, 1)
                do(dve.scalar_tensor_tensor(out=hid[:, :, 0:N], in0=th[:, :, 0:N], scalar=1.0, in1=m.ps[:, 1:3, 0:N],
                                            op0=ALU.add, op1=ALU.mult))
                do(dve.tensor_scalar(hid[:, :, 0:N], hid[:, :, 0:N], 0.5, None, ALU.mult), hid_ready)
                dve.wait_ge(kv_done, 1)
                dve.wait_ge(zeroed, 1)
                for r in range(2):
                    half = slice(64 * r, 64 * r + 64)
                    do(dve.tensor_copy(kc[half, r, 0:N], m.ps[half, 3, 0:N]))
                do(dve.tensor_copy(vc[0:N, :], m.ps[0:N, 4, 0:P]), kv_ready)
                dve.wait_ge(scored, 1)
                ps = m.ps[:, 5, 0:GH * TT * N].rearrange("p (h c) -> p h c", h=GH)
                s4 = sc[:, :, :].rearrange("p (h t) n -> p h (t n)", h=GH)
                over_heads = lambda v: v.unsqueeze(1).to_broadcast([P, GH, TT * N])
                over_keys = lambda v: v.unsqueeze(2).to_broadcast([P, GH * TT, N])
                do(dve.tensor_tensor(s4, ps, over_heads(m.cmp_add), ALU.add))
                do(dve.tensor_reduce(st[:, 0, :], sc[:, :, :], AX.X, ALU.max))
                do(dve.tensor_tensor(sc[:, :, :], sc[:, :, :], over_keys(st[:, 0, :]), ALU.subtract), shifted)
                dve.wait_ge(exped, 1)
                do(dve.tensor_reduce(st[:, 1, :], sc[:, :, :], AX.X, ALU.add))
                do(dve.reciprocal(st[:, 1, :], st[:, 1, :]))
                do(dve.tensor_tensor(sc[:, :, :], sc[:, :, :], over_keys(st[:, 1, :]), ALU.mult))
                do(dve.tensor_tensor(s4, s4, over_heads(m.cmp_mul), ALU.mult), p_ready)
                for h in range(GH):
                    dve.wait_ge(valued, h + 1)
                    half = slice(64 * (h % 2), 64 * (h % 2) + 64)
                    do(dve.tensor_tensor(merged[half, 2 + h // 2, :], m.ps[half, 4 + h, :], gates[half, h // 2, :],
                                         ALU.mult))


def linear_attention(nc, m, l, gate_w2, fm, tm, merged, room):
    C = m.cols3[:, l, :]
    GB = 6
    with stage(nc) as (sem, sb):
        w_in, own, own_act, gate_done, ln_ready, scan_ready, diffed, exp_ready, scaled, att_done, att_ready, kl_turned, \
            kl_ready, kv_done, kv_used, state_ready, zeroed, o_done, squared, summed, rooted, silu = (
                sem(n) for n in ("w_in", "own", "own_act", "gate_done", "ln_ready", "scan_ready", "diffed",
                                 "exp_ready", "scaled", "att_done", "att_ready", "kl_turned", "kl_ready", "kv_done",
                                 "kv_used", "state_ready", "zeroed", "o_done", "squared", "summed", "rooted", "silu"))
        w2 = sb("gate_w2", [DK + RANK, P])
        la = sb("log_a", [P, 3, S])
        carry = sb("carry", [P, S])
        b = sb("cum", [P, 3, S])
        e = sb("exps", [P, 4, S])
        qk = sb("scaled_qk", [P, 4, S])
        att = sb("att", [P, GH, TT, P])
        vz = sb("vz", [P, TT, GH, P])
        klz = sb("klz", [P, 2, TT, P])
        state = room.rearrange("p a (b c) -> p (a b) c", c=GW)
        kvm = sb("kvm", [P, GW])
        sq = sb("sq", [P, 2, S])
        r = sb("root", [P, 2, S])
        chunks = lambda v: v.rearrange("p (n c) -> p n c", c=CHUNK)
        at = lambda c: chunks(b[:, 0, :])[:, :, c:c + 1].to_broadcast([P, NCH, CHUNK])
        with nc.Block() as block:
            @block.sync
            def _(sp):
                sp.dma_start(w2[DK:DK + RANK, :], gate_w2[l]).then_inc(w_in, 16)

            @block.gpsimd
            def _(pool):
                pool.memset(carry[:, :], 1.0).then_inc(zeroed, 1)
                pool.wait_ge(zeroed, 1)
                pool.memset(chunks(carry[:, :])[:, :, 0:1], 0.0).then_inc(zeroed, 1)
                pool.memset(klz[:, :, :, :], 0.0).then_inc(zeroed, 1)
                pool.memset(att[:, :, :, :], 0.0).then_inc(zeroed, 1)
                pool.memset(vz[:, :, :, :], 0.0).then_inc(zeroed, 1)
                pool.memset(state[:, 0, :], 0.0).then_inc(zeroed, 1)
                pool.wait_ge(zeroed, 6)
                for h in range(GH):
                    c0 = (h % 2) * HD
                    pool.tensor_copy(vz[:, :, h, c0:c0 + HD], tm[:, :, 2 * HD + h * HD:2 * HD + (h + 1) * HD])\
                        .then_inc(zeroed, 1)

            @block.scalar
            def _(act):
                do = Steps(act, own_act)
                act.wait_ge(gate_done, 1)
                do(act.activation(la[:, 0, :], m.ps[:, 0, :], ACT.Identity, bias=C[:, GB:GB + 1]))
                do(act.activation(la[:, 1, :], la[:, 0, :], ACT.Abs))
                do(act.activation(la[:, 1, :], la[:, 1, :], ACT.Exp, scale=-1.0))
                do(act.activation(la[:, 1, :], la[:, 1, :], ACT.Ln, bias=1.0), ln_ready)
                act.wait_ge(diffed, 1)
                do(act.activation(e[:, 0, :], b[:, 1, :], ACT.Exp))
                do(act.activation(e[:, 1, :], b[:, 1, :], ACT.Exp, scale=-1.0))
                do(act.activation(e[:, 2, :], b[:, 2, :], ACT.Exp, scale=-1.0))
                do(act.activation(e[:, 3, :], b[:, 0, :], ACT.Exp), exp_ready)
                for j in range(2):
                    do(act.activation(la[:, 1 + j, :], fm[:, FM["lg"] + j, :], ACT.Tanh, scale=0.5), silu)
                act.wait_ge(o_done, 1)
                for j in range(2):
                    do(act.activation(sq[:, j, :], m.ps[:, 4 + j, :], ACT.Square), squared)
                act.wait_ge(summed, 2)
                do(act.activation(r[:, :, :], m.ps[:, 0:2, :], ACT.Sqrt, scale=1.0 / HD, bias=m.eps[:, 0:1]), rooted)

            @block.vector
            def _(dve):
                do = Steps(dve, own)
                dve.wait_ge(ln_ready, 1)
                do(dve.scalar_tensor_tensor(out=la[:, 2, :], in0=la[:, 0, :], scalar=0.0, in1=la[:, 1, :],
                                            op0=ALU.min, op1=ALU.subtract))
                do(dve.tensor_scalar(la[:, 2, :], la[:, 2, :], 1.0 / TAU, None, ALU.mult))
                dve.wait_ge(zeroed, 6 + GH)
                do(dve.tensor_tensor_scan(b[:, 0, :], carry[:, :], la[:, 2, :], 0.0, ALU.mult, ALU.add))
                do(dve.tensor_tensor(chunks(b[:, 1, :]), chunks(b[:, 0, :]), at(CHUNK // 2), ALU.subtract))
                do(dve.tensor_tensor(chunks(b[:, 2, :]), chunks(b[:, 0, :]), at(CHUNK - 1), ALU.subtract), diffed)
                dve.wait_ge(exp_ready, 1)
                q, k = fm[:, FM["lq"], :], fm[:, FM["lk"], :]
                stt = lambda out, x, s, y, sem=None: do(dve.scalar_tensor_tensor(
                    out=out, in0=x, scalar=s, in1=y, op0=ALU.mult, op1=ALU.mult), sem)
                stt(qk[:, 2, :], k, 1.0, e[:, 2, :], scaled)
                stt(qk[:, 1, :], k, 1.0, e[:, 1, :], scaled)
                stt(qk[:, 0, :], q, DK ** -0.5, e[:, 0, :], scaled)
                stt(qk[:, 3, :], q, DK ** -0.5, e[:, 3, :], scaled)
                dve.wait_ge(kl_turned, 1)
                for par in range(2):
                    half = slice(64 * par, 64 * par + 64)
                    do(dve.tensor_copy(klz[half, par, :, :], m.ps[half, 6, :].rearrange("p (t c) -> p t c", t=TT)),
                       kl_ready)
                for h in range(GH):
                    dve.wait_ge(att_done, h + 1)
                    for par in range(2):
                        half = slice(64 * par, 64 * par + 64)
                        src = m.ps[half, h, :].rearrange("p (t c) -> p t c", t=TT)[:, :, half]
                        do(dve.tensor_scalar(att[half, h, :, half], src, 3e38, -3e38, ALU.min, ALU.max))
                    do(dve.tensor_tensor(att[:, h, :, :], att[:, h, :, :],
                                         m.chunk.unsqueeze(1).to_broadcast([P, TT, P]), ALU.mult), att_ready)
                for n in range(NCH - 1):
                    dve.wait_ge(kv_done, n + 1)
                    do(dve.tensor_tensor(kvm[:, :], m.ps[:, 6 + n % 2, 0:GW], m.state_mask, ALU.mult), kv_used)
                    decay = e[:, 3, (n + 1) * CHUNK - 1:(n + 1) * CHUNK]
                    do(dve.scalar_tensor_tensor(out=state[:, n + 1, :], in0=state[:, n, :], scalar=decay,
                                                in1=kvm[:, :], op0=ALU.mult, op1=ALU.add), state_ready)
                dve.wait_ge(silu, 2)
                for j in range(2):
                    do(dve.scalar_tensor_tensor(out=la[:, 1 + j, :], in0=la[:, 1 + j, :], scalar=1.0,
                                                in1=fm[:, FM["lg"] + j, :], op0=ALU.add, op1=ALU.mult))
                dve.wait_ge(rooted, 1)
                do(dve.reciprocal(r[:, :, :], r[:, :, :]))
                for j in range(2):
                    stt(r[:, j, :], r[:, j, :], 0.5, la[:, 1 + j, :])
                    do(dve.tensor_tensor(merged[:, 4 + j, :], m.ps[:, 4 + j, :], r[:, j, :], ALU.mult))

            @block.tensor
            def _(pe):
                pe.wait_ge(w_in, 16)
                pe.matmul(m.ps[:, 0, :], w2[DK:DK + RANK, :], fm[DK:DK + RANK, FM["small"], :], start=True,
                          stop=True).then_inc(gate_done, 1)
                pe.wait_ge(scaled, 1)
                for t in range(TT):
                    last = pe.transpose(m.ps[:, 6, t * P:(t + 1) * P], qk[:, 2, t * P:(t + 1) * P], m.ident)
                last.then_inc(kl_turned, 1)
                pe.wait_ge(scaled, 3)
                for h in range(GH):
                    rows = slice(DK * h, DK * h + DK)
                    for t in range(TT):
                        tok = slice(t * P, (t + 1) * P)
                        last = pe.matmul(m.ps[:, h, tok], qk[rows, 1, tok], qk[rows, 0, tok], start=True, stop=True,
                                         tile_position=(DK * h, 0))
                    last.then_inc(att_done, 1)
                pe.wait_ge(kl_ready, 2)
                for n in range(NCH - 1):
                    if n >= 2:
                        pe.wait_ge(kv_used, n - 1)
                    pe.matmul(m.ps[:, 6 + n % 2, 0:GW], klz[:, n % 2, n // 2, :], tm[:, n // 2, 2 * HD:2 * HD + GW],
                              start=True, stop=True).then_inc(kv_done, 1)
                pe.wait_ge(att_ready, GH)
                pe.wait_ge(scaled, 4)
                pe.wait_ge(state_ready, NCH - 1)
                for j in range(2):
                    first = True
                    for t in range(TT):
                        for h in (2 * j, 2 * j + 1):
                            pe.matmul(m.ps[:, 4 + j, t * P:(t + 1) * P], vz[:, t, h, :], att[:, h, t, :],
                                      start=first, stop=False, skip_group_check=True)
                            first = False
                        for n in (2 * t, 2 * t + 1):
                            if n:
                                last = pe.matmul(m.ps[:, 4 + j, n * CHUNK:(n + 1) * CHUNK],
                                                 state[:, n, j * P:(j + 1) * P], qk[:, 3, n * CHUNK:(n + 1) * CHUNK],
                                                 start=False, stop=(n == NCH - 1), skip_group_check=True)
                last.then_inc(o_done, 1)
                for j in range(2):
                    pe.wait_ge(squared, j + 1)
                    pe.matmul(m.ps[:, j, :], m.halves, sq[:, j, :], start=True, stop=True).then_inc(summed, 1)


def spatial_gate(nc, m, l, ws, bias, fm, tm, merged):
    G = TT * GH
    with stage(nc) as (sem, sb):
        w_in, zeroed, turned, own, w_ready, v_ready, mixed, rooted, summed = (
            sem(n) for n in ("w_in", "zeroed", "turned", "own", "w_ready", "v_ready", "mixed", "rooted", "summed"))
        w = sb("ws", [P, GH, P])
        wt = sb("ws_turned", [P, GH, P])
        bs = sb("bias", [P, 2, P])
        v = sb("v", [P, TT, GW])
        sq = sb("sq", [P, TT, GW])
        vz = sb("vz", [P, TT, GH, P])
        st = sb("st", [P, 2, G])
        tmp = sb("tmp", [P, 2, S])
        by_group = lambda a: a.rearrange("p t (g c) -> p (t g) c", c=HD)
        wide = lambda a: a.unsqueeze(2).to_broadcast([P, G, HD])
        with nc.Block() as block:
            @block.sync
            def _(sp):
                sp.dma_start(w[:, :, :], ws[l].rearrange("g t s -> t g s")).then_inc(w_in, 16)
                for g in range(GH):
                    r = g % 2
                    sp.dma_start(bs[64 * r:64 * r + 64, g // 2, :], bias[l, g].partition_broadcast(64)).then_inc(w_in, 16)

            @block.gpsimd
            def _(pool):
                pool.memset(vz[:, :, :, :], 0.0).then_inc(zeroed, 1)

            @block.scalar
            def _(act):
                act.wait_ge(summed, 1)
                act.activation(st[:, 1, :], st[:, 1, :], ACT.Sqrt, scale=1.0 / HD, bias=m.eps[:, 0:1]).then_inc(rooted, 1)

            @block.tensor
            def _(pe):
                pe.wait_ge(w_in, 16 * (1 + GH))
                for g in range(GH):
                    last = pe.transpose(m.ps[:, 0, g * P:(g + 1) * P], w[:, g, :], m.ident)
                last.then_inc(turned, 1)
                pe.wait_ge(v_ready, 1)
                for j in range(2):
                    for t in range(TT):
                        for r in range(2):
                            last = pe.matmul(m.ps[:, 1 + j, t * P:(t + 1) * P], vz[:, t, 2 * j + r, :],
                                             wt[:, 2 * j + r, :], start=(r == 0), stop=(r == 1))
                    last.then_inc(mixed, 1)

            @block.vector
            def _(dve):
                do = Steps(dve, own)
                dve.wait_ge(turned, 1)
                do(dve.tensor_tensor(wt[:, :, :], m.ps[:, 0, :].rearrange("p (g c) -> p g c", g=GH),
                                     m.upper.unsqueeze(1).to_broadcast([P, GH, P]), ALU.mult))
                src = tm[:, :, 2 * HD + GW:TM]
                s3 = src.rearrange("p t (g c) -> p t g c", c=HD)
                v3, q3 = by_group(v[:, :, :]), by_group(sq[:, :, :])
                do(dve.tensor_copy(v[:, :, :], src))
                do(dve.tensor_reduce(st[:, 0, :], v3, AX.X, ALU.add))
                do(dve.tensor_scalar(st[:, 0, :], st[:, 0, :], 1.0 / HD, None, ALU.mult))
                do(dve.tensor_tensor(v3, v3, wide(st[:, 0, :]), ALU.subtract))
                do(dve.tensor_tensor(q3, v3, v3, ALU.mult))
                do(dve.tensor_reduce(st[:, 1, :], q3, AX.X, ALU.add), summed)
                dve.wait_ge(rooted, 1)
                dve.wait_ge(zeroed, 1)
                do(dve.reciprocal(st[:, 1, :], st[:, 1, :]))
                do(dve.tensor_tensor(v3, v3, wide(st[:, 1, :]), ALU.mult))
                for r in range(2):
                    do(dve.tensor_copy(vz[:, :, r::2, r * HD:(r + 1) * HD],
                                       v[:, :, :].rearrange("p t (g c) -> p t g c", c=HD)[:, :, r::2, :]),
                       v_ready if r else None)
                for j in range(2):
                    dve.wait_ge(mixed, j + 1)
                    ps = m.ps[:, 1 + j, :].rearrange("p (t c) -> p t c", t=TT)
                    out = tmp[:, j, :].rearrange("p (t c) -> p t c", t=TT)
                    do(dve.tensor_tensor(out, ps, bs[:, j, :].unsqueeze(1).to_broadcast([P, TT, P]), ALU.add))
                    do(dve.tensor_tensor(merged[:, 6 + j, :], tmp[:, j, :], fm[:, FM["mu"] + j, :], ALU.mult))


def first_block_layer(nc, m, l, a):
    with ExitStack() as mem:
        sb = lambda name, shape: mem.enter_context(nc.sbuf_tensor(f"{name}_{nc.next_id()}", shape, F32))
        hid = sb("hidden", [P, KF, S])
        yr, tb, mult = hid[:, 0:KR, :], hid[:, KR:KR + KD, :], hid[:, KR + KD:2 * KR + KD, :]
        with ExitStack() as mixer:
            sbm = lambda name, shape, dt=F32: mixer.enter_context(nc.sbuf_tensor(f"{name}_{nc.next_id()}", shape, dt))
            kpe = sbm("k_pe", [P, S])
            with ExitStack() as projection:
                sbp = lambda name, shape, dt=F32: projection.enter_context(
                    nc.sbuf_tensor(f"{name}_{nc.next_id()}", shape, dt))
                lat = sbp("latents", [P, KQ + KKV, S])
                in_projection(nc, m, l, RingMemory(sbp), a["w_in"], a["gx_w"], a["ga_w"], yr, tb, mult, lat, kpe)
                mla_latents(nc, m, l, lat)
            HALF = HEADS // 2
            q_all, k_all = sbm("q_all", [QK, HALF, S]), sbm("k_all", [QK, HALF, S])
            v_all = sbm("v_all", [P, TT, HALF * V_HEAD])
            tmp = mult[:, 6, :]
            for first in (0, HALF):
                mla_heads(nc, m, l, first, HALF // HG, a["w_uq"], a["w_ukv"], kpe, q_all, k_all, v_all, mult)

                def finish(dve, do, h, out, sem):
                    half, tile = slice(64 * (h % 2), 64 * (h % 2) + 64), (first + h) // 2
                    do(dve.scalar_tensor_tensor(out=tmp[half, :], in0=tb[half, tile, :], scalar=1.0, in1=out[half, :],
                                                op0=ALU.add, op1=ALU.mult))
                    do(dve.tensor_tensor(yr[half, tile, :], yr[half, tile, :], tmp[half, :], ALU.add), sem)

                values = lambda h: lambda b: v_all[:, b, (h // 2) * P:(h // 2 + 1) * P]
                attention(nc, m, [(q_all[:, h, :], k_all[:, h, :], values(h)) for h in range(HALF)], MLA_SCALE, finish)
        memory = RingMemory(lambda name, shape, dt=F32: mem.enter_context(
            nc.sbuf_tensor(f"{name}_{nc.next_id()}", shape, dt)))
        product_and_layer_norm(nc, m, l, memory, a["w_out"], KD, a["ln1_g"], a["ln1_b"], act_in=yr, act_scale=0.5,
                               following=tiles_ahead(a["w_up"], l, (0, D_FF, P)))
        conv_up(nc, m, l, memory, a["w_up"], a["w_mod_2"], hid, rows_ahead(a["w_down"], l))
        product_and_layer_norm(nc, m, l, memory, a["w_down"], KF, a["ln2_g"], a["ln2_b"], act_in=hid)


def second_block_layer(nc, m, l, a):
    with ExitStack() as mem:
        sb = lambda name, shape, dt=F32: mem.enter_context(nc.sbuf_tensor(f"{name}_{nc.next_id()}", shape, dt))
        hid = sb("hidden", [P, KF2, S])
        FMN = len(FM_TILES)
        merged, fm, gates = hid[:, 0:KD, :], hid[:, KD:KD + FMN, :], hid[:, KD + FMN:KD + FMN + 6, :]
        with ExitStack() as mixers:
            sbm = lambda name, shape, dt=F32: mixers.enter_context(nc.sbuf_tensor(f"{name}_{nc.next_id()}", shape, dt))
            tm = sbm("token_major", [P, TT, TM])
            with ExitStack() as projection:
                memory = RingMemory(lambda name, shape, dt=F32: projection.enter_context(
                    nc.sbuf_tensor(f"{name}_{nc.next_id()}", shape, dt)))
                modulated_turn(nc, m, l, memory, tiles_ahead(a["w_in_2"], l), (merged, fm[:, 0:KD, :]))
                in_projection_2(nc, m, l, memory, a["w_in_2"], fm)
                in_projection_tokens(nc, m, l, memory, a["w_in_2"], tm)
            with ExitStack() as nsa:
                sbn = lambda name, shape: nsa.enter_context(nc.sbuf_tensor(f"{name}_{nc.next_id()}", shape, F32))
                qr, kz, vd = sbn("qr", [P, 2, S]), sbn("kz", [P, 2, 2, S]), sbn("vd", [P, 2, TT, P])
                tmp = sbn("gated", [P, S])
                short_conv_and_rotary(nc, m, l, fm, tm, merged, qr, kz, vd, gates)
                compressed(nc, m, l, a["cmp_pos_2"], a["cmp_w1_2"], a["cmp_w2_2"], fm, gates, merged)

                def finish(dve, do, n, out, sem):
                    branch, h = divmod(n, GH)
                    half, tile = slice(64 * (h % 2), 64 * (h % 2) + 64), h // 2
                    do(dve.tensor_tensor(tmp[half, :], out[half, :], gates[half, 2 * (branch + 1) + tile, :], ALU.mult))
                    do(dve.tensor_tensor(merged[half, 2 + tile, :], merged[half, 2 + tile, :], tmp[half, :], ALU.add),
                       sem)

                values = lambda branch: lambda b: vd[:, branch, b, :]
                attention(nc, m, [(qr[:, h // 2, :], kz[:, branch, h % 2, :], values(branch))
                                  for branch in range(2) for h in range(GH)], HD ** -0.5, finish)
            linear_attention(nc, m, l, a["gla_gate_w2_2"], fm, tm, merged, gates[:, 0:NCH * GW // S, :])
            spatial_gate(nc, m, l, a["gmlp_ws_2"], a["gmlp_b_2"], fm, tm, merged)
        memory = RingMemory(sb)
        product_and_rms_norm(nc, m, l, memory, a["w_o_2"], KD, m.gain_rows[:, 0, :], act_in=merged, groups=True,
                             following=tiles_ahead(a["w_up_2"], l), turn_by=(m.in_gain[:, 1, :], m.mod[:, 3 * KD:4 * KD],
                                                                      hid[:, KD:3 * KD, :]))
        relu_up(nc, m, l, memory, a["w_up_2"], hid, rows_ahead(a["w_down_2"], l))
        product_and_rms_norm(nc, m, l, memory, a["w_down_2"], KF2, m.gain_rows[:, 1, :], act_in=hid)


class Memory:
    pass


def program(nc, a, table, where, out):
    m = Memory()
    with ExitStack() as ctx:
        def sb(name, shape, dt=F32):
            return ctx.enter_context(nc.sbuf_tensor(name, shape, dt))
        m.ps = ctx.enter_context(nc.psum_tensor("ps", [P, 8, S], F32))
        m.x = sb("x_tokens", [P, TT, D])
        m.xt_hi, m.xt_lo = sb("xt_hi", [P, KD, S], F32R), sb("xt_lo", [P, KD, S], F32R)
        m.table = sb("table", [P, table.shape[1]])
        part = lambda name: m.table[:, where[name][0]:where[name][0] + where[name][1]]
        m.ident, m.causal, m.upper, m.chunk, m.halves, m.pick = (
            part(name) for name in ("ident", "causal", "upper", "chunk", "halves", "pick"))
        m.cmp_add, m.cmp_mul, m.freq1, m.freq2, m.state_mask = (
            part(name) for name in ("cmp_add", "cmp_mul", "freq1", "freq2", "state"))
        m.ones, m.eps = sb("ones", [P, P]), sb("eps", [P, 1])
        m.ident_b, m.causal_b = sb("ident_b", [P, P], BF16), sb("causal_b", [P, P], BF16)
        m.sin2, m.cos2 = (sb(n, [P, S]) for n in ("sin2", "cos2"))
        m.cond_raw, m.cond, m.mod_sum = sb("cond_raw", [P, 1, KD]), sb("cond", [P, KD]), \
            sb("mod_sum", [P, DEPTH, N_MOD * KD])
        first = ctx.enter_context(ExitStack())
        sb1 = lambda name, shape: first.enter_context(nc.sbuf_tensor(name, shape, F32))
        m.cols3 = sb("cols3", [P, DEPTH, 95])
        m.sin1, m.cos1 = sb1("sin1", [P, S]), sb1("cos1", [P, S])
        m.cols1, m.cols2 = sb1("cols1", [P, DEPTH, 69]), sb1("cols2", [P, DEPTH, (FFN_CONV + 1) * 2 * KF])
        vectors = [(m.cond_raw[:, :, :], a["c_2"])]
        for cols, names in ((m.cols1, ("conv_w", "conv_b", "gx_b", "ga_b", "lru_lambda", "q_norm_g", "kv_norm_g")),
                            (m.cols2, ("ffn_conv_w", "ffn_conv_b")),
                            (m.cols3, ("conv_w_2", "gla_gate_b_2", "grp_gain_2", "norm_g_2", "b_mod_2"))):
            at = 0
            for name in names:
                v = a[name]
                parts = [v[:, n] for n in range(v.shape[1])] if name == "ffn_conv_w" else [v]
                for part_ in parts:
                    n = int(np.prod(part_.shape[1:])) // P
                    vectors.append((cols[:, :, at:at + n], part_))
                    at += n
        start_up(nc, m, a["x"], a["positions"], a["positions_2"], table, vectors)
        with nc.Fori(0, DEPTH) as l:
            first_block_layer(nc, m, l, a)
        first.close()
        m.mod, m.in_gain, m.out_gain, m.gain_rows = sb("mod", [P, N_MOD * KD]), sb("in_gain", [P, 2, KD]), \
            sb("out_gain", [P, 2, KD]), sb("gain_rows", [P, 2, D])
        with nc.Fori(0, DEPTH) as l:
            second_block_layer(nc, m, l, a)
        with stage(nc) as (sem, sb_):
            stored = sem("stored")
            with nc.Block() as block:
                @block.sync
                def _(sp):
                    for t in range(TT):
                        sp.dma_start(out[0, t * P:(t + 1) * P, :], m.x[:, t, :]).then_inc(stored, 16)
                    sp.wait_ge(stored, 16 * TT)


def kernel(**inputs):
    import concourse.bacc as bacc
    from concourse.bass_utils import run_bass_kernel_spmd

    nc = bacc.Bacc("TRN2", target_bir_lowering=False, num_devices=1)
    table, where = constants()
    arrays, a = {"in_table": table}, {}
    for name, value in inputs.items():
        arrays[f"in_{name}"] = value = np.ascontiguousarray(value)
        a[name] = nc.dram_tensor(f"in_{name}", value.shape, mybir.dt.from_np(value.dtype),
                                       kind="ExternalInput").ap()
    table_ap = nc.dram_tensor("in_table", table.shape, F32, kind="ExternalInput").ap()
    out = nc.dram_tensor("out", (1, S, D), F32, kind="ExternalOutput").ap()
    program(nc, a, table_ap, where, out)
    results = run_bass_kernel_spmd(nc, [arrays], core_ids=[0])
    return results.results[0]["out"]
```

```python
from contextlib import ExitStack, contextmanager

import numpy as np

import concourse.bass as bass
from concourse import mybir

F32 = mybir.dt.float32
F32R = mybir.dt.float32r
BF16 = mybir.dt.bfloat16
I32 = mybir.dt.int32
ALU = mybir.AluOpType
ACT = mybir.ActivationFunctionType
AX = mybir.AxisListType

P = 128
S = 512
D = 1024
DEPTH = 2
TT = S // P
KD = D // P
EPS = 1e-6
MASKED = -1e30

D_RNN = 1024
KR = D_RNN // P
Q_LORA, KV_LORA, QK_NOPE, QK_ROPE, V_HEAD, HEADS = 384, 256, 64, 32, 64, 16
KQ, KKV = Q_LORA // P, KV_LORA // P
QK = QK_NOPE + QK_ROPE
D_FF = 3 * D
KF = D_FF // P
ALPHA = (2 * DEPTH) ** 0.25
CONV = 4
FFN_CONV = 3
LRU_C = 8.0
MLA_SCALE = QK ** -0.5
LAT0 = 2 * D_RNN
ROPE0 = LAT0 + Q_LORA + KV_LORA
GA0 = ROPE0 + QK_ROPE
GB0 = GA0 + D

GW = D // 4
HD = 64
GH = 4
KF2 = 4 * D // P
N_MOD = 6
CONV2 = 3
CMP, STRIDE = 32, 16
N_CMP = (S - CMP) // STRIDE + 1
DK = 32
CHUNK = 64
NCH = S // CHUNK
TAU = 16.0
RANK = 16
O_KV = 4 * GW
O_G = O_KV + 6 * HD
O_LQ = O_G + 3 * GH
O_LK = O_LQ + GH * DK
O_LV = O_LK + GH * DK
O_LG = O_LV + GW
O_LR = O_LG + GW
O_MU = O_LR + RANK
O_MV = O_MU + GW

TWO_PI = 2.0 * np.pi
PI_A = float(np.float32(6.28125))
PI_B = 0.0019350051879882812
PI_C = float(TWO_PI - PI_A - PI_B)
ROUND = 1.5 * 2.0 ** 23


def constants():
    p = np.arange(P)
    parts = {}
    parts["ident"] = np.eye(P)
    parts["causal"] = np.where(p[None, :] > p[:, None], MASKED, 0.0)
    parts["upper"] = (p[:, None] <= p[None, :]) * 1.0
    parts["chunk"] = parts["upper"] * (p[:, None] // CHUNK == p[None, :] // CHUNK)
    parts["halves"] = (p[:, None] // HD == p[None, :] // HD) * 1.0
    state = np.zeros((P, GH, HD))
    for h in range(GH):
        state[h * DK:(h + 1) * DK, h] = 1.0
    parts["state"] = state.reshape(P, GH * HD)
    pick = np.zeros((P, 3, 2, P))
    for b in range(3):
        for m in range(2):
            for r in range(2):
                pick[(2 * m + r) * 3 + b, b, m, r * HD:(r + 1) * HD] = 1.0
    parts["pick"] = pick.reshape(P, 6 * P)
    t = (np.arange(TT)[None, :] * P + p[:, None])[:, :, None]
    seen = (np.arange(N_CMP) * STRIDE + CMP - 1)[None, None, :] <= t
    parts["cmp_add"] = np.where(seen, 0.0, MASKED).reshape(P, -1)
    parts["cmp_mul"] = (seen * 1.0).reshape(P, -1)
    f1 = np.float32(10000.0) ** (-np.arange(0, 32, 2, dtype=np.float32) / np.float32(32))
    parts["freq1"] = np.array([-f1[i % 32] if i % 32 < 16 else f1[i % 32 - 16] for i in p])[:, None]
    f2 = np.float32(500000.0) ** (-np.arange(0, 16, 2, dtype=np.float32) / np.float32(16))
    parts["freq2"] = np.array([-f2[i % 64] if i % 64 < 8 else (f2[i % 64 - 8] if i % 64 < 16 else 0.0)
                               for i in p])[:, None]
    at, cols, where = 0, [], {}
    for name, a in parts.items():
        where[name] = (at, a.shape[1])
        cols.append(a.astype(np.float32))
        at += a.shape[1]
    return np.ascontiguousarray(np.concatenate(cols, axis=1)), where


class Steps:

    def __init__(self, eng, own):
        self.eng, self.own, self.count = eng, own, {}

    def go(self, ins, sem=None, n=1):
        sem = sem if sem is not None else self.own
        ins.then_inc(sem, n)
        key = id(sem)
        self.count[key] = self.count.get(key, 0) + n
        return self.count[key]

    def __call__(self, ins, sem=None, n=1):
        sem = sem if sem is not None else self.own
        self.eng.wait_ge(sem, self.go(ins, sem, n))


CLEARED = []


@contextmanager
def stage(nc):
    made = []

    def sem(name):
        h = nc.alloc_semaphore(f"{name}_{nc.next_id()}")
        made.append(h)
        return h

    with ExitStack() as mem:
        def sb(name, shape, dt=F32):
            return mem.enter_context(nc.sbuf_tensor(f"{name}_{nc.next_id()}", shape, dt))
        yield sem, sb
    for h in made:
        nc.gpsimd.sem_clear(h)
    for h in CLEARED:
        nc.release_semaphore(h)
    CLEARED[:] = made


def last_stage_cleared(nc):
    nc.all_engine_barrier()
    for h in CLEARED:
        nc.release_semaphore(h)
    CLEARED[:] = []


class RingMemory:

    def __init__(self, sb, width=KD * P):
        self.raw = sb("raw", [P, WeightRing.RAW, width])
        self.hi = sb("w_hi", [P, WeightRing.SPLIT, width], F32R)
        self.lo = sb("w_lo", [P, WeightRing.SPLIT, width], F32R)
        self.start, self.ready = 0, 0

    def leave(self, chunks, ahead):
        self.start, self.ready = (self.start + chunks) % WeightRing.RAW, ahead


class WeightRing:

    RAW, SPLIT = 3, 3

    def __init__(self, sem, memory):
        self.memory, self.start, self.ready = memory, memory.start, memory.ready
        self.arrived = [sem(f"raw_arrived{i}") for i in range(self.RAW)]
        self.hi_ready, self.lo_ready, self.used = sem("w_hi_ready"), sem("w_lo_ready"), sem("w_used")

    def raw(self, i):
        return self.memory.raw[:, (self.start + i) % self.RAW, :]

    def hi(self, i):
        return self.memory.hi[:, (self.start + i) % self.SPLIT, :]

    def lo(self, i):
        return self.memory.lo[:, (self.start + i) % self.SPLIT, :]

    def loads(self, i):
        return len(range(i, self.ready - 1, -self.RAW))

    def load(self, sp, i, pieces):
        if i < self.ready:
            return
        if i - self.RAW >= self.ready:
            sp.wait_ge(self.lo_ready, i - self.RAW - self.ready + 1)
        for view, src in pieces:
            sp.dma_start(view(self.raw(i)), src).then_inc(self.arrived[i % self.RAW], 16)

    def split_hi(self, act, i, width, n=1, order=None, arrived=None):
        if i < self.ready:
            return
        act.wait_ge(self.arrived[i % self.RAW], arrived or 16 * n * self.loads(i))
        if i >= self.SPLIT:
            act.wait_ge(self.used, i - self.SPLIT + 1)
        pairs = order(self.raw(i), self.hi(i)) if order else [(self.raw(i)[:, 0:width], self.hi(i)[:, 0:width])]
        for a, b in pairs:
            last = act.activation(b, a, ACT.Copy)
        last.then_inc(self.hi_ready, 1)

    def split_lo(self, eng, i, width, order=None):
        if i < self.ready:
            return
        eng.wait_ge(self.hi_ready, i - self.ready + 1)
        if order is None:
            eng.tensor_tensor(self.lo(i)[:, 0:width], self.raw(i)[:, 0:width], self.hi(i)[:, 0:width].bitcast(F32),
                              ALU.subtract).then_inc(self.lo_ready, 1)
            return
        for (a, b), (_, c) in zip(order(self.raw(i), self.hi(i)), order(self.raw(i), self.lo(i))):
            last = eng.tensor_tensor(c, a, b.bitcast(F32), ALU.subtract)
        last.then_inc(self.lo_ready, 1)

    def wait_split(self, pe, i):
        if i >= self.ready:
            pe.wait_ge(self.lo_ready, i - self.ready + 1)

    def slot(self, i):
        return self.hi(i), self.lo(i)


def matmul3(pe, out, left, right, start, stop, **kw):
    pe.matmul(out, left[0], right[0], start=start, stop=False, **kw)
    pe.matmul(out, left[0], right[1], start=False, stop=False, **kw)
    return pe.matmul(out, left[1], right[0], start=False, stop=stop, **kw)


def conv(dve, do, out, src, taps, bias, last_sem=None):
    n = len(taps)
    if bias is None:
        do(dve.tensor_scalar(out, src, taps[-1], None, ALU.mult))
    else:
        do(dve.tensor_scalar(out, src, taps[-1], bias, ALU.mult, ALU.add))
    for back in range(1, n):
        ins = dve.scalar_tensor_tensor(out=out[:, back:], in0=src[:, :S - back], scalar=taps[n - 1 - back],
                                       in1=out[:, back:], op0=ALU.mult, op1=ALU.add)
        do(ins, last_sem if back == n - 1 else None)


def start_up(nc, m, x, positions, positions_2, table, vectors):
    groups, at = [], P
    sources = []
    for out, v in vectors:
        dims = "n" if len(v.shape) == 3 else ""
        layers = [v[layer].rearrange(f"{dims} (k p) -> ({dims} k) p", p=P) for layer in range(v.shape[0])]
        rows = sum(src.shape[0] for src in layers)
        if at + rows > P:
            groups.append([])
            at = 0
        groups[-1].append((out, at, rows))
        for src in layers:
            sources.append((src, len(groups) - 1, at, src.shape[0]))
            at += src.shape[0]
    G = len(groups)
    with stage(nc) as (sem, sb):
        small_in, x_in, vectors_in, cleared, done, angles, act_done, turned, hi_ready, lo_done, columns_turned, \
            columns_out = (sem(n) for n in ("small_in", "x_in", "vectors_in", "cleared", "done", "angles", "act_done",
                                            "turned", "hi_ready", "lo_done", "columns_turned", "columns_out"))
        pos_i = sb("pos_i", [P, 2, S], I32)
        ang = sb("ang", [P, 4, S])
        tmp = sb("tmp", [P, S])
        staged = sb("vector_rows", [P, G, P])
        features = lambda v, t, half: v[:, 4 * half:4 * half + 4, t * P:(t + 1) * P]
        banks = lambda t, half: m.ps[:, 2 * t + half, :].rearrange("p (k c) -> p k c", k=4)
        with nc.Block() as block:
            @block.sync
            def _(sp):
                sp.dma_start(m.table[:, :], table).then_inc(small_in, 16)
                sp.dma_start(pos_i[:, 0, :], positions[0, :].partition_broadcast(P)).then_inc(small_in, 16)
                sp.dma_start(pos_i[:, 1, :], positions_2[0, :].partition_broadcast(P)).then_inc(small_in, 16)
                for t in range(TT):
                    sp.dma_start(m.x[:, t, :], x[0, t * P:(t + 1) * P, :]).then_inc(x_in, 16)
                sp.wait_ge(cleared, 1)
                for src, g, at, rows in sources:
                    sp.dma_start(staged[at:at + rows, g, :], src).then_inc(vectors_in, 16)

            @block.gpsimd
            def _(pool):
                pool.memset(staged[:, :, :], 0.0).then_inc(cleared, 1)
                pool.memset(m.ones[:, :], 1.0).then_inc(cleared, 1)
                pool.memset(m.eps[:, :], EPS).then_inc(cleared, 1)

            @block.tensor
            def _(pe):
                pe.wait_ge(small_in, 48)
                pe.wait_ge(x_in, 16 * TT)
                for t in range(TT):
                    turn_tile(pe, m, m.x[:, t, :], t).then_inc(turned, 1)
                pe.wait_ge(vectors_in, 16 * len(sources))
                pe.wait_ge(lo_done, 2 * TT)
                for g in range(G):
                    pe.transpose(m.ps[:, g, 0:P], staged[:, g, :], m.ident).then_inc(columns_turned, 1)

            @block.scalar
            def _(act):
                for t in range(TT):
                    act.wait_ge(turned, t + 1)
                    for half in range(2):
                        act.activation(features(m.xt_hi, t, half), banks(t, half), ACT.Copy).then_inc(hi_ready, 1)
                act.wait_ge(angles, 1)
                do = Steps(act, act_done)
                for n, (sin, cos) in enumerate(((m.sin1, m.cos1), (m.sin2, m.cos2))):
                    do(act.activation(sin[:, :], ang[:, 2 * n, :], ACT.Sin))
                    do(act.activation(cos[:, :], ang[:, 2 * n + 1, :], ACT.Sin))
                act.wait_ge(columns_out, G)
                do(act.activation(m.cond[:, :], m.cond_raw[:, 0, :], ACT.Tanh, scale=0.5))

            @block.vector
            def _(dve):
                do = Steps(dve, done)
                dve.wait_ge(small_in, 48)
                do(dve.tensor_copy(m.ident_b[:, :], m.ident))
                do(dve.tensor_copy(m.causal_b[:, :], m.causal))
                for n, freq in enumerate((m.freq1, m.freq2)):
                    for c in range(2):
                        a = ang[:, 2 * n + c, :]
                        do(dve.tensor_copy(a, pos_i[:, n, :]))
                        do(dve.tensor_scalar(a, a, freq, None, ALU.mult))
                        do(dve.tensor_scalar(tmp[:, :], a, 1.0 / TWO_PI, 0.25 * c, ALU.mult, ALU.add))
                        do(dve.tensor_scalar(tmp[:, :], tmp[:, :], ROUND, ROUND, ALU.add, ALU.subtract))
                        for part in (PI_A, PI_B, PI_C):
                            do(dve.scalar_tensor_tensor(out=a, in0=tmp[:, :], scalar=-part, in1=a,
                                                        op0=ALU.mult, op1=ALU.add))
                        if c:
                            do(dve.tensor_scalar(a, a, float(np.pi / 2), None, ALU.add))
                        do(dve.tensor_scalar(a, a, 3.1415925, -3.1415925, ALU.min, ALU.max),
                           angles if n == 1 and c else None)
                for t in range(TT):
                    for half in range(2):
                        dve.wait_ge(hi_ready, 2 * t + half + 1)
                        dve.tensor_tensor(features(m.xt_lo, t, half), banks(t, half),
                                          features(m.xt_hi, t, half).bitcast(F32), ALU.subtract).then_inc(lo_done, 1)
                for g, group in enumerate(groups):
                    dve.wait_ge(columns_turned, g + 1)
                    for out, at, rows in group:
                        do(dve.tensor_copy(out, m.ps[:, g, at:at + rows].rearrange("p (l n) -> p l n", l=out.shape[1])),
                           columns_out if at == group[-1][1] else None)
                dve.wait_ge(act_done, 5)
                do(dve.scalar_tensor_tensor(out=m.cond[:, :], in0=m.cond[:, :], scalar=1.0, in1=m.cond_raw[:, 0, :],
                                            op0=ALU.add, op1=ALU.mult))
                do(dve.tensor_scalar(m.cond[:, :], m.cond[:, :], 0.5, None, ALU.mult))


def turn_tile(pe, m, src, t):
    for k in range(KD):
        last = pe.transpose(m.ps[:, 2 * t + k // 4, (k % 4) * P:(k % 4 + 1) * P], src[:, k * P:(k + 1) * P], m.ident)
    return last


class TurnedAffine:

    def __init__(self, m, sem, gain, shift, turned, tmp):
        self.m, self.gain, self.shift, self.turned = m, gain, shift, turned
        self.product_ready, self.hi_ready, self.lo_ready, self.odd_ready = (
            sem(n) for n in ("product_ready", "hi_ready", "lo_ready", "odd_ready"))
        self.tmp = tmp

    def scalar(self, act):
        act.wait_ge(self.turned, TT)
        for k in range(KD):
            banks = self.m.ps[:, k // 4::2, (k % 4) * P:(k % 4 + 1) * P]
            act.activation(self.tmp[:, k, :].rearrange("p (t c) -> p t c", t=TT), banks, ACT.Identity,
                           scale=self.gain[:, k:k + 1], bias=self.shift[:, k:k + 1]).then_inc(self.product_ready, 1)
            if k % 2 == 0:
                act.wait_ge(self.product_ready, k + 1)
                act.activation(self.m.xt_hi[:, k, :], self.tmp[:, k, :], ACT.Copy).then_inc(self.hi_ready, 1)

    def vector(self, dve):
        for k in range(KD):
            if k % 2 == 0:
                dve.wait_ge(self.hi_ready, k // 2 + 1)
            else:
                dve.wait_ge(self.product_ready, k + 1)
                dve.tensor_copy(self.m.xt_hi[:, k, :], self.tmp[:, k, :]).then_inc(self.odd_ready, 1)
                dve.wait_ge(self.odd_ready, k // 2 + 1)
            dve.tensor_tensor(self.m.xt_lo[:, k, :], self.tmp[:, k, :], self.m.xt_hi[:, k, :].bitcast(F32),
                              ALU.subtract).then_inc(self.lo_ready, 1)


class TokenProduct:

    def __init__(self, m, l, sem, sb, memory, weight, kt, act_in, following, act_scale=1.0):
        self.act_scale, self.act_in_ready = act_scale, None
        self.m, self.l, self.weight, self.kt, self.act_in, self.following = m, l, weight, kt, act_in, following
        self.ring = WeightRing(sem, memory)
        self.chunks = kt + len(following)
        self.y_ready = sem("y_ready")
        self.y = [m.ps[:, 2 * t:2 * t + 2, :].rearrange("p b n -> p (b n)") for t in range(TT)]
        if act_in is not None:
            self.a_hi_ready, self.a_lo_ready = sem("a_hi_ready"), sem("a_lo_ready")
            self.a_hi, self.a_lo = (sb(n, [P, WeightRing.SPLIT, S], F32R) for n in ("a_hi", "a_lo"))
        memory.leave(kt, len(following))

    def sync(self, sp):
        for k in range(self.kt):
            self.ring.load(sp, k, [(lambda v: v[:, 0:D], self.weight[self.l, k * P:(k + 1) * P, :])])
        for i, src in enumerate(self.following):
            self.ring.load(sp, self.kt + i, [src])

    def scalar(self, act):
        for k in range(self.chunks):
            self.ring.split_hi(act, k, D)
            if self.act_in is not None and k < self.kt:
                if k >= WeightRing.SPLIT:
                    act.wait_ge(self.ring.used, k - WeightRing.SPLIT + 1)
                if self.act_in_ready is not None:
                    act.wait_ge(self.act_in_ready, k // 2 + 1)
                act.activation(self.a_hi[:, k % WeightRing.SPLIT, :], self.act_in[:, k, :], ACT.Copy,
                               scale=self.act_scale)\
                    .then_inc(self.a_hi_ready, 1)

    def gpsimd(self, pool):
        for k in range(self.chunks):
            self.ring.split_lo(pool, k, D)

    def vector(self, dve, tiles):
        for k in tiles:
            n = k % WeightRing.SPLIT
            dve.wait_ge(self.a_hi_ready, k + 1)
            if self.act_scale == 1.0:
                dve.tensor_tensor(self.a_lo[:, n, :], self.act_in[:, k, :], self.a_hi[:, n, :].bitcast(F32),
                                  ALU.subtract).then_inc(self.a_lo_ready, 1)
            else:
                dve.scalar_tensor_tensor(out=self.a_lo[:, n, :], in0=self.act_in[:, k, :], scalar=self.act_scale,
                                         in1=self.a_hi[:, n, :].bitcast(F32), op0=ALU.mult,
                                         op1=ALU.subtract).then_inc(self.a_lo_ready, 1)

    def tensor(self, pe):
        m, kt = self.m, self.kt
        for k in range(kt):
            self.ring.wait_split(pe, k)
            weights = self.ring.slot(k)
            if self.act_in is not None:
                pe.wait_ge(self.a_lo_ready, k + 1)
                n = k % WeightRing.SPLIT
                left = (self.a_hi[:, n, :], self.a_lo[:, n, :])
            else:
                left = (m.xt_hi[:, k, :], m.xt_lo[:, k, :])
            for t in range(TT):
                rows_t = slice(t * P, (t + 1) * P)
                for a, b in ((0, 0), (0, 1), (1, 0)):
                    for half in range(2):
                        last = pe.matmul(m.ps[:, 2 * t + half, :], left[a][:, rows_t],
                                         weights[b][:, half * S:(half + 1) * S], start=(k == 0 and a + b == 0),
                                         stop=(k == kt - 1 and a == 1))
                if k == kt - 1:
                    last.then_inc(self.y_ready, 1)
            if k < kt - 1:
                last.then_inc(self.ring.used, 1)
        pe.wait_ge(self.y_ready, TT)
        pe.sem_inc(self.ring.used, 1)


def product_and_layer_norm(nc, m, l, memory, weight, kt, gain, bias, act_in=None, following=(), act_scale=1.0):
    with stage(nc) as (sem, sb):
        product = TokenProduct(m, l, sem, sb, memory, weight, kt, act_in, following, act_scale)
        own_dve, own_act, stats, root_ready, rows_in, inverted, scaled, normed, turned, hi_ready = (
            sem(n) for n in ("own_dve", "own_act", "stats", "root_ready", "rows_in", "inverted", "scaled", "normed",
                             "turned", "hi_ready"))
        gb = sb("gain_bias", [P, 2, D])
        st = sb("bn", [P, TT, 2, 6])
        mv = sb("mean_var", [P, TT, 2])
        r = sb("root", [P, TT])
        features = lambda v, t, half: v[:, 4 * half:4 * half + 4, t * P:(t + 1) * P]
        banks = lambda t, half: m.ps[:, 2 * t + half, :].rearrange("p (k c) -> p k c", k=4)
        with nc.Block() as block:
            @block.sync
            def _(sp):
                product.sync(sp)
                for n, v in enumerate((gain, bias)):
                    sp.dma_start(gb[:, n, :], v[l].partition_broadcast(P)).then_inc(rows_in, 16)

            @block.gpsimd
            def _(pool):
                product.gpsimd(pool)
                pool.wait_ge(rows_in, 32)
                for t in range(TT):
                    pool.wait_ge(scaled, t + 1)
                    pool.tensor_tensor(m.x[:, t, :], m.x[:, t, :], gb[:, 1, :], ALU.add).then_inc(normed, 1)

            @block.tensor
            def _(pe):
                product.tensor(pe)
                for t in range(TT):
                    pe.wait_ge(normed, t + 1)
                    turn_tile(pe, m, m.x[:, t, :], t).then_inc(turned, 1)

            @block.scalar
            def _(act):
                product.scalar(act)
                do = Steps(act, own_act)

                def hi(t):
                    act.wait_ge(turned, t + 1)
                    for half in range(2):
                        do.go(act.activation(features(m.xt_hi, t, half), banks(t, half), ACT.Copy), hi_ready)

                for t in range(TT):
                    act.wait_ge(stats, t + 1)
                    do.go(act.activation(r[:, t:t + 1], mv[:, t, 1:2], ACT.Sqrt, bias=m.eps[:, 0:1]), root_ready)
                    act.wait_ge(inverted, t + 1)
                    do.go(act.activation(m.x[:, t, :], m.x[:, t, :], ACT.Copy, scale=r[:, t:t + 1]), scaled)
                    if t:
                        hi(t - 1)
                hi(TT - 1)

            @block.vector
            def _(dve):
                product.vector(dve, range(kt))
                do = Steps(dve, own_dve)

                def lo(t):
                    for half in range(2):
                        dve.wait_ge(hi_ready, 2 * t + half + 1)
                        do.go(dve.tensor_tensor(features(m.xt_lo, t, half), banks(t, half),
                                                features(m.xt_hi, t, half).bitcast(F32), ALU.subtract))

                dve.wait_ge(rows_in, 32)
                for t in range(TT):
                    xt = m.x[:, t, :]
                    dve.wait_ge(product.y_ready, t + 1)
                    do(dve.scalar_tensor_tensor(out=xt, in0=xt, scalar=ALPHA, in1=product.y[t], op0=ALU.mult,
                                                op1=ALU.add))
                    for n in range(2):
                        do(dve.bn_stats(st[:, t, n, :], m.x[:, t, n * S:(n + 1) * S]))
                    do(dve.bn_aggr(mv[:, t, :], st[:, t, :, :].rearrange("p a b -> p (a b)")), stats)
                    do(dve.scalar_tensor_tensor(out=xt, in0=xt, scalar=mv[:, t, 0:1], in1=gb[:, 0, :],
                                                op0=ALU.subtract, op1=ALU.mult))
                    dve.wait_ge(root_ready, t + 1)
                    do.go(dve.reciprocal(r[:, t:t + 1], r[:, t:t + 1]), inverted)
                    if t >= 2:
                        lo(t - 2)
                lo(TT - 2)
                lo(TT - 1)


class GroupNorms:

    def __init__(self, m, l, sem, sb, merged):
        self.m, self.l, self.merged = m, l, merged
        self.squared, self.summed, self.rooted, self.normed = (
            sem(n) for n in ("group_squared", "group_summed", "group_rooted", "group_normed"))
        self.sq = sb("group_squares", [P, 2, S])
        self.root = sb("group_root", [P, KD // 2, S])

    def scalar(self, act, do):
        def root(g):
            act.wait_ge(self.summed, 2 * g + 2)
            do.go(act.activation(self.root[:, g, :], self.m.ps[:, g, :], ACT.Sqrt, scale=1.0 / GW,
                                 bias=self.m.eps[:, 0:1]), self.rooted)

        for k in range(KD):
            if k >= 2:
                act.wait_ge(self.summed, k - 1)
            do.go(act.activation(self.sq[:, k % 2, :], self.merged[:, k, :], ACT.Square), self.squared)
            if k >= 2 and k % 2:
                root(k // 2 - 1)
        root(KD // 2 - 1)

    def tensor(self, pe):
        for k in range(KD):
            pe.wait_ge(self.squared, k + 1)
            pe.matmul(self.m.ps[:, k // 2, :], self.m.ones[:, :], self.sq[:, k % 2, :], start=(k % 2 == 0),
                      stop=(k % 2 == 1)).then_inc(self.summed, 1)
        pe.wait_ge(self.rooted, KD // 2)

    def vector(self, dve, do, g):
        GG = 7
        C = self.m.cols3[:, self.l, :]
        dve.wait_ge(self.rooted, g + 1)
        r = self.root[:, g, :]
        do(dve.reciprocal(r, r))
        for k in (2 * g, 2 * g + 1):
            t = self.merged[:, k, :]
            do(dve.scalar_tensor_tensor(out=t, in0=t, scalar=C[:, GG + k:GG + k + 1], in1=r, op0=ALU.mult,
                                        op1=ALU.mult), self.normed if k % 2 else None)


def product_and_rms_norm(nc, m, l, memory, weight, kt, gain_rows, act_in=None, following=(), turn_by=None,
                         groups=False):
    with stage(nc) as (sem, sb):
        product = TokenProduct(m, l, sem, sb, memory, weight, kt, act_in, following)
        own_dve, own_act, root_ready, added, root_2_ready, normed, turned = (
            sem(n) for n in ("own_dve", "own_act", "root_ready", "added", "root_2_ready", "normed", "turned"))
        if groups:
            group_norms = GroupNorms(m, l, sem, sb, act_in)
            product.act_in_ready = group_norms.normed
        sums = sb("square_sums", [P, 2, TT])
        tmp = sb("scaled", [P, 2, D])
        if turn_by:
            gain, shift, room = turn_by
            xn = room[:, KD:2 * KD, :].rearrange("p (t k) s -> p t (k s)", t=TT)
            squares = room[:, 2 * KD:2 * KD + 4, :].rearrange("p (t k) s -> p t (k s)", t=2)
            affine = TurnedAffine(m, sem, gain, shift, turned, room[:, 0:KD, :])
        with nc.Block() as block:
            @block.sync
            def _(sp):
                product.sync(sp)

            @block.gpsimd
            def _(pool):
                product.gpsimd(pool)

            @block.tensor
            def _(pe):
                if groups:
                    group_norms.tensor(pe)
                product.tensor(pe)
                if turn_by:
                    for t in range(TT):
                        pe.wait_ge(normed, t + 1)
                        turn_tile(pe, m, xn[:, t, :], t).then_inc(turned, 1)

            @block.scalar
            def _(act):
                do = Steps(act, own_act)
                if groups:
                    group_norms.scalar(act, do)
                product.scalar(act)

                def root(n, t, src, junk, sem):
                    s = sums[:, n, t:t + 1]
                    do(act.activation(junk, src, ACT.Square, accum_out=s))
                    do.go(act.activation(s, s, ACT.Sqrt, scale=1.0 / D, bias=m.eps[:, 0:1]), sem)

                for t in range(TT + 1):
                    if t < TT:
                        act.wait_ge(product.y_ready, t + 1)
                        if t >= 2:
                            act.wait_ge(added, t - 1)
                        root(0, t, product.y[t], tmp[:, t % 2, :], root_ready)
                    if t and turn_by:
                        act.wait_ge(added, t)
                        root(1, t - 1, m.x[:, t - 1, :], squares[:, t % 2, :], root_2_ready)
                if turn_by:
                    affine.scalar(act)

            @block.vector
            def _(dve):
                do = Steps(dve, own_dve)
                if groups:
                    group_norms.vector(dve, do, 0)
                    for g in range(KD // 2):
                        if g + 1 < KD // 2:
                            group_norms.vector(dve, do, g + 1)
                        product.vector(dve, range(2 * g, 2 * g + 2))
                else:
                    product.vector(dve, range(kt))
                for t in range(TT + 1):
                    if t < TT:
                        xt, s = m.x[:, t, :], sums[:, 0, t:t + 1]
                        dve.wait_ge(root_ready, t + 1)
                        do(dve.reciprocal(s, s))
                        do(dve.scalar_tensor_tensor(out=tmp[:, t % 2, :], in0=product.y[t], scalar=s,
                                                    in1=gain_rows, op0=ALU.mult, op1=ALU.mult))
                        do(dve.tensor_tensor(xt, xt, tmp[:, t % 2, :], ALU.add), added)
                    if t and turn_by:
                        s = sums[:, 1, t - 1:t]
                        dve.wait_ge(root_2_ready, t)
                        do(dve.reciprocal(s, s))
                        do(dve.tensor_scalar(xn[:, t - 1, :], m.x[:, t - 1, :], s, None, ALU.mult), normed)
                if turn_by:
                    affine.vector(dve)


def modulated_turn(nc, m, l, memory, first_tiles, room):
    C = m.cols3[:, l, :]
    NG, BM = 15, 47
    with stage(nc) as (sem, sb):
        ring = WeightRing(sem, memory)
        own, own_act, summed, normed, turned = (sem(n) for n in ("own", "own_act", "summed", "normed", "turned"))
        sums = sb("square_sums", [P, TT])
        xn = room[1][:, 0:KD, :].rearrange("p (t k) s -> p t (k s)", t=TT)
        squares = room[1][:, KD:KD + 4, :].rearrange("p (t k) s -> p t (k s)", t=2)
        affine = TurnedAffine(m, sem, m.in_gain[:, 0, :], m.mod[:, 0:KD], turned, room[0])
        with nc.Block() as block:
            @block.sync
            def _(sp):
                for i, src in enumerate(first_tiles):
                    ring.load(sp, i, [src])

            @block.gpsimd
            def _(pool):
                for i in range(len(first_tiles)):
                    ring.split_lo(pool, i, KD * P)

            @block.scalar
            def _(act):
                do = Steps(act, own_act)
                for t in range(TT):
                    s = sums[:, t:t + 1]
                    do(act.activation(squares[:, t % 2, :], m.x[:, t, :], ACT.Square, accum_out=s))
                    do(act.activation(s, s, ACT.Sqrt, scale=1.0 / D, bias=m.eps[:, 0:1]), summed)
                for i in range(len(first_tiles)):
                    ring.split_hi(act, i, KD * P)
                affine.scalar(act)

            @block.tensor
            def _(pe):
                for t in range(TT):
                    pe.wait_ge(normed, t + 1)
                    turn_tile(pe, m, xn[:, t, :], t).then_inc(turned, 1)

            @block.vector
            def _(dve):
                do = Steps(dve, own)
                do(dve.tensor_tensor(m.mod[:, :], m.mod_sum[:, l, :], C[:, BM:BM + N_MOD * KD], ALU.add))
                for n, (sc, g) in enumerate(((1, 0), (4, 2))):
                    do(dve.scalar_tensor_tensor(out=m.in_gain[:, n, :], in0=m.mod[:, sc * KD:(sc + 1) * KD], scalar=1.0,
                                                in1=C[:, NG + g * KD:NG + (g + 1) * KD], op0=ALU.add, op1=ALU.mult))
                for n, (gt, g) in enumerate(((2, 1), (5, 3))):
                    do(dve.tensor_tensor(m.out_gain[:, n, :], m.mod[:, gt * KD:(gt + 1) * KD],
                                         C[:, NG + g * KD:NG + (g + 1) * KD], ALU.mult))
                for t in range(TT):
                    s = sums[:, t:t + 1]
                    dve.wait_ge(summed, t + 1)
                    do(dve.reciprocal(s, s))
                    do(dve.tensor_scalar(xn[:, t, :], m.x[:, t, :], s, None, ALU.mult), normed)
                affine.vector(dve)
    memory.leave(0, len(first_tiles))


def tile_weights(w, l, c0, n=P):
    return w[l, :, c0:c0 + n].rearrange("(k p) c -> p k c", p=P)


def tiles_ahead(w, l, columns=(0, P, 2 * P)):
    return [(tile_view, tile_weights(w, l, c)) for c in columns]


def rows_ahead(w, l, n=3):
    return [(lambda v: v[:, 0:D], w[l, k * P:(k + 1) * P, :]) for k in range(n)]


def tile_view(v):
    return v[:, 0:KD * P].rearrange("p (k c) -> p k c", k=KD)


def tile_product(pe, m, ring, i, out, cols=P):
    w_hi, w_lo = (tile_view(v) for v in ring.slot(i))
    for k in range(KD):
        last = matmul3(pe, out, (w_hi[:, k, 0:cols], w_lo[:, k, 0:cols]), (m.xt_hi[:, k, :], m.xt_lo[:, k, :]),
                       k == 0, k == KD - 1)
    return last


def in_projection(nc, m, l, memory, w_in, gx_w, ga_w, yr, tb, mult, lat, kpe):
    C = m.cols1[:, l, :]
    cw = lambda tap, j: C[:, 8 * tap + j:8 * tap + j + 1]
    col = lambda base, j: C[:, base + j:base + j + 1]
    CB, GXB, GAB, LAM, QG = 32, 40, 48, 56, 64
    N_LAT = KQ + KKV
    LAT, LAT_SUM = KR, KR + 2
    G_TILE = KR + N_LAT + 1
    ROOTS = {G_TILE: (0, G_TILE - KR), 2 * KR + 1: (G_TILE - KR, KR)}
    GB_TILE = KR + N_LAT + 1 + KR + KD
    tiles = [("x", j, j * P) for j in range(KR)] + [("lat", j, LAT0 + j * P) for j in range(KQ + KKV)] \
        + [("rope", 0, ROPE0)] + [("g", j, D_RNN + j * P) for j in range(KR)] \
        + [("ga", j, GA0 + j * P) for j in range(KD)] + [("gb", j, GB0 + j * P) for j in range(KD)]
    on_act = {"g", "ga", "gb"}
    BANKS = 4
    emptied = []
    for i, (kind, _, _) in enumerate(tiles):
        emptied.append(sum((k in on_act) == (kind in on_act) for k, _, _ in tiles[:i + 1]))
    with stage(nc) as (sem, sb):
        ring = WeightRing(sem, memory)
        memory.leave(len(tiles), 0)
        act_emptied, dve_emptied, own_dve, own_act, gates_done, gate_w_in, zeroed, lru_ready, tanh_ready, \
            in_ready, mult_ready, gated, ta_ready, cols_ready, ratio_ready = (
                sem(n) for n in ("act_emptied", "dve_emptied", "own_dve", "own_act", "gates_done",
                                 "gate_w_in", "zeroed", "lru_ready", "tanh_ready", "in_ready", "mult_ready", "gated",
                                 "ta_ready", "cols_ready", "ratio_ready"))
        squared, summed, rooted, lat_ready, lat_hi = (sem("lat_" + n) for n in ("squared", "summed", "rooted", "ready",
                                                                                "hi"))
        gw = sb("gate_blocks", [P, 2, KR, P])
        xc = sb("x_conv", [P, 2, S])
        th = sb("gate_tanh", [P, 2, 2, S])
        decay = tb
        inp = yr
        sq, root = th[:, 0, 0:2, :], th[:, 1, 0:2, :]
        gel = sb("gelu", [P, 2, S])
        tap = sb("gate_a_tanh", [P, 2, S])
        rot = sb("rot", [P, 3, S])
        c = sb("lru_columns", [P, 8, KR])
        def rope_order(raw, out):
            src = tile_view(raw)[:, :, 0:QK_ROPE]
            return [(src, tile_view(out)[:, :, QK_ROPE * q:QK_ROPE * (q + 1)]) for q in range(4)]

        with nc.Block() as block:
            @block.sync
            def _(sp):
                sp.wait_ge(zeroed, 1)
                for n, w in enumerate((gx_w, ga_w)):
                    for r in range(2):
                        blocks = w[l].rearrange("(j r) a b -> r a j b", r=2)
                        sp.dma_start(gw[64 * r:64 * r + 64, n, :, 64 * r:64 * r + 64], blocks[r]).then_inc(gate_w_in, 16)
                for i, (kind, j, c0) in enumerate(tiles):
                    n = QK_ROPE if kind == "rope" else P
                    ring.load(sp, i, [(lambda v, n=n: tile_view(v)[:, :, 0:n], tile_weights(w_in, l, c0, n))])

            @block.gpsimd
            def _(pool):
                pool.memset(gw[:, :, :, :], 0.0).then_inc(zeroed, 1)
                for i, (kind, _, _) in enumerate(tiles):
                    ring.split_lo(pool, i, KD * P, order=rope_order if kind == "rope" else None)

            @block.tensor
            def _(pe):
                def gates(j):
                    pe.wait_ge(dve_emptied, j + 1)
                    if j >= 2:
                        pe.wait_ge(tanh_ready, j - 1)
                    for n in range(2):
                        last = pe.matmul(m.ps[:, 4 + 2 * (j % 2) + n, :], gw[:, n, j, :], xc[:, j % 2, :],
                                         start=True, stop=True)
                    last.then_inc(gates_done, 1)

                pe.wait_ge(gate_w_in, 64)
                for i, (kind, j, _) in enumerate(tiles):
                    ring.wait_split(pe, i)
                    if i >= BANKS:
                        pe.wait_ge(act_emptied if tiles[i - BANKS][0] in on_act else dve_emptied, emptied[i - BANKS])
                    tile_product(pe, m, ring, i, m.ps[:, i % BANKS, :]).then_inc(ring.used, 1)
                    if 1 <= i <= KR:
                        gates(i - 1)
                    n = i - LAT_SUM
                    if 0 <= n < N_LAT:
                        pe.wait_ge(squared, n + 1)
                        pe.matmul(m.ps[:, 4 + (n >= KQ), :], m.ones[:, :], sq[:, n % 2, :], start=n in (0, KQ),
                                  stop=n in (KQ - 1, N_LAT - 1)).then_inc(summed, 1)

            @block.scalar
            def _(act):
                do = Steps(act, own_act)
                lam = C[:, LAM:LAM + KR]
                do(act.activation(c[:, 0, :], lam, ACT.Abs))
                do(act.activation(c[:, 1, :], c[:, 0, :], ACT.Exp, scale=-1.0))
                act.activation(c[:, 2, :], c[:, 1, :], ACT.Ln, bias=1.0).then_inc(cols_ready, 1)
                for i in range(2):
                    ring.split_hi(act, i, KD * P)

                def gate(j):
                    act.wait_ge(gates_done, j + 1)
                    if j == 0:
                        act.wait_ge(lru_ready, 1)
                    if j >= 2:
                        act.wait_ge(in_ready, j - 1)
                    b = 4 + 2 * (j % 2)
                    t3 = th[:, j % 2, :, :]
                    do.go(act.activation(t3[:, 0, :], m.ps[:, b, :], ACT.Tanh, scale=0.5, bias=c[:, 4, j:j + 1]))
                    do(act.activation(t3[:, 1, :], m.ps[:, b + 1, :], ACT.Tanh, scale=0.5, bias=c[:, 5, j:j + 1]))
                    do.go(act.activation(decay[:, j, :], t3[:, 1, :], ACT.Exp, scale=c[:, 7, j:j + 1],
                                         bias=c[:, 7, j:j + 1]))
                    do(act.activation(mult[:, j, :], t3[:, 1, :], ACT.Tanh, scale=c[:, 6, j:j + 1],
                                      bias=c[:, 6, j:j + 1]), tanh_ready)

                for i, (kind, j, _) in enumerate(tiles):
                    if i + 2 < len(tiles):
                        ring.split_hi(act, i + 2, KD * P, order=rope_order if tiles[i + 2][0] == "rope" else None)
                    if 1 <= i <= KR:
                        gate(i - 1)
                    if i == KR + 1:
                        act.wait_ge(in_ready, KR)
                    if i in ROOTS:
                        j0, j1 = ROOTS[i]
                        act.wait_ge(ratio_ready, j1)
                        do(act.activation(mult[:, j0:j1, :], mult[:, j0:j1, :], ACT.Sqrt, scale=0.5), mult_ready)
                    n = i - LAT - 1
                    if 0 <= n < N_LAT:
                        act.wait_ge(dve_emptied, LAT + n + 1)
                        if n >= 2:
                            act.wait_ge(summed, n - 1)
                        do.go(act.activation(sq[:, n % 2, :], lat[:, n, :], ACT.Square), squared)
                    if i == LAT_SUM + N_LAT:
                        act.wait_ge(summed, N_LAT)
                        do.go(act.activation(root[:, 0, :], m.ps[:, 4, :], ACT.Sqrt, scale=1.0 / Q_LORA,
                                             bias=m.eps[:, 0:1]), rooted)
                        do.go(act.activation(root[:, 1, :], m.ps[:, 5, :], ACT.Sqrt, scale=1.0 / KV_LORA,
                                             bias=m.eps[:, 0:1]), rooted)
                    if kind in on_act:
                        act.wait_ge(ring.used, i + 1)
                    if kind == "g":
                        if j >= 2:
                            act.wait_ge(gated, j - 1)
                        do(act.activation(gel[:, j % 2, :], m.ps[:, i % BANKS, :], ACT.Gelu_apprx_tanh), act_emptied)
                    if kind == "ga":
                        if j >= 2:
                            act.wait_ge(ta_ready, j - 1)
                        do(act.activation(tap[:, j % 2, :], m.ps[:, i % BANKS, :], ACT.Tanh, scale=0.5), act_emptied)
                    if kind == "gb":
                        if j == 0:
                            act.wait_ge(ta_ready, 1)
                        do(act.activation(tb[:, j, :], m.ps[:, i % BANKS, :], ACT.Tanh, scale=0.5), act_emptied)
                for n in range(N_LAT):
                    act.wait_ge(lat_ready, n + 1)
                    do.go(act.activation(m.xt_hi[:, n, :], lat[:, n, :], ACT.Copy), lat_hi)

            @block.vector
            def _(dve):
                do = Steps(dve, own_dve)
                lam = C[:, LAM:LAM + KR]
                do(dve.tensor_scalar(c[:, 4, :], C[:, GXB:GXB + KR], 0.5, None, ALU.mult))
                do(dve.tensor_scalar(c[:, 5, :], C[:, GAB:GAB + KR], 0.5, None, ALU.mult))
                dve.wait_ge(cols_ready, 1)
                e, ln = c[:, 1, :], c[:, 2, :]
                do(dve.tensor_scalar(c[:, 0, :], e, 1.0, None, ALU.add))
                do(dve.tensor_scalar(c[:, 3, :], c[:, 0, :], 1.0, None, ALU.is_equal))
                do(dve.tensor_scalar(c[:, 0, :], c[:, 0, :], -1.0, None, ALU.add))
                do(dve.tensor_tensor(c[:, 0, :], c[:, 0, :], c[:, 3, :], ALU.add))
                do(dve.reciprocal(c[:, 0, :], c[:, 0, :]))
                do(dve.tensor_tensor(ln, ln, c[:, 3, :], ALU.add))
                do(dve.tensor_tensor(ln, ln, e, ALU.mult))
                do(dve.tensor_tensor(ln, ln, c[:, 0, :], ALU.mult))
                do(dve.tensor_scalar(c[:, 0, :], lam, -1.0, 0.0, ALU.mult, ALU.max))
                do(dve.tensor_tensor(ln, ln, c[:, 0, :], ALU.add))
                do(dve.tensor_scalar(c[:, 6, :], ln, LRU_C / 2, None, ALU.mult))
                do(dve.tensor_scalar(c[:, 7, :], ln, -LRU_C / 2, None, ALU.mult), lru_ready)

                def after_gates(j):
                    dve.wait_ge(tanh_ready, j + 1)
                    t3 = th[:, j % 2, :, :]
                    do(dve.scalar_tensor_tensor(out=inp[:, j, :], in0=t3[:, 0, :], scalar=1.0, in1=xc[:, j % 2, :],
                                                op0=ALU.add, op1=ALU.mult), in_ready)

                def ratio(j):
                    do(dve.tensor_scalar(rot[:, 2, :], mult[:, j, :], 1.0, None, ALU.add))
                    do(dve.reciprocal(rot[:, 2, :], rot[:, 2, :]))
                    do(dve.tensor_tensor(mult[:, j, :], mult[:, j, :], rot[:, 2, :], ALU.mult), ratio_ready)

                def recur(j):
                    do(dve.tensor_tensor(inp[:, j, :], inp[:, j, :], mult[:, j, :], ALU.mult))
                    do(dve.tensor_tensor_scan(mult[:, j, :], decay[:, j, :], inp[:, j, :], 0.0, ALU.mult, ALU.add))

                for i, (kind, j, _) in enumerate(tiles):
                    ps = m.ps[:, i % BANKS, :]
                    if kind not in on_act:
                        dve.wait_ge(ring.used, i + 1)
                    if kind == "x":
                        conv(dve, do, xc[:, j % 2, :], ps, [cw(tap_, j) for tap_ in range(CONV)], col(CB, j), dve_emptied)
                    if 1 <= i <= KR:
                        after_gates(i - 1)
                    if kind == "lat":
                        do(dve.tensor_copy(lat[:, j, :], ps), dve_emptied)
                    if kind == "rope":
                        do(dve.tensor_copy(rot[:, 0, :], ps), dve_emptied)
                        do(dve.stream_shuffle(rot[:, 1, :], rot[:, 0, :], SWAP16))
                        do(dve.tensor_tensor(rot[:, 0, :], rot[:, 0, :], m.cos1[:, :], ALU.mult))
                        do(dve.tensor_tensor(rot[:, 1, :], rot[:, 1, :], m.sin1[:, :], ALU.mult))
                        do(dve.tensor_tensor(kpe[:, :], rot[:, 0, :], rot[:, 1, :], ALU.add))
                    if KR < i <= 2 * KR:
                        ratio(i - KR - 1)
                    if kind == "g":
                        dve.wait_ge(mult_ready, 1 if j < ROOTS[G_TILE][1] else 2)
                        recur(j)
                        dve.wait_ge(act_emptied, j + 1)
                        do(dve.tensor_tensor(yr[:, j, :], mult[:, j, :], gel[:, j % 2, :], ALU.mult), gated)
                    if kind == "ga":
                        dve.wait_ge(act_emptied, KR + j + 1)
                        do(dve.scalar_tensor_tensor(out=yr[:, j, :], in0=tap[:, j % 2, :], scalar=1.0,
                                                    in1=yr[:, j, :], op0=ALU.add, op1=ALU.mult), ta_ready)
                    n = i - GB_TILE - 1
                    if n == 0:
                        dve.wait_ge(rooted, 2)
                        do(dve.reciprocal(root, root))
                    if 0 <= n < N_LAT:
                        do(dve.scalar_tensor_tensor(out=lat[:, n, :], in0=lat[:, n, :], scalar=col(QG, n),
                                                    in1=root[:, int(n >= KQ), :], op0=ALU.mult, op1=ALU.mult), lat_ready)
                dve.wait_ge(ring.used, len(tiles))
                for n in range(N_LAT):
                    dve.wait_ge(lat_hi, n + 1)
                    do.go(dve.tensor_tensor(m.xt_lo[:, n, :], lat[:, n, :], m.xt_hi[:, n, :].bitcast(F32), ALU.subtract))


SWAP16 = [(i + 16) % 32 for i in range(32)]
SWAP8 = [i + 8 if i < 8 else i - 8 if i < 16 else i for i in range(32)]


HG = 4


def mla_heads(nc, m, l, first, groups, w_uq, w_ukv, kpe, q_all, k_all, v_all, room):
    with stage(nc) as (sem, sb):
        ring = WeightRing(sem, RingMemory(sb, HG * QK * KQ))
        own_dve, own_act, out_ready, dve_emptied, act_emptied, spread, roped, v_ready, v_out = (
            sem(n) for n in ("own_dve", "own_act", "out_ready", "dve_emptied", "act_emptied", "spread", "roped",
                             "v_ready", "v_out"))
        rot = room[:, 0:4, :].rearrange("p (g n) s -> p g n s", g=2)
        q_pe = room[:, 4:6, :]
        WQ, WK = HG * QK, HG * (QK_NOPE + V_HEAD)

        def by_part(raw, out, kt, width, cut):
            r = raw[:, 0:kt * width].rearrange("p (k h e) -> p k h e", k=kt, h=HG)
            o = out[:, 0:kt * width].rearrange("p (k c) -> p k c", k=kt)
            pairs = []
            for k in range(kt):
                pairs.append((r[:, k, :, 0:cut], o[:, k, 0:HG * cut].rearrange("p (h e) -> p h e", h=HG)))
                pairs.append((r[:, k, :, cut:], o[:, k, HG * cut:].rearrange("p (h e) -> p h e", h=HG)))
            return pairs

        uq_order = lambda raw, out: by_part(raw, out, KQ, WQ, QK_NOPE)
        ukv_order = lambda raw, out: by_part(raw, out, KKV, WK, QK_NOPE)

        with nc.Block() as block:
            @block.sync
            def _(sp):
                for g in range(groups):
                    h0 = first + g * HG
                    wq = w_uq[l, :, h0 * QK:(h0 + HG) * QK].rearrange("(k p) c -> p k c", p=P)
                    ring.load(sp, 2 * g, [(lambda v: v[:, 0:KQ * WQ].rearrange("p (k c) -> p k c", k=KQ), wq)])
                    wk = w_ukv[l, :, h0 * P:(h0 + HG) * P].rearrange("(k p) c -> p k c", p=P)
                    ring.load(sp, 2 * g + 1, [(lambda v: v[:, 0:KKV * WK].rearrange("p (k c) -> p k c", k=KKV), wk)])
                for h in range(groups * HG):
                    sp.dma_start(k_all[QK_NOPE:QK, h, :], kpe[0:QK_ROPE, :]).then_inc(spread, 16)
                for g in range(groups):
                    sp.wait_ge(roped, g + 1)
                    for h in range(HG):
                        sp.dma_start(q_all[QK_NOPE:QK, g * HG + h, :],
                                     q_pe[32 * h:32 * h + 32, g % 2, :]).then_inc(spread, 16)
                sp.wait_ge(spread, 16 * 2 * groups * HG)

            @block.gpsimd
            def _(pool):
                for g in range(groups):
                    ring.split_lo(pool, 2 * g, 0, order=uq_order)
                    ring.split_lo(pool, 2 * g + 1, 0, order=ukv_order)

            @block.scalar
            def _(act):
                do = Steps(act, own_act)

                def split(c):
                    if c < 2 * groups:
                        ring.split_hi(act, c, 0, order=ukv_order if c % 2 else uq_order)

                for c in range(3):
                    split(c)
                for g in range(groups):
                    for n, i in enumerate((0, 1, 3, 4)):
                        if n == 2:
                            split(2 * g + 3)
                        act.wait_ge(out_ready, 5 * g + i + 1)
                        to = q_all if n < 2 else k_all
                        ps = m.ps[:, (5 * g + i) % 6, :]
                        for r in range(2):
                            h = g * HG + 2 * (n % 2) + r
                            do(act.activation(to[0:QK_NOPE, h, :], ps[64 * r:64 * r + 64, :], ACT.Copy),
                               act_emptied if r else None)
                    split(2 * g + 4)

            @block.vector
            def _(dve):
                do = Steps(dve, own_dve)
                for g in range(groups):
                    dve.wait_ge(out_ready, 5 * g + 3)
                    a, b = rot[:, g % 2, 0, :], rot[:, g % 2, 1, :]
                    do(dve.tensor_copy(a, m.ps[:, (5 * g + 2) % 6, :]), dve_emptied)
                    do(dve.stream_shuffle(b, a, SWAP16))
                    do(dve.tensor_tensor(a, a, m.cos1[:, :], ALU.mult))
                    do(dve.tensor_tensor(b, b, m.sin1[:, :], ALU.mult))
                    do(dve.tensor_tensor(q_pe[:, g % 2, :], a, b, ALU.add), roped)
                    dve.wait_ge(v_ready, g + 1)
                    vg = m.ps[:, 6:8, :].rearrange("p b (t c) -> p (b t) c", t=2)
                    do(dve.tensor_copy(v_all[:, :, g * HG * V_HEAD:(g + 1) * HG * V_HEAD], vg), v_out)

            @block.tensor
            def _(pe):
                def emptied(i):
                    g, n = divmod(i, 5)
                    if n == 2:
                        pe.wait_ge(dve_emptied, g + 1)
                    else:
                        pe.wait_ge(act_emptied, 4 * g + (1, 2, 0, 3, 4)[n])

                for g in range(groups):
                    for n in range(5):
                        i = 5 * g + n
                        if n in (0, 3):
                            ring.wait_split(pe, 2 * g + (n == 3))
                        if i >= 6:
                            emptied(i - 6)
                        kt, k0, wide = (KQ, 0, WQ) if n < 3 else (KKV, KQ, WK)
                        w = [v[:, 0:kt * wide].rearrange("p (k c) -> p k c", k=kt) for v in ring.slot(2 * g + (n >= 3))]
                        c0 = (n if n < 3 else n - 3) * P
                        for k in range(kt):
                            last = matmul3(pe, m.ps[:, i % 6, :], (w[0][:, k, c0:c0 + P], w[1][:, k, c0:c0 + P]),
                                           (m.xt_hi[:, k0 + k, :], m.xt_lo[:, k0 + k, :]), k == 0, k == kt - 1)
                        last.then_inc(out_ready, 1)
                        if n == 2:
                            pe.wait_ge(out_ready, i + 1)
                            pe.sem_inc(ring.used, 1)
                    if g:
                        pe.wait_ge(v_out, g)
                    for t in range(TT):
                        out = m.ps[:, 6 + t // 2, 256 * (t % 2):256 * (t % 2) + 256]
                        for k in range(KKV):
                            left = [v[:, KQ + k, t * P:(t + 1) * P] for v in (m.xt_hi, m.xt_lo)]
                            last = matmul3(pe, out, left, (w[0][:, k, HG * QK_NOPE:], w[1][:, k, HG * QK_NOPE:]),
                                           k == 0, k == KKV - 1)
                    last.then_inc(v_ready, 1)
                    pe.wait_ge(v_ready, g + 1)
                    pe.sem_inc(ring.used, 1)


def attention(nc, m, heads, scale, finish, loads=()):
    with stage(nc) as (sem, sb):
        loaded = sem("loaded")
        scored, peaked, exped, normed, turned, copied, valued, finished, own_dve = (
            sem(n) for n in ("scored", "peaked", "exped", "normed", "turned", "copied", "valued", "finished",
                             "own_dve"))
        SCORES, PROBS, TURNED = 4, 8, 3
        LAG_TURN, LAG_COPY, LAG_VALUES = 4, 5, 6
        p = sb("probs", [P, PROBS, S])
        pt = sb("probs_turned", [P, TURNED, S])
        st = sb("softmax", [P, 4, 8])
        U = len(heads) * TT
        ORDER = (0, 2, 1, 3)
        with nc.Block() as block:
            if loads:
                @block.sync
                def _(sp):
                    for to, source in loads:
                        sp.dma_start(to, source).then_inc(loaded, 16)
                    sp.wait_ge(loaded, 16 * len(loads))

            @block.tensor
            def _(pe):
                def score(u):
                    h, t = u // TT, ORDER[u % TT]
                    q, k, _ = heads[h]
                    n = (t + 1) * P
                    if u >= SCORES:
                        pe.wait_ge(exped, u - SCORES + 1)
                    bank = m.ps[:, u % SCORES, :]
                    pe.matmul(bank[:, 0:n], q[:, t * P:(t + 1) * P], k[:, 0:n], start=True, stop=True)
                    pe.matmul(bank[:, t * P:n], m.ident_b[:, :], m.causal_b[:, :], start=False, stop=True,
                              skip_group_check=True).then_inc(scored, 1)

                def turn_probs(u):
                    pe.wait_ge(normed, u + 1)
                    if u >= 2:
                        pe.wait_ge(copied, u - 1)
                    for b in range(ORDER[u % TT] + 1):
                        last = pe.transpose(m.ps[:, 4 + u % 2, b * P:(b + 1) * P],
                                            p[:, u % PROBS, b * P:(b + 1) * P], m.ident)
                    last.then_inc(turned, 1)

                def values(u):
                    h, t = u // TT, ORDER[u % TT]
                    pe.wait_ge(copied, u + 1)
                    if u % TT == 0 and h >= 2:
                        pe.wait_ge(finished, h - 1)
                    for b in range(t + 1):
                        last = pe.matmul(m.ps[:, 6 + h % 2, t * P:(t + 1) * P], heads[h][2](b),
                                         pt[:, u % TURNED, b * P:(b + 1) * P], start=(b == 0), stop=(b == t))
                    last.then_inc(valued, 1)

                for u in range(U + LAG_VALUES):
                    if u < U:
                        score(u)
                    if 0 <= u - LAG_TURN < U:
                        turn_probs(u - LAG_TURN)
                    if 0 <= u - LAG_VALUES < U:
                        values(u - LAG_VALUES)

            @block.vector
            def _(dve):
                do = Steps(dve, own_dve)
                for u in range(U + LAG_VALUES + 4):
                    if u < U:
                        n = (ORDER[u % TT] + 1) * P
                        dve.wait_ge(scored, u + 1)
                        do(dve.tensor_reduce(st[:, 3, u % 8:u % 8 + 1], m.ps[:, u % SCORES, 0:n], AX.X, ALU.max))
                        do.go(dve.tensor_scalar(st[:, 0, u % 8:u % 8 + 1], st[:, 3, u % 8:u % 8 + 1], -scale, None,
                                                ALU.mult), peaked)
                    v = u - 1
                    if 0 <= v < U:
                        n = (ORDER[v % TT] + 1) * P
                        dve.wait_ge(exped, v + 1)
                        do(dve.reciprocal(st[:, 2, v % 8:v % 8 + 1], st[:, 1, v % 8:v % 8 + 1]))
                        do.go(dve.tensor_scalar(p[:, v % PROBS, 0:n], p[:, v % PROBS, 0:n], st[:, 2, v % 8:v % 8 + 1],
                                                None, ALU.mult), normed)
                    w = u - LAG_VALUES - 3
                    if w >= 0 and w % TT == TT - 1:
                        h = w // TT
                        dve.wait_ge(valued, (h + 1) * TT)
                        finish(dve, do, h, m.ps[:, 6 + h % 2, :], finished)

            @block.scalar
            def _(act):
                for u in range(U + LAG_COPY):
                    if u < U:
                        n = (ORDER[u % TT] + 1) * P
                        act.wait_ge(peaked, u + 1)
                        if u >= PROBS:
                            act.wait_ge(turned, u - PROBS + 1)
                        act.activation(p[:, u % PROBS, 0:n], m.ps[:, u % SCORES, 0:n], ACT.Exp, scale=scale,
                                       bias=st[:, 0, u % 8:u % 8 + 1], accum_out=st[:, 1, u % 8:u % 8 + 1])\
                            .then_inc(exped, 1)
                    v = u - LAG_COPY
                    if v >= 0:
                        n = (ORDER[v % TT] + 1) * P
                        act.wait_ge(turned, v + 1)
                        if v >= TURNED:
                            act.wait_ge(valued, v - TURNED + 1)
                        act.activation(pt[:, v % TURNED, 0:n], m.ps[:, 4 + v % 2, 0:n], ACT.Copy).then_inc(copied, 1)


MOD_COLS = 1536


def conv_up(nc, m, l, memory, w_up, w_mod, hid, following):
    tap = lambda n, j: m.cols2[:, l, 2 * KF * n + j:2 * KF * n + j + 1]
    with stage(nc) as (sem, sb):
        ring = WeightRing(sem, memory)
        memory.leave(2 * KF, len(following))
        own, conved, gelued, emptied, mod_used, mod_summed, mod_copied = (
            sem(n) for n in ("own", "conved", "gelued", "emptied", "mod_used", "mod_summed", "mod_copied"))
        mod_in = [sem(f"mod_in{i}") for i in range(2)]
        buf = sb("convolved", [P, 2, 2, S])
        gel = sb("gelu", [P, 2, S])
        w_m = sb("w_mod", [P, 2, MOD_COLS])
        acc = sb("mod_acc", [P, N_MOD * D])
        BANKS, TILES = 6, 2 * KF
        PARTS = N_MOD * D // MOD_COLS
        CHUNKS = KD * PARTS
        MOD_SUMS = 4
        LAG = 4
        with nc.Block() as block:
            @block.sync
            def _(sp):
                for i in range(TILES):
                    j, half = divmod(i, 2)
                    ring.load(sp, i, [(tile_view, tile_weights(w_up, l, half * D_FF + j * P))])
                    c = i - LAG - 2
                    if 0 <= c < CHUNKS:
                        k, part = divmod(c, PARTS)
                        if c >= 2:
                            sp.wait_ge(mod_used, c - 1)
                        sp.dma_start(w_m[:, c % 2, :], w_mod[l, k * P:(k + 1) * P, part * MOD_COLS:(part + 1) * MOD_COLS])\
                            .then_inc(mod_in[c % 2], 16)

                for i, src in enumerate(following):
                    ring.load(sp, TILES + i, [src])

            @block.gpsimd
            def _(pool):
                for i in range(TILES + len(following)):
                    ring.split_lo(pool, i, KD * P)

            @block.tensor
            def _(pe):
                for i in range(TILES):
                    ring.wait_split(pe, i)
                    if i >= BANKS:
                        pe.wait_ge(emptied, i - BANKS + 1)
                    tile_product(pe, m, ring, i, m.ps[:, i % BANKS, :]).then_inc(ring.used, 1)
                    first = (i - TILES) * MOD_SUMS + N_MOD * KD
                    if first == 0:
                        pe.wait_ge(mod_used, CHUNKS)
                    if first >= 0:
                        for j in range(first, first + MOD_SUMS):
                            last = pe.matmul(m.ps[:, 6, j:j + 1], acc[:, j * P:(j + 1) * P], m.ones[:, 0:1],
                                             start=True, stop=True)
                last.then_inc(mod_summed, 1)

            @block.vector
            def _(dve):
                do = Steps(dve, own)
                for i in range(TILES + 1):
                    j, half = divmod(i, 2)
                    if i < TILES:
                        dve.wait_ge(ring.used, i + 1)
                        if half == 0 and j >= 2:
                            dve.wait_ge(gelued, j - 1)
                        conv(dve, do, buf[:, j % 2, half, :], m.ps[:, i % BANKS, :],
                             [tap(n, half * KF + j) for n in range(FFN_CONV)], tap(3, half * KF + j), emptied)
                    c = i - LAG
                    if 0 <= c < CHUNKS:
                        k, part = divmod(c, PARTS)
                        dve.wait_ge(mod_in[c % 2], 16 * (c // 2 + 1))
                        to, w, silu = acc[:, part * MOD_COLS:(part + 1) * MOD_COLS], w_m[:, c % 2, :], m.cond[:, k:k + 1]
                        if k == 0:
                            do(dve.tensor_scalar(to, w, silu, None, ALU.mult), mod_used)
                        else:
                            do(dve.scalar_tensor_tensor(out=to, in0=w, scalar=silu, in1=to, op0=ALU.mult,
                                                        op1=ALU.add), mod_used)
                    if half == 0 and j:
                        dve.wait_ge(gelued, j)
                        do(dve.tensor_tensor(hid[:, j - 1, :], gel[:, (j - 1) % 2, :], buf[:, (j - 1) % 2, 1, :],
                                             ALU.mult), conved)
                dve.wait_ge(mod_summed, 1)
                do(dve.tensor_copy(m.mod_sum[:, l, :], m.ps[:, 6, 0:N_MOD * KD]), mod_copied)

            @block.scalar
            def _(act):
                for i in range(2):
                    ring.split_hi(act, i, KD * P)
                for i in range(TILES + 1):
                    if i + 2 < TILES + len(following):
                        ring.split_hi(act, i + 2, KD * P)
                    if i % 2:
                        j = i // 2
                        act.wait_ge(emptied, 2 * j + 1)
                        if j >= 2:
                            act.wait_ge(conved, j - 1)
                        act.activation(gel[:, j % 2, :], buf[:, j % 2, 0, :], ACT.Gelu_apprx_tanh).then_inc(gelued, 1)


def relu_up(nc, m, l, memory, w_up, hid, following):
    with stage(nc) as (sem, sb):
        ring = WeightRing(sem, memory)
        memory.leave(KF2, len(following))
        emptied, squared = sem("emptied"), sem("squared")
        pos = sb("positive", [P, 2, S])
        BANKS = 6
        with nc.Block() as block:
            @block.sync
            def _(sp):
                for i in range(KF2):
                    ring.load(sp, i, [(tile_view, tile_weights(w_up, l, i * P))])
                for i, src in enumerate(following):
                    ring.load(sp, KF2 + i, [src])

            @block.gpsimd
            def _(pool):
                for i in range(KF2 + len(following)):
                    ring.split_lo(pool, i, KD * P)

            @block.tensor
            def _(pe):
                for i in range(KF2):
                    ring.wait_split(pe, i)
                    if i >= BANKS:
                        pe.wait_ge(emptied, i - BANKS + 1)
                    tile_product(pe, m, ring, i, m.ps[:, i % BANKS, :]).then_inc(ring.used, 1)

            @block.vector
            def _(dve):
                for i in range(KF2):
                    dve.wait_ge(ring.used, i + 1)
                    if i >= 2:
                        dve.wait_ge(squared, i - 1)
                    dve.tensor_scalar(pos[:, i % 2, :], m.ps[:, i % BANKS, :], 0.0, None, ALU.max).then_inc(emptied, 1)
                    dve.wait_ge(emptied, i + 1)
                    dve.tensor_tensor(hid[:, i, :], pos[:, i % 2, :], pos[:, i % 2, :], ALU.mult).then_inc(squared, 1)

            @block.scalar
            def _(act):
                for i in range(KF2 + len(following)):
                    ring.split_hi(act, i, KD * P)


FM = {"ah": 0, "ab": 2, "ac": 4, "q": 6, "cmp": 8, "slc": 9, "win": 10, "small": 11, "lq": 12, "lk": 13, "lg": 14,
      "mu": 16}
FM_TILES = [[(0, i * P, P)] for i in range(9)] \
    + [[(0, O_KV + 2 * HD, HD), (HD, O_KV + 2 * HD, HD)], [(0, O_KV + 4 * HD, HD), (HD, O_KV + 4 * HD, HD)],
       [(0, O_G, DK), (DK, O_LR, RANK)], [(0, O_LQ, P)], [(0, O_LK, P)], [(0, O_LG, P)], [(0, O_LG + P, P)],
       [(0, O_MU, P)], [(0, O_MU + P, P)]]
TM_COLS = [(0, O_KV + 3 * HD, HD), (HD, O_KV + 5 * HD, HD), (2 * HD, O_LV, GW), (2 * HD + GW, O_MV, GW)]
TM = 2 * HD + 2 * GW


def in_projection_2(nc, m, l, memory, w_in, fm, tm, merged, qr, kz, vd, gates):
    C = m.cols3[:, l, :]
    TILES, A, BANKS = len(FM_TILES), 2 * HD + GW, 6
    FIRST_GATE = FM["small"] + 1
    rows = lambda i: FM_TILES[i][-1][0] + FM_TILES[i][-1][2]
    narrow = lambda v, i: tile_view(v)[:, :, 0:rows(i)] if i < TILES else v[:, 0:TM]
    order = lambda raw, out, i: [(narrow(raw, i), narrow(out, i))]
    with stage(nc) as (sem, sb):
        ring = WeightRing(sem, memory)
        memory.leave(TILES + KD, 0)
        diag_ready, gain_spread, gain_out = sem("diag_ready"), sem("gain_spread"), sem("gain_out")
        diag = sb("diag", [P, 4, P])
        GAIN_TILES = {0: (0, 0), 1: (0, 4), 6: (1, 0), 7: (1, 4)}
        GAIN_COPIES = {3: 0, 9: 1}
        emptied, own, zeroed, tanh, sig_ready, spread, copied, values_out = (
            sem(n) for n in ("emptied", "own", "zeroed", "tanh", "sig_ready", "spread", "copied",
                             "values_out"))
        a = sb("a", [P, 2, S])
        sig = sb("sig", [P, S])
        want, arrivals = [], [0] * ring.RAW
        for i in range(TILES + KD):
            pieces = len(FM_TILES[i] if i < TILES else TM_COLS)
            arrivals[i % ring.RAW] += 16 * pieces * (i >= ring.ready)
            want.append(arrivals[i % ring.RAW])
        with nc.Block() as block:
            @block.sync
            def _(sp):
                for i, cols in enumerate(FM_TILES):
                    ring.load(sp, i, [(lambda v, a=a, n=n: tile_view(v)[:, :, a:a + n], tile_weights(w_in, l, c, n))
                                      for a, c, n in cols])
                for k in range(KD):
                    ring.load(sp, TILES + k, [(lambda v, a=a, n=n: v[:, a:a + n], w_in[l, k * P:(k + 1) * P, c:c + n])
                                              for a, c, n in TM_COLS])

            @block.gpsimd
            def _(pool):
                pool.memset(kz[:, :, :, :], 0.0).then_inc(zeroed, 1)
                for i in range(TILES + KD):
                    ring.split_lo(pool, i, 0, order=lambda raw, out, i=i: order(raw, out, i))

            @block.scalar
            def _(act):
                for i in range(TILES + KD):
                    ring.split_hi(act, i, 0, order=lambda raw, out, i=i: order(raw, out, i), arrived=want[i])
                    if i == FM["small"] + 2:
                        act.wait_ge(emptied, FM["small"] + 1)
                        act.activation(sig[0:3 * GH, :], fm[0:3 * GH, FM["small"], :], ACT.Tanh, scale=0.5)\
                            .then_inc(tanh, 1)
                    g = i - 2 - FIRST_GATE
                    if 0 <= g < 6:
                        act.wait_ge(spread, g + 1)
                        act.activation(gates[:, g, :], m.ps[:, 6 + g % 2, :], ACT.Copy).then_inc(copied, 1)
                act.wait_ge(ring.used, TILES + KD)
                for t in range(TT):
                    act.activation(tm[:, t, 0:A], m.ps[:, t, 0:A], ACT.Copy).then_inc(values_out, 1)

            @block.tensor
            def _(pe):
                for i in range(TILES):
                    ring.wait_split(pe, i)
                    if i >= BANKS:
                        pe.wait_ge(emptied, i - BANKS + 1)
                    tile_product(pe, m, ring, i, m.ps[0:rows(i), i % BANKS, :], rows(i)).then_inc(ring.used, 1)
                    if i - 1 in GAIN_TILES:
                        n, k0 = GAIN_TILES[i - 1]
                        pe.wait_ge(diag_ready, n * KD + k0 + 4)
                        if n and k0 == 0:
                            pe.wait_ge(gain_out, 1)
                        for k in range(k0, k0 + 4):
                            last = pe.matmul(m.ps[:, 6 + k // 4, (k % 4) * P:(k % 4 + 1) * P], m.ones[:, :],
                                             diag[:, k % 4, :], start=True, stop=True)
                        last.then_inc(gain_spread, 1)
                    g = i - FIRST_GATE
                    if 0 <= g < 6:
                        if g == 0:
                            pe.wait_ge(sig_ready, 1)
                            pe.wait_ge(gain_out, 2)
                        if g >= 2:
                            pe.wait_ge(copied, g - 1)
                        pe.matmul(m.ps[:, 6 + g % 2, :], m.pick[0:3 * GH, g * P:(g + 1) * P], sig[0:3 * GH, :],
                                  start=True, stop=True).then_inc(spread, 1)
                for k in range(KD):
                    ring.wait_split(pe, TILES + k)
                    if k == 0:
                        pe.wait_ge(emptied, TILES)
                        pe.wait_ge(copied, 6)
                    w = ring.slot(TILES + k)
                    for t in range(TT):
                        left = [v[:, k, t * P:(t + 1) * P] for v in (m.xt_hi, m.xt_lo)]
                        matmul3(pe, m.ps[:, t, 0:A], left, (w[0][:, 0:A], w[1][:, 0:A]), k == 0, k == KD - 1)
                        last = matmul3(pe, m.ps[:, TT + t, 0:GW], left, (w[0][:, A:TM], w[1][:, A:TM]),
                                       k == 0, k == KD - 1)
                    last.then_inc(ring.used, 1)

            @block.vector
            def _(dve):
                do = Steps(dve, own)

                def short_conv(j):
                    do(dve.tensor_tensor(a[:, 0, :], fm[:, FM["ac"] + j, :], fm[:, FM["ah"] + j, :], ALU.mult))
                    conv(dve, do, a[:, 1, :], a[:, 0, :], [C[:, 2 * n + j:2 * n + j + 1] for n in range(CONV2)], None)
                    do(dve.tensor_tensor(merged[:, j, :], a[:, 1, :], fm[:, FM["ab"] + j, :], ALU.mult))

                def rotate(n, src):
                    do(dve.stream_shuffle(a[:, 0, :], fm[:, src, :], SWAP8))
                    do(dve.tensor_tensor(a[:, 0, :], a[:, 0, :], m.sin2[:, :], ALU.mult))
                    do(dve.tensor_tensor(a[:, 1, :], fm[:, src, :], m.cos2[:, :], ALU.mult))
                    if n < 2:
                        do(dve.tensor_tensor(qr[:, n, :], a[:, 0, :], a[:, 1, :], ALU.add))
                    else:
                        for r in range(2):
                            half = slice(64 * r, 64 * r + 64)
                            do(dve.tensor_tensor(kz[half, n - 2, r, :], a[half, 0, :], a[half, 1, :], ALU.add))

                for i in range(TILES):
                    dve.wait_ge(ring.used, i + 1)
                    do(dve.tensor_copy(fm[0:rows(i), i, :], m.ps[0:rows(i), i % BANKS, :]), emptied)
                    if i in GAIN_TILES:
                        n, k0 = GAIN_TILES[i]
                        if n or k0:
                            dve.wait_ge(gain_spread, 2 * n + k0 // 4)
                        for k in range(k0, k0 + 4):
                            do.go(dve.tensor_scalar(diag[:, k % 4, :], m.ident, m.out_gain[:, n, k:k + 1], None,
                                                    ALU.mult), diag_ready)
                    if i in GAIN_COPIES:
                        n = GAIN_COPIES[i]
                        dve.wait_ge(gain_spread, 2 * n + 2)
                        do.go(dve.tensor_copy(m.gain_rows[:, n, :], m.ps[:, 6:8, :].rearrange("p b c -> p (b c)")),
                              gain_out)
                    if i in (FM["ac"], FM["ac"] + 1):
                        short_conv(i - FM["ac"])
                    if i in (FM["q"], FM["q"] + 1):
                        rotate(i - FM["q"], i)
                    if i == FM["slc"]:
                        dve.wait_ge(zeroed, 1)
                    if i in (FM["slc"], FM["win"]):
                        rotate(2 + (i == FM["win"]), i)
                    if i == FM["small"] + 1:
                        dve.wait_ge(tanh, 1)
                        do(dve.tensor_scalar(sig[0:3 * GH, :], sig[0:3 * GH, :], 0.5, 0.5, ALU.mult, ALU.add), sig_ready)
                dve.wait_ge(ring.used, TILES + KD)
                for t in range(TT):
                    do.go(dve.tensor_copy(tm[:, t, A:TM], m.ps[:, TT + t, 0:GW]))
                dve.wait_ge(values_out, TT)
                for b in range(2):
                    for r in range(2):
                        do.go(dve.tensor_copy(vd[:, b, :, r * HD:(r + 1) * HD], tm[:, :, b * HD:(b + 1) * HD]))


class MixerWeights:

    def __init__(self, l, sb, a):
        self.cmp_w1 = sb("cmp_w1", [P, CMP, P])
        self.cmp_w2, self.cmp_pos = sb("cmp_w2", [P, 2, P]), sb("cmp_pos", [CMP, P])
        self.gla_gate_w2 = sb("gla_gate_w2", [DK + RANK, P])
        self.mlp_ws, self.mlp_bias = sb("mlp_ws", [P, GH, P]), sb("mlp_bias", [P, 2, P])
        self.loads = [(self.gla_gate_w2[DK:DK + RANK, :], a["gla_gate_w2_2"][l])]
        for j in range(2):
            rows = slice(j * HD, (j + 1) * HD)
            self.loads.append((self.cmp_pos[:, rows], a["cmp_pos_2"][l, j]))
            self.loads.append((self.cmp_w1[rows, :, :], a["cmp_w1_2"][l, j].rearrange("(r d) c -> d r c", d=HD)))
            for r in range(2):
                self.loads.append((self.cmp_w2[:, j, r * HD:(r + 1) * HD], a["cmp_w2_2"][l, j]))
        self.loads.append((self.mlp_ws[:, :, :], a["gmlp_ws_2"][l].rearrange("g t s -> t g s")))
        for g in range(GH):
            half = slice(64 * (g % 2), 64 * (g % 2) + 64)
            self.loads.append((self.mlp_bias[half, g // 2, :], a["gmlp_b_2"][l, g].partition_broadcast(64)))


def pooled_linear_and_gmlp(nc, m, l, weights, fm, tm, gates, merged):
    C = m.cols3[:, l, :]
    GB = 6
    scale = HD ** -0.5
    N = N_CMP
    G = TT * GH
    ATT, CMP_HID, CMP_POS, MLP_WS, GLA_GATE = 0, 4, 5, 6, 7
    CMP_KV, CMP_SCORES, GLA_KL, GLA_KV, GLA_O, MLP_MIX, GLA_SUMS, CMP_TURNED, CMP_OUT = 5, 4, 7, 6, 2, 0, 0, 4, 6
    with stage(nc) as (sem, sb):
        own, own_act = sem("own"), sem("own_act")
        cmp_zeroed, cmp_pos_turned, cmp_z_ready, cmp_hid_done, cmp_hid_turned, cmp_tanh, cmp_hid_ready, cmp_kv_done, \
            cmp_kv_ready, cmp_scored, cmp_shifted, cmp_exped, cmp_p_ready, cmp_turned, cmp_pct_ready, cmp_valued, \
            cmp_taken = (
                sem("cmp_" + n) for n in ("zeroed", "pos_turned", "z_ready", "hid_done", "hid_turned", "tanh", "hid_ready",
                                          "kv_done", "kv_ready", "scored", "shifted", "exped", "p_ready", "turned",
                                          "pct_ready", "valued", "taken"))
        gla_gate_done, gla_ln_ready, gla_diffed, gla_exp_ready, gla_scaled, gla_att_done, gla_att_ready, \
            gla_kl_turned, gla_kl_ready, gla_kv_done, gla_kv_used, gla_state_ready, gla_zeroed, gla_o_done, \
            gla_squared, gla_summed, gla_rooted, gla_silu = (
                sem("gla_" + n) for n in ("gate_done", "ln_ready", "diffed", "exp_ready", "scaled", "att_done",
                                          "att_ready", "kl_turned", "kl_ready", "kv_done", "kv_used", "state_ready",
                                          "zeroed", "o_done", "squared", "summed", "rooted", "silu"))
        mlp_zeroed, mlp_turned, mlp_wt_ready, mlp_v_ready, mlp_mixed, mlp_rooted, mlp_summed, mlp_taken = (
            sem("mlp_" + n) for n in ("zeroed", "turned", "wt_ready", "v_ready", "mixed", "rooted", "summed",
                                      "taken"))
        w1, w2, pos = weights.cmp_w1, weights.cmp_w2, weights.cmp_pos
        pos_t = sb("cmp_pos_t", [P, CMP])
        z = sb("cmp_windows", [P, 2 * N, CMP])
        hid_rows, th = sb("cmp_hidden_rows", [2 * N, P]), sb("cmp_hidden_tanh", [2 * N, P])
        hid = sb("cmp_hidden", [P, 2 * N])
        kc = sb("cmp_kc", [P, 2, 32])
        vc = sb("cmp_vc", [32, P])
        sc = sb("cmp_scores", [P, GH * TT, N])
        st = sb("cmp_sums", [P, 2, GH * TT])
        pct = sb("cmp_probs_turned", [32, GH, S])
        gw2 = weights.gla_gate_w2
        la, b = fm[:, 0:3, :], fm[:, 3:6, :]
        carry = sb("gla_carry", [P, S])
        cmp_tmp = carry
        e = sb("gla_exps", [P, 4, S])
        qk = sb("gla_scaled_qk", [P, 4, S])
        att = sb("gla_att", [P, GH, TT, P])
        vz = sb("gla_vz", [P, TT, GH, P])
        klz = sb("gla_klz", [P, 2, TT, P])
        state = gates[:, 2:2 + NCH * GW // S, :].rearrange("p a (b c) -> p (a b) c", c=GW)
        kvm = sb("gla_kvm", [P, GW])
        sq, r = qk[:, 0:2, :], b[:, 0:2, :]
        chunks = lambda v: v.rearrange("p (n c) -> p n c", c=CHUNK)
        at = lambda c: chunks(b[:, 0, :])[:, :, c:c + 1].to_broadcast([P, NCH, CHUNK])
        w, bs = weights.mlp_ws, weights.mlp_bias
        wt = sb("mlp_ws_turned", [P, GH, P])
        mvz = sb("mlp_v_halves", [P, TT, GH, P])
        v = sb("mlp_v", [P, TT, GW])
        vsq = qk[:, 0:2, :].rearrange("p a (b c) -> p (a b) c", c=GW)
        vst = sb("mlp_st", [P, 2, G])
        mlp_tmp = fm[:, FM["slc"]:FM["slc"] + 2, :]
        by_group = lambda x: x.rearrange("p t (g c) -> p (t g) c", c=HD)
        wide = lambda x: x.unsqueeze(2).to_broadcast([P, G, HD])
        with nc.Block() as block:
            @block.gpsimd
            def _(pool):
                pool.memset(z[:, :, :], 0.0).then_inc(cmp_zeroed, 1)
                pool.memset(kc[:, :, :], 0.0).then_inc(cmp_zeroed, 1)
                pool.memset(carry[:, :], 1.0).then_inc(gla_zeroed, 1)
                pool.wait_ge(gla_zeroed, 1)
                pool.memset(chunks(carry[:, :])[:, :, 0:1], 0.0).then_inc(gla_zeroed, 1)
                pool.memset(mvz[:, :, :, :], 0.0).then_inc(mlp_zeroed, 1)
                pool.memset(klz[:, :, :, :], 0.0).then_inc(gla_zeroed, 1)
                pool.memset(att[:, :, :, :], 0.0).then_inc(gla_zeroed, 1)
                pool.memset(state[:, 0, :], 0.0).then_inc(gla_zeroed, 1)
                pool.memset(vz[:, :, :, :], 0.0).then_inc(gla_zeroed, 1)
                pool.wait_ge(gla_zeroed, 6)
                for h in range(GH):
                    c0 = (h % 2) * HD
                    pool.tensor_copy(vz[:, :, h, c0:c0 + HD], tm[:, :, 2 * HD + h * HD:2 * HD + (h + 1) * HD])\
                        .then_inc(gla_zeroed, 1)

            @block.tensor
            def _(pe):
                def gla_kv(n):
                    if n == 0:
                        pe.wait_ge(gla_kl_ready, 2)
                    if n >= 2:
                        pe.wait_ge(gla_kv_used, n - 1)
                    pe.matmul(m.ps[:, GLA_KV + n % 2, 0:GW], klz[:, n % 2, n // 2, :],
                              tm[:, n // 2, 2 * HD:2 * HD + GW], start=True, stop=True).then_inc(gla_kv_done, 1)

                pe.matmul(m.ps[:, GLA_GATE, :], gw2[DK:DK + RANK, :], fm[DK:DK + RANK, FM["small"], :], start=True,
                          stop=True).then_inc(gla_gate_done, 1)
                pe.transpose(m.ps[:, CMP_POS, 0:CMP], pos[:, :], m.ident[0:CMP, 0:CMP]).then_inc(cmp_pos_turned, 1)
                for g in range(GH):
                    last = pe.transpose(m.ps[:, MLP_WS, g * P:(g + 1) * P], w[:, g, :], m.ident)
                last.then_inc(mlp_turned, 1)
                pe.wait_ge(cmp_z_ready, 4)
                for r1 in range(CMP):
                    last = pe.matmul(m.ps[0:2 * N, CMP_HID, 0:P], z[:, :, r1], w1[:, r1, :],
                                     start=(r1 == 0), stop=(r1 == CMP - 1))
                last.then_inc(cmp_hid_done, 1)
                pe.wait_ge(gla_scaled, 1)
                for t in range(TT):
                    last = pe.transpose(m.ps[:, GLA_KL, t * P:(t + 1) * P], qk[:, 2, t * P:(t + 1) * P], m.ident)
                last.then_inc(gla_kl_turned, 1)
                pe.wait_ge(gla_scaled, 3)
                for h in range(GH):
                    rows = slice(DK * h, DK * h + DK)
                    for t in range(TT):
                        tok = slice(t * P, (t + 1) * P)
                        last = pe.matmul(m.ps[:, ATT + h, tok], qk[rows, 1, tok], qk[rows, 0, tok], start=True,
                                         stop=True, tile_position=(DK * h, 0))
                    last.then_inc(gla_att_done, 1)
                pe.wait_ge(cmp_hid_ready, 1)
                pe.transpose(m.ps[:, CMP_HID, 0:2 * N], hid_rows[:, :], m.ident[0:2 * N, 0:2 * N])\
                    .then_inc(cmp_hid_turned, 1)
                pe.wait_ge(cmp_hid_ready, 2)
                pe.matmul(m.ps[:, CMP_KV, 0:N], w2[:, 0, :], hid[:, 0:N], start=True, stop=True)
                pe.matmul(m.ps[0:N, CMP_KV, P:2 * P], hid[:, N:2 * N], w2[:, 1, :], start=True, stop=True)\
                    .then_inc(cmp_kv_done, 1)
                pe.wait_ge(mlp_wt_ready, 1)
                gla_kv(0)
                gla_kv(1)
                pe.wait_ge(cmp_kv_ready, 1)
                for u in range(GH * TT):
                    h, t = divmod(u, TT)
                    last = pe.matmul(m.ps[:, CMP_SCORES, u * N:(u + 1) * N], fm[:, FM["q"] + h // 2, t * P:(t + 1) * P],
                                     kc[:, h % 2, 0:N], start=True, stop=True)
                last.then_inc(cmp_scored, 1)
                gla_kv(2)
                gla_kv(3)
                pe.wait_ge(mlp_v_ready, 1)
                pe.wait_ge(gla_att_ready, GH)
                for j in range(2):
                    for t in range(TT):
                        for r1 in range(2):
                            last = pe.matmul(m.ps[:, MLP_MIX + j, t * P:(t + 1) * P], mvz[:, t, 2 * j + r1, :],
                                             wt[:, 2 * j + r1, :], start=(r1 == 0), stop=(r1 == 1))
                    last.then_inc(mlp_mixed, 1)
                for n in range(4, NCH - 1):
                    gla_kv(n)

                def cmp_turn(pair):
                    if pair:
                        pe.wait_ge(cmp_pct_ready, 2)
                    for u in range(2 * pair * TT, 2 * (pair + 1) * TT):
                        h, t = divmod(u, TT)
                        last = pe.transpose(m.ps[0:N, CMP_TURNED + h % 2, t * P:(t + 1) * P], sc[:, u, :], m.ident)
                    last.then_inc(cmp_turned, 1)

                pe.wait_ge(cmp_p_ready, 1)
                cmp_turn(0)
                pe.wait_ge(gla_zeroed, 6 + GH)
                pe.wait_ge(gla_scaled, 4)
                pe.wait_ge(gla_state_ready, NCH - 1)
                for j in range(2):
                    first = True
                    for t in range(TT):
                        for h in (2 * j, 2 * j + 1):
                            pe.matmul(m.ps[:, GLA_O + j, t * P:(t + 1) * P], vz[:, t, h, :], att[:, h, t, :],
                                      start=first, stop=False, skip_group_check=True)
                            first = False
                        for n in (2 * t, 2 * t + 1):
                            if n:
                                last = pe.matmul(m.ps[:, GLA_O + j, n * CHUNK:(n + 1) * CHUNK],
                                                 state[:, n, j * P:(j + 1) * P], qk[:, 3, n * CHUNK:(n + 1) * CHUNK],
                                                 start=False, stop=(n == NCH - 1), skip_group_check=True)
                last.then_inc(gla_o_done, 1)
                cmp_turn(1)
                for h in range(GH):
                    pe.wait_ge(cmp_pct_ready, h + 1)
                    if h >= 2:
                        pe.wait_ge(cmp_taken, h - 1)
                    pe.matmul(m.ps[:, CMP_OUT + h % 2, :], vc[0:N, :], pct[0:N, h, :], start=True, stop=True)\
                        .then_inc(cmp_valued, 1)
                pe.wait_ge(mlp_taken, 2)
                for j in range(2):
                    pe.wait_ge(gla_squared, j + 1)
                    pe.matmul(m.ps[:, GLA_SUMS + j, :], m.halves, sq[:, j, :], start=True, stop=True)\
                        .then_inc(gla_summed, 1)

            @block.scalar
            def _(act):
                do = Steps(act, own_act)
                act.wait_ge(gla_gate_done, 1)
                do(act.activation(la[:, 0, :], m.ps[:, GLA_GATE, :], ACT.Identity, bias=C[:, GB:GB + 1]))
                do(act.activation(la[:, 1, :], la[:, 0, :], ACT.Abs))
                do(act.activation(la[:, 1, :], la[:, 1, :], ACT.Exp, scale=-1.0))
                do(act.activation(la[:, 1, :], la[:, 1, :], ACT.Ln, bias=1.0), gla_ln_ready)
                act.wait_ge(gla_diffed, 1)
                do.go(act.activation(e[:, 2, :], b[:, 2, :], ACT.Exp, scale=-1.0), gla_exp_ready)
                do.go(act.activation(e[:, 1, :], b[:, 1, :], ACT.Exp, scale=-1.0), gla_exp_ready)
                do.go(act.activation(e[:, 0, :], b[:, 1, :], ACT.Exp), gla_exp_ready)
                do.go(act.activation(e[:, 3, :], b[:, 0, :], ACT.Exp), gla_exp_ready)
                act.wait_ge(mlp_summed, 1)
                do.go(act.activation(vst[:, 1, :], vst[:, 1, :], ACT.Sqrt, scale=1.0 / HD, bias=m.eps[:, 0:1]), mlp_rooted)
                act.wait_ge(cmp_hid_done, 1)
                do.go(act.activation(th[:, :], m.ps[0:2 * N, CMP_HID, 0:P], ACT.Tanh, scale=0.5), cmp_tanh)
                for j in range(2):
                    do.go(act.activation(la[:, 1 + j, :], fm[:, FM["lg"] + j, :], ACT.Tanh, scale=0.5), gla_silu)
                act.wait_ge(cmp_shifted, 1)
                do.go(act.activation(sc[:, :, :], sc[:, :, :], ACT.Exp, scale=scale), cmp_exped)
                for pair in range(2):
                    act.wait_ge(cmp_turned, pair + 1)
                    for h in (2 * pair, 2 * pair + 1):
                        do.go(act.activation(pct[0:N, h, :], m.ps[0:N, CMP_TURNED + h % 2, :], ACT.Copy), cmp_pct_ready)
                    if pair == 0:
                        act.wait_ge(gla_o_done, 1)
                        for j in range(2):
                            do.go(act.activation(sq[:, j, :], m.ps[:, GLA_O + j, :], ACT.Square), gla_squared)
                for j in range(2):
                    act.wait_ge(gla_summed, j + 1)
                    do.go(act.activation(r[:, j, :], m.ps[:, GLA_SUMS + j, :], ACT.Sqrt, scale=1.0 / HD,
                                         bias=m.eps[:, 0:1]), gla_rooted)

            @block.vector
            def _(dve):
                do = Steps(dve, own)
                dve.wait_ge(cmp_pos_turned, 1)
                do(dve.tensor_copy(pos_t[:, :], m.ps[:, CMP_POS, 0:CMP]))
                blocks = fm[:, FM["cmp"], :].rearrange("p (n r) -> p n r", r=STRIDE)
                dve.wait_ge(cmp_zeroed, 2)
                for n in range(2):
                    for j in range(2):
                        half = slice(64 * j, 64 * j + 64)
                        add = pos_t[half, n * STRIDE:(n + 1) * STRIDE].unsqueeze(1).to_broadcast([64, N, STRIDE])
                        do(dve.tensor_tensor(z[half, j * N:(j + 1) * N, n * STRIDE:(n + 1) * STRIDE],
                                             blocks[half, n:n + N, :], add, ALU.add), cmp_z_ready)
                dve.wait_ge(gla_ln_ready, 1)
                do(dve.scalar_tensor_tensor(out=la[:, 2, :], in0=la[:, 0, :], scalar=0.0, in1=la[:, 1, :],
                                            op0=ALU.min, op1=ALU.subtract))
                do(dve.tensor_scalar(la[:, 2, :], la[:, 2, :], 1.0 / TAU, None, ALU.mult))
                dve.wait_ge(gla_zeroed, 2)
                do(dve.tensor_tensor_scan(b[:, 0, :], carry[:, :], la[:, 2, :], 0.0, ALU.mult, ALU.add))
                do(dve.tensor_tensor(chunks(b[:, 1, :]), chunks(b[:, 0, :]), at(CHUNK // 2), ALU.subtract))
                do(dve.tensor_tensor(chunks(b[:, 2, :]), chunks(b[:, 0, :]), at(CHUNK - 1), ALU.subtract), gla_diffed)
                dve.wait_ge(mlp_turned, 1)
                do(dve.tensor_tensor(wt[:, :, :], m.ps[:, MLP_WS, :].rearrange("p (g c) -> p g c", g=GH),
                                     m.upper.unsqueeze(1).to_broadcast([P, GH, P]), ALU.mult), mlp_wt_ready)
                src = tm[:, :, 2 * HD + GW:TM]
                s3 = lambda x: x.rearrange("p t (g c) -> p t g c", c=HD)
                v3, q3 = by_group(v[:, :, :]), by_group(vsq)
                do(dve.tensor_copy(v[:, :, :], src))
                do(dve.tensor_reduce(vst[:, 0, :], v3, AX.X, ALU.add))
                do(dve.tensor_scalar(vst[:, 0, :], vst[:, 0, :], 1.0 / HD, None, ALU.mult))
                do(dve.tensor_tensor(v3, v3, wide(vst[:, 0, :]), ALU.subtract))
                do(dve.tensor_tensor(q3, v3, v3, ALU.mult))
                do(dve.tensor_reduce(vst[:, 1, :], q3, AX.X, ALU.add), mlp_summed)
                q, k = fm[:, FM["lq"], :], fm[:, FM["lk"], :]
                for n, (to, x, s) in enumerate(((2, k, 1.0), (1, k, 1.0), (0, q, DK ** -0.5), (3, q, DK ** -0.5))):
                    dve.wait_ge(gla_exp_ready, n + 1)
                    do(dve.scalar_tensor_tensor(out=qk[:, to, :], in0=x, scalar=s, in1=e[:, to, :], op0=ALU.mult,
                                                op1=ALU.mult), gla_scaled)
                dve.wait_ge(cmp_tanh, 1)
                do(dve.scalar_tensor_tensor(out=hid_rows[:, :], in0=th[:, :], scalar=1.0,
                                            in1=m.ps[0:2 * N, CMP_HID, 0:P], op0=ALU.add, op1=ALU.mult))
                do(dve.tensor_scalar(hid_rows[:, :], hid_rows[:, :], 0.5, None, ALU.mult), cmp_hid_ready)
                dve.wait_ge(gla_kl_turned, 1)
                dve.wait_ge(gla_zeroed, 6)
                for par in range(2):
                    half = slice(64 * par, 64 * par + 64)
                    do(dve.tensor_copy(klz[half, par, :, :], m.ps[half, GLA_KL, :].rearrange("p (t c) -> p t c", t=TT)),
                       gla_kl_ready)
                dve.wait_ge(cmp_hid_turned, 1)
                do(dve.tensor_copy(hid[:, :], m.ps[:, CMP_HID, 0:2 * N]), cmp_hid_ready)
                dve.wait_ge(mlp_rooted, 1)
                dve.wait_ge(mlp_zeroed, 1)
                do(dve.reciprocal(vst[:, 1, :], vst[:, 1, :]))
                do(dve.tensor_tensor(v3, v3, wide(vst[:, 1, :]), ALU.mult))
                for r1 in range(2):
                    do(dve.tensor_copy(mvz[:, :, r1::2, r1 * HD:(r1 + 1) * HD], s3(v[:, :, :])[:, :, r1::2, :]),
                       mlp_v_ready if r1 else None)
                dve.wait_ge(cmp_kv_done, 1)
                for r1 in range(2):
                    half = slice(64 * r1, 64 * r1 + 64)
                    do(dve.tensor_copy(kc[half, r1, 0:N], m.ps[half, CMP_KV, 0:N]))
                do(dve.tensor_copy(vc[0:N, :], m.ps[0:N, CMP_KV, P:2 * P]), cmp_kv_ready)

                def gla_state(n):
                    dve.wait_ge(gla_kv_done, n + 1)
                    do(dve.tensor_tensor(kvm[:, :], m.ps[:, GLA_KV + n % 2, 0:GW], m.state_mask, ALU.mult), gla_kv_used)
                    decay = e[:, 3, (n + 1) * CHUNK - 1:(n + 1) * CHUNK]
                    do(dve.scalar_tensor_tensor(out=state[:, n + 1, :], in0=state[:, n, :], scalar=decay,
                                                in1=kvm[:, :], op0=ALU.mult, op1=ALU.add), gla_state_ready)

                for h in range(GH):
                    dve.wait_ge(gla_att_done, h + 1)
                    for par in range(2):
                        half = slice(64 * par, 64 * par + 64)
                        part = m.ps[half, ATT + h, :].rearrange("p (t c) -> p t c", t=TT)[:, :, half]
                        do(dve.tensor_scalar(att[half, h, :, half], part, 3e38, -3e38, ALU.min, ALU.max))
                    do(dve.tensor_tensor(att[:, h, :, :], att[:, h, :, :],
                                         m.chunk.unsqueeze(1).to_broadcast([P, TT, P]), ALU.mult), gla_att_ready)
                    if h < 2:
                        gla_state(h)
                dve.wait_ge(cmp_scored, 1)
                scores = m.ps[:, CMP_SCORES, 0:GH * TT * N].rearrange("p (h c) -> p h c", h=GH)
                s4 = sc[:, :, :].rearrange("p (h t) n -> p h (t n)", h=GH)
                over_heads = lambda x: x.unsqueeze(1).to_broadcast([P, GH, TT * N])
                over_keys = lambda x: x.unsqueeze(2).to_broadcast([P, GH * TT, N])
                do(dve.tensor_tensor(s4, scores, over_heads(m.cmp_add), ALU.add))
                do(dve.tensor_reduce(st[:, 0, :], sc[:, :, :], AX.X, ALU.max))
                do(dve.tensor_tensor(sc[:, :, :], sc[:, :, :], over_keys(st[:, 0, :]), ALU.subtract), cmp_shifted)
                gla_state(2)
                gla_state(3)
                dve.wait_ge(cmp_exped, 1)
                do(dve.tensor_reduce(st[:, 1, :], sc[:, :, :], AX.X, ALU.add))
                do(dve.reciprocal(st[:, 1, :], st[:, 1, :]))
                do(dve.tensor_tensor(sc[:, :, :], sc[:, :, :], over_keys(st[:, 1, :]), ALU.mult))
                do(dve.tensor_tensor(s4, s4, over_heads(m.cmp_mul), ALU.mult), cmp_p_ready)
                for n in range(4, NCH - 1):
                    gla_state(n)
                for j in range(2):
                    dve.wait_ge(mlp_mixed, j + 1)
                    mix = m.ps[:, MLP_MIX + j, :].rearrange("p (t c) -> p t c", t=TT)
                    out = mlp_tmp[:, j, :].rearrange("p (t c) -> p t c", t=TT)
                    do(dve.tensor_tensor(out, mix, bs[:, j, :].unsqueeze(1).to_broadcast([P, TT, P]), ALU.add), mlp_taken)
                    do(dve.tensor_tensor(merged[:, 6 + j, :], mlp_tmp[:, j, :], fm[:, FM["mu"] + j, :], ALU.mult))
                dve.wait_ge(gla_silu, 2)
                for j in range(2):
                    do(dve.scalar_tensor_tensor(out=la[:, 1 + j, :], in0=la[:, 1 + j, :], scalar=1.0,
                                                in1=fm[:, FM["lg"] + j, :], op0=ALU.add, op1=ALU.mult))
                for h in range(GH):
                    dve.wait_ge(cmp_valued, h + 1)
                    half, tile = slice(64 * (h % 2), 64 * (h % 2) + 64), h // 2
                    do(dve.tensor_tensor(cmp_tmp[half, :], m.ps[half, CMP_OUT + h % 2, :], gates[half, tile, :],
                                         ALU.mult), cmp_taken)
                    do(dve.tensor_tensor(merged[half, 2 + tile, :], merged[half, 2 + tile, :], cmp_tmp[half, :], ALU.add))
                for j in range(2):
                    dve.wait_ge(gla_rooted, j + 1)
                    do(dve.reciprocal(r[:, j, :], r[:, j, :]))
                    do(dve.scalar_tensor_tensor(out=r[:, j, :], in0=r[:, j, :], scalar=0.5, in1=la[:, 1 + j, :],
                                                op0=ALU.mult, op1=ALU.mult))
                    do(dve.tensor_tensor(merged[:, 4 + j, :], m.ps[:, GLA_O + j, :], r[:, j, :], ALU.mult))


def first_block_layer(nc, m, l, a):
    with ExitStack() as mem:
        sb = lambda name, shape: mem.enter_context(nc.sbuf_tensor(f"{name}_{nc.next_id()}", shape, F32))
        hid = sb("hidden", [P, KF, S])
        yr, tb, mult = hid[:, 0:KR, :], hid[:, KR:KR + KD, :], hid[:, KR + KD:2 * KR + KD, :]
        with ExitStack() as mixer:
            sbm = lambda name, shape, dt=F32: mixer.enter_context(nc.sbuf_tensor(f"{name}_{nc.next_id()}", shape, dt))
            kpe = sbm("k_pe", [P, S])
            with ExitStack() as projection:
                sbp = lambda name, shape, dt=F32: projection.enter_context(
                    nc.sbuf_tensor(f"{name}_{nc.next_id()}", shape, dt))
                lat = sbp("latents", [P, KQ + KKV, S])
                in_projection(nc, m, l, RingMemory(sbp), a["w_in"], a["gx_w"], a["ga_w"], yr, tb, mult, lat, kpe)
            HALF = HEADS // 2
            q_all, k_all = sbm("q_all", [QK, HALF, S]), sbm("k_all", [QK, HALF, S])
            v_all = sbm("v_all", [P, TT, HALF * V_HEAD])
            tmp = mult[:, 6, :]
            for first in (0, HALF):
                mla_heads(nc, m, l, first, HALF // HG, a["w_uq"], a["w_ukv"], kpe, q_all, k_all, v_all, mult)

                def finish(dve, do, h, out, sem):
                    half, tile = slice(64 * (h % 2), 64 * (h % 2) + 64), (first + h) // 2
                    do(dve.scalar_tensor_tensor(out=tmp[half, :], in0=tb[half, tile, :], scalar=1.0, in1=out[half, :],
                                                op0=ALU.add, op1=ALU.mult))
                    do(dve.tensor_tensor(yr[half, tile, :], yr[half, tile, :], tmp[half, :], ALU.add), sem)

                values = lambda h: lambda b: v_all[:, b, (h // 2) * P:(h // 2 + 1) * P]
                attention(nc, m, [(q_all[:, h, :], k_all[:, h, :], values(h)) for h in range(HALF)], MLA_SCALE, finish)
        memory = RingMemory(lambda name, shape, dt=F32: mem.enter_context(
            nc.sbuf_tensor(f"{name}_{nc.next_id()}", shape, dt)))
        product_and_layer_norm(nc, m, l, memory, a["w_out"], KD, a["ln1_g"], a["ln1_b"], act_in=yr, act_scale=0.5,
                               following=tiles_ahead(a["w_up"], l, (0, D_FF, P)))
        conv_up(nc, m, l, memory, a["w_up"], a["w_mod_2"], hid, rows_ahead(a["w_down"], l))
        product_and_layer_norm(nc, m, l, memory, a["w_down"], KF, a["ln2_g"], a["ln2_b"], act_in=hid)


def second_block_layer(nc, m, l, a):
    with ExitStack() as mem:
        sb = lambda name, shape, dt=F32: mem.enter_context(nc.sbuf_tensor(f"{name}_{nc.next_id()}", shape, dt))
        hid = sb("hidden", [P, KF2, S])
        FMN = len(FM_TILES)
        merged, fm, gates = hid[:, 0:KD, :], hid[:, KD:KD + FMN, :], hid[:, KD + FMN:KD + FMN + 6, :]
        with ExitStack() as mixers:
            sbm = lambda name, shape, dt=F32: mixers.enter_context(nc.sbuf_tensor(f"{name}_{nc.next_id()}", shape, dt))
            tm = sbm("token_major", [P, TT, TM])
            with ExitStack() as nsa:
                sbn = lambda name, shape, dt=F32: nsa.enter_context(nc.sbuf_tensor(f"{name}_{nc.next_id()}", shape, dt))
                small = lambda name, shape: mixers.enter_context(
                    nc.sbuf_tensor(f"{name}_{nc.next_id()}", shape, F32, side="right"))
                qr, kz, vd = sbn("qr", [P, 2, S]), sbn("kz", [P, 2, 2, S]), sbn("vd", [P, 2, TT, P])
                with turned_activations(nc, m), ExitStack() as projection:
                    memory = RingMemory(lambda name, shape, dt=F32: projection.enter_context(
                        nc.sbuf_tensor(f"{name}_{nc.next_id()}", shape, dt)))
                    modulated_turn(nc, m, l, memory, tiles_ahead(a["w_in_2"], l), (merged, fm[:, 0:KD + 4, :]))
                    in_projection_2(nc, m, l, memory, a["w_in_2"], fm, tm, merged, qr, kz, vd, gates)
                weights = MixerWeights(l, small, a)
                tmp = sbn("gated", [P, S])

                def finish(dve, do, n, out, sem):
                    branch, h = divmod(n, GH)
                    half, tile = slice(64 * (h % 2), 64 * (h % 2) + 64), h // 2
                    gate, to = gates[half, 2 * (branch + 1) + tile, :], merged[half, 2 + tile, :]
                    if branch == 0:
                        do(dve.tensor_tensor(to, out[half, :], gate, ALU.mult), sem)
                    else:
                        do(dve.tensor_tensor(tmp[half, :], out[half, :], gate, ALU.mult))
                        do(dve.tensor_tensor(to, to, tmp[half, :], ALU.add), sem)

                values = lambda branch: lambda b: vd[:, branch, b, :]
                attention(nc, m, [(qr[:, h // 2, :], kz[:, branch, h % 2, :], values(branch))
                                  for branch in range(2) for h in range(GH)], HD ** -0.5, finish, weights.loads)
            pooled_linear_and_gmlp(nc, m, l, weights, fm, tm, gates, merged)
        memory = RingMemory(sb)
        with turned_activations(nc, m):
            product_and_rms_norm(nc, m, l, memory, a["w_o_2"], KD, m.gain_rows[:, 0, :], act_in=merged, groups=True,
                                 following=tiles_ahead(a["w_up_2"], l),
                                 turn_by=(m.in_gain[:, 1, :], m.mod[:, 3 * KD:4 * KD], hid[:, KD:3 * KD + 4, :]))
            relu_up(nc, m, l, memory, a["w_up_2"], hid, rows_ahead(a["w_down_2"], l))
        product_and_rms_norm(nc, m, l, memory, a["w_down_2"], KF2, m.gain_rows[:, 1, :], act_in=hid)


@contextmanager
def turned_activations(nc, m):
    with nc.sbuf_tensor(f"xt_hi_{nc.next_id()}", [P, KD, S], F32R, side="right") as hi, \
            nc.sbuf_tensor(f"xt_lo_{nc.next_id()}", [P, KD, S], F32R, side="right") as lo:
        m.xt_hi, m.xt_lo = hi, lo
        yield


class Memory:
    pass


def program(nc, a, table, where, out):
    m = Memory()
    CLEARED[:] = []
    with ExitStack() as ctx:
        def sb(name, shape, dt=F32):
            return ctx.enter_context(nc.sbuf_tensor(name, shape, dt))
        m.ps = ctx.enter_context(nc.psum_tensor("ps", [P, 8, S], F32))
        m.x = sb("x_tokens", [P, TT, D])
        m.table = sb("table", [P, table.shape[1]])
        part = lambda name: m.table[:, where[name][0]:where[name][0] + where[name][1]]
        m.ident, m.causal, m.upper, m.chunk, m.halves, m.pick = (
            part(name) for name in ("ident", "causal", "upper", "chunk", "halves", "pick"))
        m.cmp_add, m.cmp_mul, m.freq1, m.freq2, m.state_mask = (
            part(name) for name in ("cmp_add", "cmp_mul", "freq1", "freq2", "state"))
        m.ones, m.eps = sb("ones", [P, P]), sb("eps", [P, 1])
        m.ident_b, m.causal_b = sb("ident_b", [P, P], BF16), sb("causal_b", [P, P], BF16)
        m.sin2, m.cos2 = (sb(n, [P, S]) for n in ("sin2", "cos2"))
        m.cond_raw, m.cond, m.mod_sum = sb("cond_raw", [P, 1, KD]), sb("cond", [P, KD]), \
            sb("mod_sum", [P, DEPTH, N_MOD * KD])
        first = ctx.enter_context(ExitStack())
        sb1 = lambda name, shape: first.enter_context(nc.sbuf_tensor(name, shape, F32))
        m.cols3 = sb("cols3", [P, DEPTH, 95])
        m.sin1, m.cos1 = sb1("sin1", [P, S]), sb1("cos1", [P, S])
        m.cols1, m.cols2 = sb1("cols1", [P, DEPTH, 69]), sb1("cols2", [P, DEPTH, (FFN_CONV + 1) * 2 * KF])
        vectors = [(m.cond_raw[:, :, :], a["c_2"])]
        for cols, names in ((m.cols1, ("conv_w", "conv_b", "gx_b", "ga_b", "lru_lambda", "q_norm_g", "kv_norm_g")),
                            (m.cols2, ("ffn_conv_w", "ffn_conv_b")),
                            (m.cols3, ("conv_w_2", "gla_gate_b_2", "grp_gain_2", "norm_g_2", "b_mod_2"))):
            at = 0
            for name in names:
                v = a[name]
                parts = [v[:, n] for n in range(v.shape[1])] if name == "ffn_conv_w" else [v]
                for part_ in parts:
                    n = int(np.prod(part_.shape[1:])) // P
                    vectors.append((cols[:, :, at:at + n], part_))
                    at += n
        with turned_activations(nc, m):
            start_up(nc, m, a["x"], a["positions"], a["positions_2"], table, vectors)
            with nc.Fori(0, DEPTH) as l:
                first_block_layer(nc, m, l, a)
                last_stage_cleared(nc)
        first.close()
        m.mod, m.in_gain, m.out_gain, m.gain_rows = sb("mod", [P, N_MOD * KD]), sb("in_gain", [P, 2, KD]), \
            sb("out_gain", [P, 2, KD]), sb("gain_rows", [P, 2, D])
        with nc.Fori(0, DEPTH) as l:
            second_block_layer(nc, m, l, a)
            last_stage_cleared(nc)
        with stage(nc) as (sem, _):
            stored = sem("stored")
            with nc.Block() as block:
                @block.sync
                def _(sp):
                    for t in range(TT):
                        sp.dma_start(out[0, t * P:(t + 1) * P, :], m.x[:, t, :]).then_inc(stored, 16)
                    sp.wait_ge(stored, 16 * TT)


def kernel(**inputs):
    import concourse.bacc as bacc
    from concourse.bass_utils import run_bass_kernel_spmd

    nc = bacc.Bacc("TRN2", target_bir_lowering=False, num_devices=1)
    table, where = constants()
    arrays, a = {"in_table": table}, {}
    for name, value in inputs.items():
        arrays[f"in_{name}"] = value = np.ascontiguousarray(value)
        a[name] = nc.dram_tensor(f"in_{name}", value.shape, mybir.dt.from_np(value.dtype),
                                       kind="ExternalInput").ap()
    table_ap = nc.dram_tensor("in_table", table.shape, F32, kind="ExternalInput").ap()
    out = nc.dram_tensor("out", (1, S, D), F32, kind="ExternalOutput").ap()
    program(nc, a, table_ap, where, out)
    results = run_bass_kernel_spmd(nc, [arrays], core_ids=[0])
    return results.results[0]["out"]
```
